# Optimizing a Trainium2 kernel written in Bass

```python
import math
import jax, jax.numpy as jnp
from jax import lax
import numpy as np

D_MODEL = 1024
BATCH = 1
SEQ = 256
DEPTH = 2

HEAD_DIM = 64
H_SB = 4
H_DSA = 4
H_IDX = 4
D_IDX = 64
TOPK_MAX = 256
H_SW = 8
KV_SW = 2
WINDOW = 128
BLOCK = 128
N_BRANCH = 3
N_BUCKETS = 32
MAX_DISTANCE = 128
N_MEM = 256
H_X = 4
XHEAD_DIM = 128
D_FF_DENSE = (11 * D_MODEL) // 4
N_EXPERTS = 8
TOP_K_EXPERTS = 2
D_FF_EXPERT = (7 * D_MODEL) // 2
N_DENSE_LAYERS = (DEPTH + 1) // 2
N_MOE_LAYERS = DEPTH // 2
EPS = 1e-6

IN_SIZES = (
    H_SB * HEAD_DIM, H_SB * HEAD_DIM, H_SB * HEAD_DIM,
    H_DSA * HEAD_DIM, HEAD_DIM, HEAD_DIM,
    H_IDX * D_IDX, D_IDX, H_IDX,
    H_SW * HEAD_DIM, KV_SW * HEAD_DIM, KV_SW * HEAD_DIM,
    N_BRANCH * D_MODEL,
)
N_IN = sum(IN_SIZES)

kernel_name = 'hybrid_gated_sb_dsa_swa_moe'

def rmsnorm(x, g):
    xf = x.astype(jnp.float32)
    y = xf * lax.rsqrt(jnp.mean(xf * xf, axis=-1, keepdims=True) + EPS)
    return (y * g.astype(jnp.float32)).astype(x.dtype)

def _split(t, sizes):
    return jnp.split(t, np.cumsum(sizes)[:-1].tolist(), axis=-1)

def t5_bucket(rel):
    n = jnp.maximum(rel, 0)
    max_exact = N_BUCKETS // 2
    nf = jnp.maximum(n, 1).astype(jnp.float32)
    large = max_exact + (jnp.log(nf / max_exact) / math.log(MAX_DISTANCE / max_exact)
                         * (N_BUCKETS - max_exact)).astype(jnp.int32)
    large = jnp.minimum(large, N_BUCKETS - 1)
    return jnp.where(n < max_exact, n, large)

def stick_breaking_attention(q, k, v):
    B_, S_, H, d = q.shape
    nblk = S_ // BLOCK
    scale = d ** -0.5
    kpos = jnp.arange(S_)

    def block(i):
        q0 = i * BLOCK
        qpos = q0 + jnp.arange(BLOCK)
        q_blk = lax.dynamic_slice_in_dim(q, q0, BLOCK, axis=1)
        z = jnp.einsum('bthd,bshd->bhts', q_blk, k, preferred_element_type=jnp.float32) * scale
        causal = kpos[None, :] < qpos[:, None]
        log_beta = jax.nn.log_sigmoid(z)
        log_keep = jnp.where(causal, jax.nn.log_sigmoid(-z), 0.0)
        rev = lax.cumsum(log_keep, axis=3, reverse=True) - log_keep
        att = jnp.where(causal, jnp.exp(log_beta + rev), 0.0)
        return jnp.einsum('bhts,bshd->bthd', att.astype(v.dtype), v)

    out = lax.map(block, jnp.arange(nblk))
    return out.transpose(1, 0, 2, 3, 4).reshape(B_, S_, H, d)

def dsa_attention(q, k, v, q_idx, k_idx, w_idx, bias_tab):
    B_, S_, H, d = q.shape
    topk = min(TOPK_MAX, S_ // 4)
    nblk = S_ // BLOCK
    kpos = jnp.arange(S_)
    gather = jax.vmap(lambda t, i: t[i])

    def block(i):
        q0 = i * BLOCK
        qpos = q0 + jnp.arange(BLOCK)
        q_blk = lax.dynamic_slice_in_dim(q, q0, BLOCK, axis=1)
        qi_blk = lax.dynamic_slice_in_dim(q_idx, q0, BLOCK, axis=1)
        wi_blk = lax.dynamic_slice_in_dim(w_idx, q0, BLOCK, axis=1)
        act = jax.nn.relu(jnp.einsum('bthe,bse->bths', qi_blk, k_idx,
                                     preferred_element_type=jnp.float32) * D_IDX ** -0.5)
        score = jnp.einsum('bth,bths->bts', wi_blk.astype(jnp.float32), act)
        score = jnp.where(kpos[None, None, :] <= qpos[None, :, None], score, -jnp.inf)
        _, idx = lax.top_k(score, topk)
        valid = idx <= qpos[None, :, None]
        k_sel = gather(k, idx)
        v_sel = gather(v, idx)
        s = jnp.einsum('bthd,btkd->bhtk', q_blk, k_sel, preferred_element_type=jnp.float32) * d ** -0.5
        bias = bias_tab[t5_bucket(qpos[None, :, None] - idx)]
        s = s + bias.transpose(0, 3, 1, 2).astype(jnp.float32)
        s = jnp.where(valid[:, None], s, -jnp.inf)
        p = jax.nn.softmax(s, axis=-1)
        return jnp.einsum('bhtk,btkd->bthd', p.astype(v.dtype), v_sel)

    out = lax.map(block, jnp.arange(nblk))
    return out.transpose(1, 0, 2, 3, 4).reshape(B_, S_, H, d)

def sliding_window_attention(q, k, v, sinks, bias_tab):
    B_, S_, H, d = q.shape
    G = H // KV_SW
    nblk = S_ // BLOCK
    qb = q.reshape(B_, nblk, BLOCK, KV_SW, G, d)
    kb = k.reshape(B_, nblk, BLOCK, KV_SW, d)
    vb = v.reshape(B_, nblk, BLOCK, KV_SW, d)
    pad = jnp.zeros_like(kb[:, :1])
    k2 = jnp.concatenate([jnp.concatenate([pad, kb[:, :-1]], axis=1), kb], axis=2)
    v2 = jnp.concatenate([jnp.concatenate([pad, vb[:, :-1]], axis=1), vb], axis=2)
    s = jnp.einsum('bnqkgd,bnjkd->bnkgqj', qb, k2, preferred_element_type=jnp.float32) * d ** -0.5
    kj = jnp.arange(2 * BLOCK)[None, :]
    rel = (jnp.arange(BLOCK)[:, None] + BLOCK) - kj
    in_win = (rel >= 0) & (rel < WINDOW)
    has_prev = (jnp.arange(nblk)[:, None, None] > 0) | (kj[None] >= BLOCK)
    mask = in_win[None] & has_prev
    bias = bias_tab[t5_bucket(rel)].transpose(2, 0, 1).reshape(KV_SW, G, BLOCK, 2 * BLOCK)
    s = s + bias[None, None].astype(jnp.float32)
    s = jnp.where(mask[None, :, None, None], s, -jnp.inf)
    sink = sinks.astype(jnp.float32).reshape(KV_SW, G)[None, None, :, :, None, None]
    m = jnp.maximum(jnp.max(s, axis=-1, keepdims=True), sink)
    e = jnp.exp(s - m)
    p = e / (jnp.sum(e, axis=-1, keepdims=True) + jnp.exp(sink - m))
    o = jnp.einsum('bnkgqj,bnjkd->bnqkgd', p.astype(v.dtype), v2)
    return o.reshape(B_, S_, H, d)

def cross_attention(xn, memn, w_q, w_kv, w_o, q_gain, k_gain):
    B_, S_, _ = xn.shape
    M = memn.shape[1]
    q = rmsnorm((xn @ w_q).reshape(B_, S_, H_X, XHEAD_DIM), q_gain)
    k, v = _split(memn @ w_kv, (H_X * XHEAD_DIM, H_X * XHEAD_DIM))
    k = rmsnorm(k.reshape(B_, M, H_X, XHEAD_DIM), k_gain)
    v = v.reshape(B_, M, H_X, XHEAD_DIM)
    s = jnp.einsum('bshd,bmhd->bhsm', q, k, preferred_element_type=jnp.float32) * XHEAD_DIM ** -0.5
    p = jax.nn.softmax(s, axis=-1)
    o = jnp.einsum('bhsm,bmhd->bshd', p.astype(v.dtype), v)
    return o.reshape(B_, S_, H_X * XHEAD_DIM) @ w_o

def swiglu(h, w_gu, w_down):
    g, u = jnp.split(h @ w_gu, 2, axis=-1)
    return (jax.nn.silu(g) * u) @ w_down

def moe_swiglu(h, w_router, w_gu, w_down):
    B_, S_, D = h.shape
    t = h.reshape(-1, D)
    logits = jnp.dot(t, w_router, preferred_element_type=jnp.float32)
    top_val, top_idx = lax.top_k(logits, TOP_K_EXPERTS)
    top_gate = jax.nn.softmax(top_val, axis=-1)
    gate = jnp.sum(jax.nn.one_hot(top_idx, N_EXPERTS, dtype=jnp.float32) * top_gate[..., None], axis=1)
    out = jnp.zeros(t.shape, jnp.float32)
    for e in range(N_EXPERTS):
        out = out + gate[:, e:e + 1] * swiglu(t, w_gu[e], w_down[e]).astype(jnp.float32)
    return out.astype(h.dtype).reshape(B_, S_, D)

def setup_inputs(seed: int = 0) -> dict:
    key = jax.random.key(seed)
    ks = iter(jax.random.split(key, 32))
    D = D_MODEL

    def nrm(shape, scale):
        return jax.random.normal(next(ks), shape, jnp.float32) * scale

    def gain(shape):
        return 1.0 + nrm(shape, 0.02)

    w_a = H_SB * HEAD_DIM
    w_b = H_DSA * HEAD_DIM
    w_c = H_SW * HEAD_DIM
    w_x = H_X * XHEAD_DIM
    return {
        'x': nrm((BATCH, SEQ, D), 1.0),
        'mem': nrm((BATCH, N_MEM, D), 1.0),
        'rel_bias': nrm((N_BUCKETS, H_DSA + H_SW), 0.2),
        'norm_mix': gain((DEPTH, D)),
        'w_in': nrm((DEPTH, D, N_IN), D ** -0.5),
        'b_gate': nrm((DEPTH, N_BRANCH, D), 0.02),
        'qn_dsa': gain((DEPTH, HEAD_DIM)),
        'kn_dsa': gain((DEPTH, HEAD_DIM)),
        'qn_swa': gain((DEPTH, HEAD_DIM)),
        'kn_swa': gain((DEPTH, HEAD_DIM)),
        'sinks': nrm((DEPTH, H_SW), 0.5),
        'w_pa': nrm((DEPTH, w_a, D), w_a ** -0.5),
        'w_pb': nrm((DEPTH, w_b, D), w_b ** -0.5),
        'w_pc': nrm((DEPTH, w_c, D), w_c ** -0.5),
        'w_out': nrm((DEPTH, D, D), D ** -0.5),
        'norm_x': gain((DEPTH, D)),
        'norm_mem': gain((DEPTH, D)),
        'w_xq': nrm((DEPTH, D, w_x), D ** -0.5),
        'w_xkv': nrm((DEPTH, D, 2 * w_x), D ** -0.5),
        'w_xo': nrm((DEPTH, w_x, D), w_x ** -0.5),
        'qn_x': gain((DEPTH, XHEAD_DIM)),
        'kn_x': gain((DEPTH, XHEAD_DIM)),
        'norm_ffn': gain((DEPTH, D)),
        'w_gu_dense': nrm((N_DENSE_LAYERS, D, 2 * D_FF_DENSE), D ** -0.5),
        'w_down_dense': nrm((N_DENSE_LAYERS, D_FF_DENSE, D), D_FF_DENSE ** -0.5),
        'w_router': nrm((N_MOE_LAYERS, D, N_EXPERTS), D ** -0.5),
        'w_gu_moe': nrm((N_MOE_LAYERS, N_EXPERTS, D, 2 * D_FF_EXPERT), D ** -0.5),
        'w_down_moe': nrm((N_MOE_LAYERS, N_EXPERTS, D_FF_EXPERT, D), D_FF_EXPERT ** -0.5),
    }

def reference(x, mem, rel_bias, norm_mix, w_in, b_gate, qn_dsa, kn_dsa, qn_swa, kn_swa, sinks,
              w_pa, w_pb, w_pc, w_out, norm_x, norm_mem, w_xq, w_xkv, w_xo, qn_x, kn_x,
              norm_ffn, w_gu_dense, w_down_dense, w_router, w_gu_moe, w_down_moe):
    B_, S_, D = x.shape
    bias_dsa = rel_bias[:, :H_DSA]
    bias_swa = rel_bias[:, H_DSA:]

    def heads(t, n, d):
        return t.reshape(B_, S_, n, d)

    for l in range(DEPTH):
        h = rmsnorm(x, norm_mix[l])
        qa, ka, va, qb, kb, vb, qi, ki, wi, qc, kc, vc, g = _split(h @ w_in[l], IN_SIZES)
        o_a = stick_breaking_attention(heads(qa, H_SB, HEAD_DIM), heads(ka, H_SB, HEAD_DIM),
                                       heads(va, H_SB, HEAD_DIM))
        o_b = dsa_attention(rmsnorm(heads(qb, H_DSA, HEAD_DIM), qn_dsa[l]), rmsnorm(kb, kn_dsa[l]), vb,
                            heads(qi, H_IDX, D_IDX), ki, wi, bias_dsa)
        o_c = sliding_window_attention(rmsnorm(heads(qc, H_SW, HEAD_DIM), qn_swa[l]),
                                       rmsnorm(heads(kc, KV_SW, HEAD_DIM), kn_swa[l]),
                                       heads(vc, KV_SW, HEAD_DIM), sinks[l], bias_swa)
        gates = jax.nn.sigmoid((g.reshape(B_, S_, N_BRANCH, D) + b_gate[l]).astype(jnp.float32)).astype(x.dtype)
        merged = (gates[:, :, 0] * (o_a.reshape(B_, S_, -1) @ w_pa[l])
                  + gates[:, :, 1] * (o_b.reshape(B_, S_, -1) @ w_pb[l])
                  + gates[:, :, 2] * (o_c.reshape(B_, S_, -1) @ w_pc[l]))
        x = x + merged @ w_out[l]
        x = x + cross_attention(rmsnorm(x, norm_x[l]), rmsnorm(mem, norm_mem[l]),
                                w_xq[l], w_xkv[l], w_xo[l], qn_x[l], kn_x[l])
        hf = rmsnorm(x, norm_ffn[l])
        if l % 2 == 0:
            x = x + swiglu(hf, w_gu_dense[l // 2], w_down_dense[l // 2])
        else:
            x = x + moe_swiglu(hf, w_router[l // 2], w_gu_moe[l // 2], w_down_moe[l // 2])
    return x


_drawn_inputs = setup_inputs


def setup_inputs(seed=0):
    import zlib

    import numpy as np

    out = dict(_drawn_inputs(seed))
    spreads = {}
    factors = {'b_gate': 2.764,
     'qn_dsa': 3.494,
     'kn_dsa': 2.748,
     'qn_swa': 8.0,
     'kn_swa': 8.0,
     'sinks': 16.479,
     'norm_x': 2.776,
     'qn_x': 3.154,
     'kn_x': 8.0}
    for name, (base, spread) in spreads.items():
        noise = np.random.default_rng([zlib.crc32(name.encode()), seed]).standard_normal(out[name].shape)
        drawn = base * np.exp(spread * noise) if base else spread * noise
        out[name] = __import__('jax').numpy.asarray(drawn.astype(out[name].dtype))
    for name, factor in factors.items():
        out[name] = (out[name] * factor).astype(out[name].dtype)
    return out
```

```python
import math
from contextlib import ExitStack

import concourse.bass as bass
from concourse import mybir

F32 = mybir.dt.float32
F32R = mybir.dt.float32r
I32 = mybir.dt.int32
U32 = mybir.dt.uint32
ALU = mybir.AluOpType
ACT = mybir.ActivationFunctionType
AX = mybir.AxisListType

P = 128
EPS = 1e-6
BIG = 1e30
TAKEN = -3e38
HD = 64
TOPK = 64
SLOT = 2048
RING = 3
FC = 256
NB = 512
COL = dict(qa=0, ka=256, va=512, qb=768, kb=1024, vb=1088, qi=1152, ki=1408, wi=1472, qc=1476, kc=1988,
           vc=2116, g=2244)


def build(nc, t, out):
    L, D, N_IN = t["w_in"].shape
    S = t["x"].shape[1]
    TT = S // P
    KC = D // P
    F_DENSE = t["w_down_dense"].shape[1]
    N_EXP, F_MOE = t["w_down_moe"].shape[1:3]
    H = 12
    N_DENSE, N_MOE = F_DENSE // FC, F_MOE // FC
    assert (S, D, TT, KC) == (256, 1024, 2, 8)

    plan = []

    def add_block(w, row0, kcs, c0, n):
        v = w[row0:row0 + P * kcs, c0:c0 + n].rearrange("(k p) n -> p k n", p=P)
        plan.append((v, kcs, n))

    blocks = {}

    def add_linear(name, l, w, k, n):
        blocks[name, l] = len(plan)
        for c0 in range(0, n, NB):
            for r0 in range(0, k, 4 * P):
                add_block(w, r0, min(4, (k - r0) // P), c0, min(NB, n - c0))

    FFN0 = {}
    for l in range(L):
        add_linear("in", l, t["w_in"][l], D, N_IN)
        add_linear("xkv", l, t["w_xkv"][l], D, 1024)
        add_linear("pa", l, t["w_pa"][l], 256, D)
        add_linear("pb", l, t["w_pb"][l], 256, D)
        add_linear("pc", l, t["w_pc"][l], 512, D)
        add_linear("out", l, t["w_out"][l], D, D)
        add_linear("xq", l, t["w_xq"][l], D, 512)
        add_linear("xo", l, t["w_xo"][l], 512, D)
        FFN0[l] = len(plan)
        if l == 0:
            plan.extend([(None, 4, NB)] * (3 * (F_DENSE // FC)))
    n_in_blocks = -(-N_IN // NB)
    order = [("in", n_in_blocks), ("xkv", 2), ("pa", 2), ("pb", 2), ("pc", 2), ("out", 2), ("xq", 1), ("xo", 2)]
    per_layer = sum(n for _, n in order)
    blk0 = {}
    for l in range(L):
        at = l * per_layer
        for name, n in order:
            blk0[name, l] = at
            at += n

    ctx = ExitStack()
    with ctx:
        def sb(name, shape, dt=F32):
            return ctx.enter_context(nc.sbuf_tensor(name, shape, dt))

        sems = {}

        def sem(name):
            if name not in sems:
                sems[name] = ctx.enter_context(nc.semaphore(name))
            return sems[name]

        raw = sb("raw", [P, RING, SLOT])
        w_hi = sb("w_hi", [P, RING, SLOT], F32R)
        w_lo = sb("w_lo", [P, RING, SLOT], F32R)
        x_sb = sb("x_sb", [P, TT, D])
        z = sb("z", [P, TT, N_IN])
        scratch = sb("scratch", [P, 6144])
        hT_hi = sb("hT_hi", [P, KC, S], F32R)
        hT_lo = sb("hT_lo", [P, KC, S], F32R)
        headsT = sb("headsT", [P, 15, S])
        mem_kv = sb("mem_kv", [P, 2, 1024])
        bias = sb("bias", [P, H, 2 * P])
        aT_hi = sb("aT_hi", [P, 2, S], F32R)
        aT_lo = sb("aT_lo", [P, 2, S], F32R)
        consts = sb("consts", [P, 6, P])
        gains = sb("gains", [P, 64])
        hgain = sb("hgain", [P, 256])
        sel_add = sb("sel_add", [P, 3 * P])
        sink = sb("sink", [P, 8])
        w_router = sb("w_router", [P, KC, N_EXP])
        st = sb("st", [P, 176])
        n_iter = sb("n_iter", [1, 1], I32)
        idx8 = sb("idx8", [P, TT, 8], U32)
        ident, after_tri, ones, before_tri, iota, causal_add = (consts[:, i, :] for i in range(6))

        ps = ctx.enter_context(nc.psum_tensor("ps", [P, 8, NB], F32))
        psf = ps[:, :, :].rearrange("p b n -> p (b n)")
        scratch_dram = nc.dram_tensor("bias_by_distance", (H, P, 3 * P), F32, kind="Internal").ap()

        sc = scratch[:, :]
        xn = sc[:, 0:2048].rearrange("p (t d) -> p t d", t=TT)
        hTf = sc[:, 2048:4096].rearrange("p (k s) -> p k s", k=KC)
        mem_n = sc[:, 4096:6144].rearrange("p (t d) -> p t d", t=TT)
        heads_n = sc[:, 1920:4224].rearrange("p (t d) -> p t d", t=TT)
        gates = z[:, :, COL["g"]:]
        ss, var, rstd, tmp = st[:, 0:32], st[:, 32:64], st[:, 64:96], st[:, 96:128]
        mx, negm, rsum = st[:, 128:140], st[:, 140:152], st[:, 152:164]
        s8 = st[:, 164:176]

        def bc(ap, shape):
            return ap.to_broadcast(shape)

        def raw_val(s):
            return 32 * (s // RING + 1)

        def load_slot(sp, s):
            src, kcs, n = plan[s]
            dst = raw[:, s % RING, 0:kcs * n].rearrange("p (k n) -> p k n", k=kcs)
            h = kcs // 2
            sp.dma_start(dst[:, 0:h, :], src[:, 0:h, :]).then_inc(sem(f"raw_full{s % RING}"), 16)
            sp.dma_start(dst[:, h:, :], src[:, h:, :]).then_inc(sem(f"raw_full{s % RING}"), 16)

        def load_gu(sp, ring, w, c, half, F):
            dst = raw[:, ring, :].rearrange("p (k n) -> p k n", k=4)
            rows = w[half * 4 * P:(half + 1) * 4 * P]
            for i in range(2):
                src = rows[:, bass.ds(c * FC + i * F, FC)].rearrange("(k p) n -> p k n", p=P)
                sp.dma_start(dst[:, :, i * FC:(i + 1) * FC], src).then_inc(sem(f"raw_full{ring}"), 16)

        def load_down(sp, ring, w, c):
            dst = raw[:, ring, :].rearrange("p (k n) -> p k n", k=2)
            for k in range(2):
                sp.dma_start(dst[:, k, :], w[bass.ds(c * FC + k * P, P), :]).then_inc(sem(f"raw_full{ring}"), 16)

        def sp_ffn(sp, s0, off, w_gu, w_down, F, n):
            def free(s):
                sp.wait_ge(sem("lo_done"), off + (s - RING + 1))
            for half in range(2):
                free(s0 + half)
                load_gu(sp, (s0 + half) % RING, w_gu, 0, half, F)
            with sp.Fori(1, n) as c:
                for half in range(2):
                    free(c * 3 + (s0 - 1 + half))
                    load_gu(sp, (s0 - 1 + half) % RING, w_gu, c, half, F)
                free(c * 3 + (s0 + 1))
                load_down(sp, (s0 + 1) % RING, w_down, c - 1)
            free(s0 + 3 * n - 1)
            load_down(sp, (s0 + 3 * n - 1) % RING, w_down, n - 1)

        def sp_program(sp):
            for l in range(L):
                for s in range(blocks["in", l], FFN0[l]):
                    if s >= RING:
                        sp.wait_ge(sem("lo_done"), s - RING + 1)
                    load_slot(sp, s)
                if l == 0:
                    sp_ffn(sp, FFN0[0], 0, t["w_gu_dense"][0], t["w_down_dense"][0], F_DENSE, N_DENSE)
            sp.wait_ge(sem("routed"), 1)
            n_it = sp.value_load(n_iter[0:1, 0:1], min_val=N_EXP, max_val=2 * N_EXP)
            wg = t["w_gu_moe"][0].rearrange("e d f -> (e d) f")
            wd = t["w_down_moe"][0].rearrange("e f d -> (e f) d")
            with sp.Fori(0, n_it) as it:
                e = it % N_EXP
                sp_ffn(sp, FFN0[1], it * (3 * N_MOE), wg[bass.ds(e * D, D), :], wd[bass.ds(e * F_MOE, F_MOE), :],
                       F_MOE, N_MOE)
            sp.wait_ge(sem("x_final"), 1)
            sp.dma_start(out[0].rearrange("(t p) d -> p t d", p=P), x_sb[:, :, :]).then_inc(sem("stored"), 16)
            sp.wait_ge(sem("stored"), 16)

        set_up = headsT[:, 0:4, :].rearrange("p b s -> p (b s)")
        gain_rows, rel_rows = set_up[0:64, 0:P], set_up[0:32, P:P + H]
        bucket_rows, dist_rows = set_up[0:32, 2 * P:5 * P], set_up[0:H, 5 * P:8 * P]
        window = sel_add[:, 0:2 * P]

        def preset_z(pool, l):
            pool.memset(z[:, :, 0:COL["g"]], 0.0).then_inc(sem("z_zero"), 1)
            bg = t["b_gate"][l:l + 1].rearrange("a b d -> a (b d)")
            for i in range(TT):
                pool.dma_start(z[:, i, COL["g"]:], bg.to_broadcast([P, N_IN - COL["g"]])).then_inc(sem("z_bias"), 16)

        def load_memory(pool):
            pool.dma_start(mem_n, t["mem"][0].rearrange("(t p) d -> p t d", p=P)).then_inc(sem("mem_in"), 16)

        def load_head_gains(pool, l):
            pool.dma_start(sink[:, :], t["sinks"][l:l + 1].to_broadcast([P, 8])).then_inc(sem("hgain_in"), 16)
            for i, name in enumerate(("qn_dsa", "kn_dsa", "qn_swa", "kn_swa")):
                pool.dma_start(hgain[:, HD * i:HD * (i + 1)], t[name][l:l + 1].to_broadcast([P, HD])) \
                    .then_inc(sem("hgain_in"), 16)

        def load_cross_gains(pool, l):
            pool.wait_ge(sem("heads_n"), l + 1)
            for i, name in enumerate(("qn_x", "kn_x")):
                pool.dma_start(hgain[:, P * i:P * i + P], t[name][l:l + 1].to_broadcast([P, P])) \
                    .then_inc(sem("xgain_in"), 16)

        def pool_program(pool):
            load_memory(pool)
            pool.dma_start(consts[:, :, :], t["c_tiles"].rearrange("i p n -> p i n")).then_inc(sem("const_in"), 16)
            for i, name in enumerate(("norm_mix", "norm_mem", "norm_x", "norm_ffn")):
                pool.dma_start(gain_rows[16 * i:16 * i + 16, :], t[name].rearrange("l (c p) -> (l c) p", p=P)) \
                    .then_inc(sem("gain_in"), 16)
            pool.dma_start(rel_rows, t["rel_bias"]).then_inc(sem("gain_in"), 16)
            pool.dma_start(bucket_rows, t["c_bucket"]).then_inc(sem("gain_in"), 16)
            preset_z(pool, 0)
            load_head_gains(pool, 0)
            pool.wait_ge(sem("dist_sb"), 1)
            pool.dma_start(scratch_dram, dist_rows.unsqueeze(1).to_broadcast([H, P, 3 * P])) \
                .then_inc(sem("dist_out"), 16)
            pool.dma_start(window, t["c_window"]).then_inc(sem("bias_in"), 16)
            pool.dma_start(w_router[:, :, :], t["w_router"][0].rearrange("(k p) e -> p k e", p=P)) \
                .then_inc(sem("router_in"), 16)
            pool.wait_ge(sem("dist_out"), 16)
            for i, h in enumerate([0, 2, 1, 3] + list(range(4, H))):
                src = bass.AP(scratch_dram.tensor, h * 3 * P * P + P - 1, [[3 * P - 1, P], [1, 2 * P]])
                pool.dma_start(bias[:, i, :], src).then_inc(sem("bias_in"), 16)
            load_cross_gains(pool, 0)
            for l in range(1, L):
                pool.wait_ge(sem("merged"), l)
                preset_z(pool, l)
                pool.wait_ge(sem("x_heads_n"), l)
                load_head_gains(pool, l)
                pool.wait_ge(sem("ffn_added"), l)
                load_memory(pool)
                load_cross_gains(pool, l)

        class Count:
            def __init__(self):
                self.n = 0

        def act_split(act, ring, width, raw_v, free_v):
            act.wait_ge(sem(f"raw_full{ring}"), raw_v)
            if free_v is not None:
                act.wait_ge(sem("mm_done"), free_v)
            act.activation(w_hi[:, ring, 0:width], raw[:, ring, 0:width], ACT.Copy).then_inc(sem("hi_done"), 1)

        def dve_split(v, ring, width, hi_v):
            v.wait_ge(sem("hi_done"), hi_v)
            v.tensor_tensor(w_lo[:, ring, 0:width], raw[:, ring, 0:width], w_hi[:, ring, 0:width].bitcast(F32),
                            ALU.subtract).then_inc(sem("lo_done"), 1)

        def act_split_to(act, cnt, end):
            while cnt.n < end:
                s = cnt.n
                _, kcs, n = plan[s]
                act_split(act, s % RING, kcs * n, raw_val(s), s - RING + 1 if s >= RING else None)
                cnt.n += 1

        def dve_split_to(v, cnt, end):
            while cnt.n < end:
                s = cnt.n
                _, kcs, n = plan[s]
                dve_split(v, s % RING, kcs * n, s + 1)
                cnt.n += 1

        def slots_of(name, l):
            nblk = dict(order)[name]
            k2 = 2 if name in ("in", "xkv", "out", "xq") else 1
            return blocks[name, l], nblk, k2

        def ahead(split_to, eng, cnt, last, limit):
            split_to(eng, cnt, min(last + RING, limit))

        RS = {"mix": 0, "heads": 1, "x": 2, "xqk": 3, "ffn": 4}
        RS_N = {"mix": 4, "heads": 30, "x": 2, "xqk": 16, "ffn": 2}

        def act_rsqrt(act, name, l):
            n, k = RS_N[name], len(RS) * l + RS[name]
            act.wait_ge(sem("var"), k + 1)
            act.activation(tmp[:, 0:n], var[:, 0:n], ACT.Ln)
            act.drain()
            act.activation(rstd[:, 0:n], tmp[:, 0:n], ACT.Exp, scale=-0.5).then_inc(sem("rs0"), 1)

        def dve_rsqrt(v, name, l, width):
            n, k = RS_N[name], len(RS) * l + RS[name]
            v.drain()
            v.tensor_scalar(var[:, 0:n], ss[:, 0:n], 1.0 / width, EPS, ALU.mult, ALU.add).then_inc(sem("var"), 1)
            v.wait_ge(sem("rs0"), k + 1)
            v.tensor_tensor(tmp[:, 0:n], rstd[:, 0:n], rstd[:, 0:n], ALU.mult)
            v.drain()
            v.tensor_tensor(tmp[:, 0:n], tmp[:, 0:n], var[:, 0:n], ALU.mult)
            v.drain()
            v.tensor_scalar(tmp[:, 0:n], tmp[:, 0:n], -0.5, 1.5, ALU.mult, ALU.add)
            v.drain()
            return v.tensor_tensor(rstd[:, 0:n], rstd[:, 0:n], tmp[:, 0:n], ALU.mult)

        def dve_sumsq(v, src, junk, col):
            for i in range(TT):
                v.tensor_tensor_reduce(junk, src[:, i, :], src[:, i, :], 1.0, 0.0, ALU.mult, ALU.add,
                                       ss[:, col + i:col + i + 1])
                v.drain()

        def pe_turn(pe, name, src, nchunk=KC):
            for half in range(2):
                ks = range(half * nchunk // 2, (half + 1) * nchunk // 2)
                for k in ks:
                    for i in range(TT):
                        ins = pe.transpose(psf[:, k * S + i * P:k * S + (i + 1) * P], src[:, i, k * P:(k + 1) * P],
                                           ident)
                ins.then_inc(sem(name + "_T"), 1)

        def halves(nchunk=KC):
            return [(i, slice(i * nchunk // 2, (i + 1) * nchunk // 2)) for i in range(2)]

        psT = psf[:, 0:KC * S].rearrange("p (k s) -> p k s", k=KC)
        GAIN = {"mix": 0, "mem": 1, "x": 2, "ffn": 3}

        def dve_gain(v, name, l):
            g0 = (GAIN[name] * L + l) * KC
            for i, ks in halves():
                v.wait_ge(sem(name + "_T"), 2 * l + i + 1)
                g = gains[:, g0 + ks.start:g0 + ks.stop].unsqueeze(2)
                v.tensor_tensor(hTf[:, ks, :], psT[:, ks, :], bc(g, [P, KC // 2, S]), ALU.mult) \
                    .then_inc(sem(name + "_F"), 1)

        def act_hi(act, name, l, src, ready, nchunk=KC, mm=None):
            if mm is not None:
                act.wait_ge(sem("mm_done"), mm)
            for i, ks in halves(nchunk):
                act.wait_ge(sem(ready), 2 * l + i + 1)
                act.activation(hT_hi[:, ks, :], src[:, ks, :], ACT.Copy).then_inc(sem(name + "_H"), 1)

        def dve_lo(v, name, l, src, nchunk=KC):
            for i, ks in halves(nchunk):
                v.wait_ge(sem(name + "_H"), 2 * l + i + 1)
                v.tensor_tensor(hT_lo[:, ks, :], src[:, ks, :], hT_hi[:, ks, :].bitcast(F32), ALU.subtract) \
                    .then_inc(sem(name + "_L"), 1)

        def pe_products(pe, acc, hk, wk, start, stop, hi=hT_hi, lo=hT_lo):
            for j, ((k, cols), (wh, wl)) in enumerate(zip(hk, wk)):
                a, b = hi[:, k, cols], lo[:, k, cols]
                last = j == len(hk) - 1
                pe.matmul(acc, a, wh, start=start and j == 0, stop=False)
                pe.matmul(acc, b, wh, start=False, stop=False)
                ins = pe.matmul(acc, a, wl, start=False, stop=stop and last)
            return ins

        def pe_block_slot(pe, ring, kcs, n, k0, lo_v, first, final, blk_v, tile_done=True):
            pe.wait_ge(sem("lo_done"), lo_v)
            wh = w_hi[:, ring, 0:kcs * n].rearrange("p (k n) -> p k n", k=kcs)
            wl = w_lo[:, ring, 0:kcs * n].rearrange("p (k n) -> p k n", k=kcs)
            for i in range(TT):
                if first and blk_v[i] is not None:
                    pe.wait_ge(sem("evac"), blk_v[i])
                cols = slice(i * P, (i + 1) * P)
                ins = pe_products(pe, ps[:, 4 + i, 0:n], [(k0 + k, cols) for k in range(kcs)],
                                  [(wh[:, k, :], wl[:, k, :]) for k in range(kcs)], first, final)
                if i == 0 and final:
                    ins.then_inc(sem("tile0_done"), 1)
            ins.then_inc(sem("mm_done"), 1)

        def pe_linear(pe, name, l, k0=0, b0=0, nblk=None):
            s, nb_all, per = slots_of(name, l)
            nblk = nblk or nb_all
            for b in range(b0, nblk):
                blk = blk0[name, l] + b
                for h in range(per):
                    ss_ = s + b * per + h
                    _, kcs, n = plan[ss_]
                    evs = [2 * blk - 1 + i if blk else None for i in range(TT)]
                    pe_block_slot(pe, ss_ % RING, kcs, n, k0 + 4 * h, ss_ + 1, h == 0, h == per - 1, evs)

        def dve_linear(v, cnt, name, l, take, limit, b0=0):
            s, nblk, per = slots_of(name, l)
            for b in range(b0, nblk):
                last = s + (b + 1) * per - 1
                ahead(dve_split_to, v, cnt, last, limit)
                blk = blk0[name, l] + b
                v.wait_ge(sem("tile0_done"), blk + 1)
                take(b, 0).then_inc(sem("evac"), 1)
                v.wait_ge(sem("mm_done"), last + 1)
                take(b, 1).then_inc(sem("evac"), 1)

        IN_LOOP = 3

        def pe_win(pe, l):
            s0, b00 = blocks["in", l], blk0["in", l]
            if l == 0:
                pe_linear(pe, "in", l, nblk=3)
            it0 = 1 if l == 0 else 0
            with pe.Fori(it0, IN_LOOP) as i:
                for j in range(6):
                    s = i * 6 + (s0 + j)
                    b = i * 3 + (b00 + j // 2)
                    evs = [b * 2 + (q - 1) for q in range(TT)]
                    pe_block_slot(pe, (s0 + j) % RING, 4, NB, 4 * (j % 2), s + 1, j % 2 == 0, j % 2 == 1, evs)
            pe_linear(pe, "in", l, b0=9)

        def act_win(act, l, cnt, limit):
            s0 = blocks["in", l]
            act_split_to(act, cnt, s0 + 3)
            with act.Fori(0, IN_LOOP) as i:
                for j in range(6):
                    s = i * 6 + (s0 + 3 + j)
                    base = s0 + 3 + j
                    act_split(act, base % RING, SLOT, i * 64 + raw_val(base), s - RING + 1)
            cnt.n = s0 + 21
            act_split_to(act, cnt, limit)

        def dve_win(v, l, cnt, limit):
            s0, b00 = blocks["in", l], blk0["in", l]
            dve_split_to(v, cnt, s0 + 2)
            v.wait_ge(sem("z_zero"), l + 1)
            v.wait_ge(sem("z_bias"), 32 * (l + 1))
            with v.Fori(0, IN_LOOP) as i:
                for j in range(3):
                    for h in range(2):
                        s = i * 6 + (s0 + 2 + 2 * j + h)
                        dve_split(v, (s0 + 2 + 2 * j + h) % RING, SLOT, s + 1)
                    b = i * 3 + j
                    dst = z[:, :, bass.ds(b * NB, NB)]
                    v.wait_ge(sem("tile0_done"), b + (b00 + 1))
                    v.tensor_tensor(dst[:, 0, :], ps[:, 4, :], dst[:, 0, :], ALU.add).then_inc(sem("evac"), 1)
                    v.wait_ge(sem("mm_done"), i * 6 + (s0 + 2 * j + 2))
                    v.tensor_tensor(dst[:, 1, :], ps[:, 5, :], dst[:, 1, :], ALU.add).then_inc(sem("evac"), 1)
            cnt.n = s0 + 20

            def take(b, i):
                n = min(NB, N_IN - b * NB)
                dst = z[:, i, b * NB:b * NB + n]
                return v.tensor_tensor(dst, ps[:, 4 + i, 0:n], dst, ALU.add)
            dve_linear(v, cnt, "in", l, take, limit, b0=9)

        a_sb = headsT[:, 0:2, :]
        silu_sb = headsT[:, 2:4, :]

        def psA(T):
            return ps[:, 6, 0:2 * T * P].rearrange("p (f s) -> p f s", f=2)

        def pe_ffn(pe, s0, off, coff, T, n):
            def gate_up(c, half):
                s, ring = c * 3 + (s0 - 1 + half), (s0 - 1 + half) % RING
                if isinstance(c, int) and c == 0:
                    s, ring = s0 + half, (s0 + half) % RING
                pe.wait_ge(sem("lo_done"), off + (s + 1))
                wh = w_hi[:, ring, :].rearrange("p (k n) -> p k n", k=4)
                wl = w_lo[:, ring, :].rearrange("p (k n) -> p k n", k=4)
                for i in range(T):
                    ins = pe_products(pe, ps[:, 4 + i, :], [(4 * half + k, slice(i * P, (i + 1) * P)) for k in range(4)],
                                      [(wh[:, k, :], wl[:, k, :]) for k in range(4)], half == 0, half == 1)
                ins.then_inc(sem("mm_done"), 1)

            def turn(c):
                pe.wait_ge(sem("act_done"), coff + (c + 1))
                for i in range(T):
                    for f in range(2):
                        ins = pe.transpose(ps[:, 6, (f * T + i) * P:(f * T + i + 1) * P],
                                           a_sb[:, i, f * P:(f + 1) * P], ident)
                ins.then_inc(sem("aT_turned"), 1)

            def down(c, s, ring, first, last):
                pe.wait_ge(sem("lo_done"), off + (s + 1))
                pe.wait_ge(sem("aT_split"), coff + (c + 1))
                wh = w_hi[:, ring, :].rearrange("p (k n) -> p k n", k=2)
                wl = w_lo[:, ring, :].rearrange("p (k n) -> p k n", k=2)
                for i in range(T):
                    for h in range(2):
                        cols = slice(h * NB, (h + 1) * NB)
                        ins = pe_products(pe, ps[:, 2 * i + h, :], [(f, slice(i * P, (i + 1) * P)) for f in range(2)],
                                          [(wh[:, f, cols], wl[:, f, cols]) for f in range(2)], first, last,
                                          hi=aT_hi, lo=aT_lo)
                ins.then_inc(sem("mm_done"), 1)

            def chunk(c, first):
                pe.wait_ge(sem("act_done"), coff + c)
                gate_up(c, 0)
                turn(c - 1)
                gate_up(c, 1)
                down(c - 1, c * 3 + (s0 + 1), (s0 + 1) % RING, first, False)

            gate_up(0, 0)
            gate_up(0, 1)
            chunk(1, True)
            with pe.Fori(2, n) as c:
                chunk(c, False)
            turn(n - 1)
            down(n - 1, s0 + 3 * n - 1, (s0 + 3 * n - 1) % RING, False, True)

        def split_order(split, act_of, aT_of, s0, n, fori):
            split(0, s0)
            split(0, s0 + 1)
            split(0, s0 + 2)
            act_of(0, s0 + 1)
            split(0, s0 + 3)
            with fori(1, n - 1) as c:
                split(c, s0 + 1)
                aT_of(c - 1)
                split(c, s0 + 2)
                act_of(c, s0)
                split(c, s0 + 3)
            split(n - 1, s0 + 1)
            aT_of(n - 2)
            act_of(n - 1, s0)
            split(n - 1, s0 + 2)
            aT_of(n - 1)

        def act_ffn(act, s0, off, coff, T, n):
            def split(c, base):
                act_split(act, base % RING, SLOT, (coff + c) * 32 + (raw_val(base) - 32 * coff_of[s0]),
                          off + (c * 3 + (base - RING + 1)))

            def silu(c, base):
                act.wait_ge(sem("mm_done"), off + (c * 3 + (base + 1)))
                act.activation(silu_sb[:, 0:T, :], ps[:, 4:4 + T, 0:FC], ACT.Silu).then_inc(sem("silu"), 1)

            def aT(c):
                act.wait_ge(sem("aT_turned"), coff + (c + 1))
                act.activation(aT_hi[:, :, 0:T * P], psA(T), ACT.Copy).then_inc(sem("aT_hi"), 1)
            split_order(split, silu, aT, s0, n, act.Fori)

        def dve_ffn(v, s0, off, coff, T, n):
            def split(c, base):
                dve_split(v, base % RING, SLOT, off + (c * 3 + (base + 1)))

            def gated(c, base):
                v.wait_ge(sem("silu"), coff + (c + 1))
                v.tensor_tensor(a_sb[:, 0:T, :], ps[:, 4:4 + T, FC:], silu_sb[:, 0:T, :], ALU.mult) \
                    .then_inc(sem("act_done"), 1)

            def aT(c):
                v.wait_ge(sem("aT_hi"), coff + (c + 1))
                v.tensor_tensor(aT_lo[:, :, 0:T * P], psA(T), aT_hi[:, :, 0:T * P].bitcast(F32), ALU.subtract) \
                    .then_inc(sem("aT_split"), 1)
            split_order(split, gated, aT, s0, n, v.Fori)

        coff_of = {FFN0[0]: 0, FFN0[1]: N_DENSE}

        def add_to_x(v):
            def take(b, i):
                dst = x_sb[:, i, b * NB:(b + 1) * NB]
                return v.tensor_tensor(dst, ps[:, 4 + i, :], dst, ALU.add)
            return take

        QA, KA, QI, KI, QB, KB, QC, KCC = 0, 2, 4, 6, 7, 9, 10, 14
        T1, T2, T3 = sc[:, 0:1536], sc[:, 1536:3072], sc[:, 3072:4608]
        IDX = {1: sc[:, 4608:5632].rearrange("p (h s) -> p h s", h=4),
               0: sc[:, 5632:6144].rearrange("p (h s) -> p h s", h=4)}
        W = {0: P, 1: 2 * P}
        SEL = {1: sel_add[:, 0:2 * P], 0: sel_add[:, 2 * P:3 * P]}
        psS = psf[:, 0:H * 2 * P].rearrange("p (h s) -> p h s", h=H)
        psPT = psf[:, 0:2 * H * P].rearrange("p (s h q) -> p s h q", s=2, h=H)
        PT = sc[:, 3072:6144].rearrange("p (s h q) -> p s h q", s=2, h=H)
        psO = psf[:, 6 * NB:6 * NB + 6 * P].rearrange("p (c q) -> p c q", c=6)

        def probs(tt):
            return sc[:, 0:H * W[tt]].rearrange("p (h s) -> p h s", h=H)

        def diag(ap, n):
            return [ap[:, 0:1024].rearrange("p (h s) -> p h s", h=4)[:, :, 0:P],
                    ap[:, 1024:1536].rearrange("p (h s) -> p h s", h=4)]

        def za_parts(ap):
            return ap[:, 0:1024], ap[:, 1024:1536]

        ps_za = (psf[:, 0:1024], ps[:, 2:4, 0:256])

        def part2(ap):
            return ap.rearrange("p (b n) -> p b n", b=2)

        xq_n = sc[:, 4096:5120].rearrange("p (t d) -> p t d", t=TT)
        xq_h = sc[:, 5120:6144].rearrange("p (t d) -> p t d", t=TT)
        xk_h = sc[:, 0:1024].rearrange("p (t d) -> p t d", t=TT)
        xk_n = mem_kv[:, 0, :].rearrange("p (t d) -> p t d", t=TT)
        xv_n = mem_kv[:, 1, :].rearrange("p (t d) -> p t d", t=TT)
        xP = sc[:, 0:2048].rearrange("p (g s) -> p g s", g=8)
        xPT = sc[:, 2048:4096].rearrange("p (m h q) -> p m h q", m=2, h=4)
        psX = psf[:, 2048:4096].rearrange("p (g s) -> p g s", g=8)
        psXT = psf[:, 0:2048].rearrange("p (m h q) -> p m h q", m=2, h=4)
        psXO = psf[:, 2048:3072].rearrange("p (h q) -> p h q", h=4)
        XS = float(P) ** -0.5

        PTe = sc[:, 2048:2304].rearrange("p (t s) -> p t s", t=TT)
        Pe = sc[:, 2304:2560]
        y_sb = sc[:, 2560:3584]
        hTg = sc[:, 4096:5120].rearrange("p (k s) -> p k s", k=KC)
        psG = psf[:, 1024:2048].rearrange("p (k s) -> p k s", k=KC)
        rt = headsT[:, 8, 0:192]
        logits = rt[:, 0:16].rearrange("p (t e) -> p t e", t=TT)
        top8 = rt[:, 16:32].rearrange("p (t e) -> p t e", t=TT)
        topi = rt[:, 32:48].rearrange("p (t e) -> p t e", t=TT)
        oh = rt[:, 48:80].rearrange("p (j t e) -> p j t e", j=2, t=TT)
        gate16 = rt[:, 80:112].rearrange("p (t r e) -> p t r e", t=TT, r=2)
        rank16 = rt[:, 112:144].rearrange("p (t r e) -> p t r e", t=TT, r=2)
        chosen = rt[:, 144:160].rearrange("p (t e) -> p t e", t=TT)
        g2 = rt[:, 160:168]
        now = rt[:, 168:172].rearrange("p (k t) -> p k t", k=2)
        n_f = rt[:, 172:176]

        def pe_mixers(pe, l):
            pe.wait_ge(sem("evac"), 2 * blk0["pa", l])
            for b, col in enumerate((COL["qa"], COL["qa"] + P, COL["ka"], COL["ka"] + P, COL["qi"], COL["qi"] + P)):
                for i in range(TT):
                    ins = pe.transpose(psf[:, b * S + i * P:b * S + (i + 1) * P], z[:, i, col:col + P], ident)
            ins.then_inc(sem("heads1_T"), 1)
            pe.wait_ge(sem("heads_n"), l + 1)
            pe.wait_ge(sem("ki_dup"), l + 1)
            for j, b in enumerate((QB, QB + 1, KB, KI, QC, QC + 1, QC + 2, QC + 3, KCC)):
                for i in range(TT):
                    ins = pe.transpose(psf[:, b * S + i * P:b * S + (i + 1) * P], heads_n[:, i, j * P:(j + 1) * P],
                                       ident)
            ins.then_inc(sem("heads2_T"), 1)
            pe.wait_ge(sem("heads1_sb"), l + 1)
            pe.wait_ge(sem("heads2_sb"), l + 1)
            pe.wait_ge(sem("heads3_sb"), l + 1)
            for i in range(2):
                for p in range(2):
                    r = slice(64 * p, 64 * p + 64)
                    q, k = headsT[r, QA + i, :], headsT[r, KA + i, :]
                    pe.matmul(ps[:, p, i * S:(i + 1) * S], k[:, 0:P], q, start=True, stop=True)
                    ins = pe.matmul(ps[:, 2 + p, i * P:(i + 1) * P], k[:, P:S], q[:, P:S], start=True, stop=True)
            ins.then_inc(sem("a_scores"), 1)
            for i in range(2):
                for p in range(2):
                    r = slice(64 * p, 64 * p + 64)
                    q, k = headsT[r, QI + i, :], headsT[r, KI, :]
                    pe.matmul(ps[:, 4 + p, i * S:(i + 1) * S], q[:, P:S], k, start=True, stop=True)
                    ins = pe.matmul(ps[:, 6 + p, i * P:(i + 1) * P], q[:, 0:P], k[:, 0:P], start=True, stop=True)
            ins.then_inc(sem("idx_scores"), 1)
            pe.wait_ge(sem("idx_relu"), l + 1)
            pe.wait_ge(sem("log_keep"), l + 1)
            for p in range(2):
                pe.matmul(ps[:, 4 + p, :], after_tri, T3[:, p * NB:(p + 1) * NB], start=True, stop=False)
                for i in range(2):
                    pe.matmul(ps[:, 4 + p, i * S + P:(i + 1) * S], ones,
                              T3[:, 1024 + (2 * p + i) * P:1024 + (2 * p + i + 1) * P], start=False, stop=i == 1)
            pe.matmul(ps[:, 6, :], after_tri, T3[:, 1024:1536], start=True, stop=True).then_inc(sem("later"), 1)
            pe.wait_ge(sem("a_att"), l + 1)
            for i in range(2):
                for p in range(2):
                    v0 = COL["va"] + (2 * i + p) * HD
                    o = ps[64 * p:64 * p + 64, 7, i * S:(i + 1) * S]
                    pe.matmul(o, z[:, 0, v0:v0 + HD], T1[:, p * NB + i * S:p * NB + (i + 1) * S],
                              start=True, stop=False)
                    ins = pe.matmul(o[:, P:S], z[:, 1, v0:v0 + HD],
                                    T1[:, 1024 + (2 * p + i) * P:1024 + (2 * p + i + 1) * P], start=False, stop=True)
            ins.then_inc(sem("a_out"), 1)
            for n, tt in enumerate((1, 0)):
                w, q = W[tt], slice(tt * P, (tt + 1) * P)
                for i in range(2):
                    for p in range(2):
                        r = slice(64 * p, 64 * p + 64)
                        pe.matmul(psS[:, 2 * p + i, 0:w], headsT[r, QB + i, q], headsT[r, KB, 0:w],
                                  start=True, stop=True)
                for i in range(4):
                    for g in range(2):
                        r = slice(64 * g, 64 * g + 64)
                        ins = pe.matmul(psS[:, 4 + 4 * g + i, 0:w], headsT[r, QC + i, q], headsT[r, KCC, 0:w],
                                        start=True, stop=True)
                ins.then_inc(sem("scores"), 1)
                pe.wait_ge(sem("probs"), 2 * l + n + 1)
                for s in range(w // P):
                    for h in range(H):
                        ins = pe.transpose(psPT[:, s, h, :], probs(tt)[:, h, s * P:(s + 1) * P], ident)
                    ins.then_inc(sem(f"probs_T{s}"), 1)
                pe.wait_ge(sem("pT0_sb"), 2 * l + n + 1)
                if tt == 1:
                    pe.wait_ge(sem("pT1_sb"), l + 1)
                pe.wait_ge(sem("oT_L"), 3 * l + n + 1)
                ns = w // P
                for p in range(2):
                    for s in range(ns):
                        pe.matmul(psO[64 * p:64 * p + 64, 0:2, :], z[:, s, COL["vb"]:COL["vb"] + HD],
                                  PT[:, s, 2 * p:2 * p + 2, :], start=s == 0, stop=s == ns - 1)
                for g in range(2):
                    for p in range(2):
                        v0 = COL["vc"] + g * HD
                        for s in range(ns):
                            ins = pe.matmul(psO[64 * p:64 * p + 64, 2 + 2 * g:4 + 2 * g, :], z[:, s, v0:v0 + HD],
                                            PT[:, s, 4 + 4 * g + p:4 + 4 * g + p + 3:2, :],
                                            start=s == 0, stop=s == ns - 1)
                ins.then_inc(sem("bc_out"), 1)

        def pe_cross(pe, l):
            pe.wait_ge(sem("x_heads_n"), l + 1)
            for j, src in enumerate((xq_h, xk_h)):
                for h in range(4):
                    for i in range(TT):
                        c = (4 * j + h) * S + i * P
                        ins = pe.transpose(psf[:, c:c + P], src[:, i, h * P:(h + 1) * P], ident)
            ins.then_inc(sem("x_heads_T"), 1)
            pe.wait_ge(sem("x_qT"), l + 1)
            pe.wait_ge(sem("x_kT"), l + 1)
            for i in range(TT):
                for h in range(4):
                    ins = pe.matmul(psX[:, 4 * i + h, :], headsT[:, h, i * P:(i + 1) * P], headsT[:, 4 + h, :],
                                    start=True, stop=True)
            ins.then_inc(sem("x_scores"), 1)
            pe.wait_ge(sem("x_probs"), l + 1)
            for m in range(2):
                for h in range(4):
                    for i in range(TT):
                        ins = pe.transpose(psXT[:, m, h, i * P:(i + 1) * P], xP[:, 4 * i + h, m * P:(m + 1) * P],
                                           ident)
                ins.then_inc(sem("x_probs_T"), 1)
            pe.wait_ge(sem("x_pT0"), l + 1)
            pe.wait_ge(sem("x_pT1"), l + 1)
            for h in range(4):
                for m in range(2):
                    ins = pe.matmul(psXO[:, h, :], xv_n[:, m, h * P:(h + 1) * P], xPT[:, m, h, :],
                                    start=m == 0, stop=m == 1)
                if h % 2:
                    ins.then_inc(sem("xo_T"), 1)

        def pe_program(pe):
            pe.wait_ge(sem("const_in"), 16)
            pe.wait_ge(sem("gain_in"), 96)
            pe.transpose(ps[:, 0, 0:64], gain_rows, ident[0:64, 0:64])
            pe.matmul(ps[0:H, 1, 0:3 * P], rel_rows, bucket_rows, start=True, stop=True) \
                .then_inc(sem("setup"), 1)
            for l in range(L):
                pe.wait_ge(sem("mix_xn"), l + 1)
                pe_turn(pe, "mix", xn)
                pe.wait_ge(sem("mix_L"), 2 * l + 2)
                pe_win(pe, l)
                pe.wait_ge(sem("mem_xn"), l + 1)
                pe_turn(pe, "mem", mem_n)
                pe.wait_ge(sem("mem_L"), 2 * l + 2)
                pe_linear(pe, "xkv", l)
                pe_mixers(pe, l)
                pe.wait_ge(sem("oT_L"), 3 * l + 3)
                pe_linear(pe, "pa", l)
                pe_linear(pe, "pb", l, k0=2)
                pe_linear(pe, "pc", l, k0=4)
                pe.wait_ge(sem("merged"), l + 1)
                pe_turn(pe, "mrg", xn)
                pe.wait_ge(sem("mrg_L"), 2 * l + 2)
                pe_linear(pe, "out", l)
                pe.wait_ge(sem("x_xn"), l + 1)
                pe_turn(pe, "x", xn)
                pe.wait_ge(sem("x_L"), 2 * l + 2)
                pe_linear(pe, "xq", l)
                pe_cross(pe, l)
                pe.wait_ge(sem("xo_L"), 2 * l + 2)
                pe_linear(pe, "xo", l)
                pe.wait_ge(sem("ffn_xn"), l + 1)
                pe_turn(pe, "ffn", xn)
                pe.wait_ge(sem("ffn_L"), 2 * l + 2)
                if l == 0:
                    pe_ffn(pe, FFN0[0], 0, 0, TT, N_DENSE)
            pe.wait_ge(sem("router_in"), 16)
            for i in range(TT):
                for k in range(KC):
                    ins = pe.matmul(ps[:, 4, 8 * i:8 * i + 8], hTf[:, k, i * P:(i + 1) * P], w_router[:, k, :],
                                    start=k == 0, stop=k == KC - 1)
            ins.then_inc(sem("logits"), 1)
            pe.wait_ge(sem("chosen"), 1)
            pe.matmul(ps[:, 5, 0:8], before_tri, chosen[:, 0, :], start=True, stop=True)
            pe.matmul(ps[:, 5, 8:16], ones, chosen[:, 0, :], start=True, stop=False)
            pe.matmul(ps[:, 5, 8:16], before_tri, chosen[:, 1, :], start=False, stop=True)
            pe.matmul(ps[:, 5, 16:24], ones, chosen[:, 0, :], start=True, stop=False)
            pe.matmul(ps[:, 5, 16:24], ones, chosen[:, 1, :], start=False, stop=True).then_inc(sem("ranks"), 1)
            pe.wait_ge(sem("routed"), 1)
            n_it = pe.value_load(n_iter[0:1, 0:1], min_val=N_EXP, max_val=2 * N_EXP)
            with pe.Fori(0, n_it) as it:
                pe.wait_ge(sem("one_hot"), it + 1)
                for i in range(TT):
                    pe.transpose(ps[:, 7, i * P:(i + 1) * P], PTe[:, i, :], ident)
                for k in range(KC):
                    for i in range(TT):
                        ins = pe.matmul(psG[:, k, :], xn[:, i, k * P:(k + 1) * P], PTe[:, i, :],
                                        start=i == 0, stop=i == 1)
                ins.then_inc(sem("gathered"), 1)
                pe.wait_ge(sem("hg_L"), it + 1)
                pe_ffn(pe, FFN0[1], it * (3 * N_MOE), it * N_MOE + N_DENSE, 1, N_MOE)
                pe.wait_ge(sem("y_sb"), it + 1)
                for i in range(TT):
                    for h in range(2):
                        ins = pe.matmul(ps[:, 2 + 2 * i + h, :], Pe[:, i * P:(i + 1) * P], y_sb[:, h * NB:(h + 1) * NB],
                                        start=True, stop=True)
                ins.then_inc(sem("scattered"), 1)

        def act_norm(act, name, l, rows, src, dst, col):
            for i in range(TT):
                ins = act.activation(dst[:, i, :], src[:, i, :], ACT.Copy, scale=rstd[:, col + i:col + i + 1])
            ins.then_inc(sem(name + "_xn"), 1)

        def end_of(name, l):
            s, nblk, per = slots_of(name, l)
            return s + nblk * per

        def act_mixers(act, l):
            act.wait_ge(sem("z_done"), l + 1)
            act.activation(gates, gates, ACT.Sigmoid).then_inc(sem("gates"), 1)
            ki = z[:, :, COL["ki"]:COL["ki"] + HD].unsqueeze(2)
            act.wait_ge(sem("var"), len(RS) * l + RS["heads"] + 1)
            for i in range(TT):
                ins = act.activation(heads_n[:, i, 3 * P:4 * P].rearrange("p (r d) -> p r d", r=2),
                                     bc(ki[:, i], [P, 2, HD]), ACT.Copy)
            ins.then_inc(sem("ki_dup"), 1)
            act_rsqrt(act, "heads", l)
            if l == 0:
                act.wait_ge(sem("bias_in"), 16 * (H + 1))
            act.wait_ge(sem("heads1_T"), l + 1)
            act.activation(headsT[:, 0:6, :].rearrange("p b s -> p (b s)"), psf[:, 0:6 * S], ACT.Copy) \
                .then_inc(sem("heads1_sb"), 1)
            act.wait_ge(sem("heads2_T"), l + 1)
            act.activation(headsT[:, 6:10, :].rearrange("p b s -> p (b s)"), psf[:, 6 * S:10 * S], ACT.Copy) \
                .then_inc(sem("heads2_sb"), 1)
            act.wait_ge(sem("a_scores"), l + 1)
            t1 = za_parts(T1)
            act.activation(t1[0], ps_za[0], ACT.Abs, scale=0.125)
            act.activation(part2(t1[1]), ps_za[1], ACT.Abs, scale=0.125).then_inc(sem("a_abs"), 1)
            act.drain()
            act.activation(T1, T1, ACT.Exp, scale=-1.0)
            act.drain()
            act.activation(T1, T1, ACT.Ln, bias=1.0).then_inc(sem("softplus"), 1)
            act.wait_ge(sem("idx_scores"), l + 1)
            act.activation(IDX[1].rearrange("p h s -> p (h s)"), psf[:, 4 * NB:6 * NB], ACT.Relu, scale=0.125)
            act.activation(part2(IDX[0].rearrange("p h s -> p (h s)")), ps[:, 6:8, 0:256], ACT.Relu, scale=0.125) \
                .then_inc(sem("idx_relu"), 1)
            act.wait_ge(sem("a_logs"), l + 1)
            act.activation(T1, T2, ACT.Exp).then_inc(sem("a_exp"), 1)
            act.wait_ge(sem("a_out"), l + 1)
            act.wait_ge(sem("mm_done"), end_of("xkv", l))
            act.activation(hT_hi[:, 0:2, :], ps[:, 7, :].rearrange("p (c s) -> p c s", c=2), ACT.Copy) \
                .then_inc(sem("oT_H"), 1)
            for n, tt in enumerate((1, 0)):
                pr = probs(tt)
                act.wait_ge(sem("row_max"), 2 * l + n + 1)
                for h in range(H):
                    act.activation(pr[:, h, :], pr[:, h, :], ACT.Exp, bias=negm[:, h:h + 1],
                                   accum_out=rsum[:, h:h + 1])
                act.activation(s8[:, 0:8], s8[:, 0:8], ACT.Exp).then_inc(sem("exps"), 1)
                act.wait_ge(sem("probs_T0"), 2 * l + n + 1)
                act.activation(PT[:, 0, :, :], psPT[:, 0, :, :], ACT.Copy).then_inc(sem("pT0_sb"), 1)
                act.wait_ge(sem("bc_out"), 2 * l + n + 1)
                act.activation(hT_hi[:, 2:8, tt * P:(tt + 1) * P], psO, ACT.Copy).then_inc(sem("oT_H"), 1)

        def act_cross(act, l):
            act_rsqrt(act, "xqk", l)
            act.wait_ge(sem("x_heads_T"), l + 1)
            act.activation(headsT[:, 0:4, :].rearrange("p b s -> p (b s)"), psf[:, 0:4 * S], ACT.Copy) \
                .then_inc(sem("x_qT"), 1)
            act.wait_ge(sem("x_max"), l + 1)
            for g in range(8):
                ins = act.activation(xP[:, g, :], psX[:, g, :], ACT.Exp, bias=negm[:, g:g + 1], scale=XS,
                                     accum_out=rsum[:, g:g + 1])
            ins.then_inc(sem("x_exps"), 1)
            act.wait_ge(sem("x_probs_T"), 2 * l + 1)
            act.activation(xPT[:, 0, :, :], psXT[:, 0, :, :], ACT.Copy).then_inc(sem("x_pT0"), 1)
            act_hi(act, "xo", l, psXO, "xo_T", 4, end_of("xq", l))

        def act_program(act):
            cnt = Count()
            act.dma_start(x_sb[:, :, :], t["x"][0].rearrange("(t p) d -> p t d", p=P)).then_inc(sem("x_in"), 16)
            act.wait_ge(sem("setup"), 1)
            act.activation(gains[:, :], ps[:, 0, 0:64], ACT.Copy).then_inc(sem("gains"), 1)
            act.activation(dist_rows, ps[0:H, 1, 0:3 * P], ACT.Copy).then_inc(sem("dist_sb"), 1)
            for l in range(L):
                lim = FFN0[l]
                act_rsqrt(act, "mix", l)
                act.wait_ge(sem("mix_rs"), l + 1)
                act_norm(act, "mix", l, None, x_sb, xn, 0)
                act_norm(act, "mem", l, None, mem_n, mem_n, 2)
                act_hi(act, "mix", l, hTf, "mix_F")
                act_win(act, l, cnt, end_of("in", l) + 2)
                act_hi(act, "mem", l, hTf, "mem_F", mm=end_of("in", l))
                act_split_to(act, cnt, end_of("xkv", l) + 2)
                act_mixers(act, l)
                act_split_to(act, cnt, end_of("pc", l) + 2)
                act_hi(act, "mrg", l, psT, "mrg_T", mm=end_of("pc", l))
                act_split_to(act, cnt, end_of("out", l) + 2)
                act_rsqrt(act, "x", l)
                act.wait_ge(sem("x_rs"), l + 1)
                act_norm(act, "x", l, None, x_sb, xn, 0)
                act_hi(act, "x", l, hTf, "x_F", mm=end_of("out", l))
                act_split_to(act, cnt, end_of("xq", l) + 2)
                act_cross(act, l)
                act_split_to(act, cnt, lim)
                act_rsqrt(act, "ffn", l)
                act.wait_ge(sem("ffn_rs"), l + 1)
                act_norm(act, "ffn", l, None, x_sb, xn, 0)
                act_hi(act, "ffn", l, hTf, "ffn_F", mm=end_of("xo", l))
                if l == 0:
                    act_ffn(act, FFN0[0], 0, 0, TT, N_DENSE)
                    cnt.n = FFN0[0] + 3 * N_DENSE
            act.wait_ge(sem("top_two"), 1)
            act.activation(g2[:, 0:2], g2[:, 0:2], ACT.Exp).then_inc(sem("gate_exp"), 1)
            act.wait_ge(sem("routed"), 1)
            n_it = act.value_load(n_iter[0:1, 0:1], min_val=N_EXP, max_val=2 * N_EXP)
            with act.Fori(0, n_it) as it:
                act.wait_ge(sem("gathered"), it + 1)
                act.activation(Pe, ps[:, 7, 0:2 * P], ACT.Copy)
                act.wait_ge(sem("hg_F"), it + 1)
                act.activation(hT_hi[:, :, 0:P], hTg, ACT.Copy).then_inc(sem("hg_H"), 1)
                act_ffn(act, FFN0[1], it * (3 * N_MOE), it * N_MOE + N_DENSE, 1, N_MOE)
                act.wait_ge(sem("mm_done"), it * (3 * N_MOE) + (FFN0[1] + 3 * N_MOE))
                act.activation(y_sb, psf[:, 0:1024], ACT.Copy).then_inc(sem("y_sb"), 1)

        def dve_topk(v, l, tt):
            acc = IDX[tt][:, 0, :]
            for j, h in enumerate((0, 2, 1, 3)):
                w = z[:, tt, COL["wi"] + j:COL["wi"] + j + 1]
                if j == 0:
                    v.tensor_scalar(acc, acc, w, None, ALU.mult)
                else:
                    v.scalar_tensor_tensor(acc, IDX[tt][:, h, :], w, acc, ALU.mult, ALU.add)
                v.drain()
            d = acc[:, tt * P:(tt + 1) * P]
            v.tensor_tensor(d, d, causal_add, ALU.add)
            v.drain()
            for _ in range(TOPK // 8):
                v.max(s8[:, 0:8], acc)
                v.drain()
                v.match_replace(acc, s8[:, 0:8], acc, TAKEN)
                v.drain()
            v.tensor_scalar(SEL[tt], acc, TAKEN / 1.5, -BIG, ALU.is_gt, ALU.mult)
            if tt == 0:
                v.drain()
                v.tensor_tensor(SEL[0], SEL[0], causal_add, ALU.add)

        def dve_mixers(v, l):
            if l == 0:
                v.wait_ge(sem("bias_in"), 16 * (H + 1))
                v.tensor_tensor(bias[:, 4:H, :], bias[:, 4:H, :], bc(window.unsqueeze(1), [P, 8, 2 * P]), ALU.add)
            v.drain()
            zb, zc = z[:, :, COL["qb"]:COL["vb"]], z[:, :, COL["qc"]:COL["vc"]]
            sqb, sqc = sc[:, 0:640], sc[:, 640:1920]
            v.tensor_tensor(sqb.rearrange("p (t d) -> p t d", t=TT), zb, zb, ALU.mult)
            v.tensor_tensor(sqc.rearrange("p (t d) -> p t d", t=TT), zc, zc, ALU.mult)
            v.drain()
            v.tensor_reduce(ss[:, 0:10], sqb.rearrange("p (h d) -> p h d", d=HD), AX.X, ALU.add)
            v.tensor_reduce(ss[:, 10:30], sqc.rearrange("p (h d) -> p h d", d=HD), AX.X, ALU.add)
            dve_rsqrt(v, "heads", l, HD)
            v.drain()
            v.wait_ge(sem("hgain_in"), 80 * (l + 1))
            v.wait_ge(sem("ki_dup"), l + 1)

            def head(i, col, r, g, dst):
                return v.scalar_tensor_tensor(heads_n[:, i, dst:dst + HD], z[:, i, col:col + HD], rstd[:, r:r + 1],
                                              hgain[:, g * HD:(g + 1) * HD], ALU.mult, ALU.mult)
            for i in range(TT):
                for h in range(4):
                    head(i, COL["qb"] + h * HD, 5 * i + h, 0, h * HD)
                for d in range(2):
                    head(i, COL["kb"], 5 * i + 4, 1, 2 * P + d * HD)
                for h in range(8):
                    head(i, COL["qc"] + h * HD, 10 + 10 * i + h, 2, 4 * P + (h % 4) * P + (h // 4) * HD)
                for g in range(2):
                    ins = head(i, COL["kc"] + g * HD, 10 + 10 * i + 8 + g, 3, 8 * P + g * HD)
            ins.then_inc(sem("heads_n"), 1)
            v.wait_ge(sem("heads2_T"), l + 1)
            v.tensor_copy(headsT[:, 10:15, :].rearrange("p b s -> p (b s)"), psf[:, 10 * S:15 * S]) \
                .then_inc(sem("heads3_sb"), 1)
            v.wait_ge(sem("a_abs"), l + 1)
            t2, t3 = za_parts(T2), za_parts(T3)
            v.tensor_scalar(t2[0], ps_za[0], 0.125, 0.0, ALU.mult, ALU.min)
            v.tensor_scalar(part2(t2[1]), ps_za[1], 0.125, 0.0, ALU.mult, ALU.min)
            v.wait_ge(sem("softplus"), l + 1)
            v.drain()
            v.tensor_tensor(T2, T2, T1, ALU.subtract)
            v.drain()
            v.scalar_tensor_tensor(t3[0], ps_za[0], -0.125, t2[0], ALU.mult, ALU.add)
            v.scalar_tensor_tensor(part2(t3[1]), ps_za[1], -0.125, part2(t2[1]), ALU.mult, ALU.add)
            v.drain()
            tri = bc(before_tri.unsqueeze(1), [P, 4, P])
            for d in diag(T3, 0):
                ins = v.tensor_tensor(d, d, tri, ALU.mult)
            ins.then_inc(sem("log_keep"), 1)
            v.wait_ge(sem("idx_relu"), l + 1)
            dve_topk(v, l, 1)
            v.wait_ge(sem("later"), l + 1)
            v.tensor_tensor(T2, psf[:, 4 * NB:7 * NB], T2, ALU.add).then_inc(sem("a_logs"), 1)
            dve_topk(v, l, 0)
            v.wait_ge(sem("a_exp"), l + 1)
            for d in diag(T1, 0):
                ins = v.tensor_tensor(d, d, tri, ALU.mult)
            ins.then_inc(sem("a_att"), 1)
            v.wait_ge(sem("oT_H"), 3 * l + 1)
            v.tensor_tensor(hT_lo[:, 0:2, :], ps[:, 7, :].rearrange("p (c s) -> p c s", c=2),
                            hT_hi[:, 0:2, :].bitcast(F32), ALU.subtract).then_inc(sem("oT_L"), 1)
            for n, tt in enumerate((1, 0)):
                pr, w = probs(tt), W[tt]
                v.wait_ge(sem("scores"), 2 * l + n + 1)
                v.scalar_tensor_tensor(pr, psS[:, :, 0:w], 0.125, bias[:, :, 2 * P - w:], ALU.mult, ALU.add)
                v.drain()
                v.tensor_tensor(pr[:, 0:4, :], pr[:, 0:4, :], bc(SEL[tt].unsqueeze(1), [P, 4, w]), ALU.add)
                v.drain()
                v.tensor_reduce(mx, pr, AX.X, ALU.max)
                v.drain()
                v.tensor_tensor(mx[:, 4:12], mx[:, 4:12], sink[:, :], ALU.max)
                v.drain()
                v.tensor_scalar(negm, mx, -1.0, None, ALU.mult)
                v.tensor_tensor(s8[:, 0:8], sink[:, :], mx[:, 4:12], ALU.subtract).then_inc(sem("row_max"), 1)
                v.wait_ge(sem("exps"), 2 * l + n + 1)
                v.tensor_tensor(rsum[:, 4:12], rsum[:, 4:12], s8[:, 0:8], ALU.add)
                v.drain()
                v.reciprocal(mx, rsum)
                v.drain()
                v.tensor_tensor(pr, pr, bc(mx.unsqueeze(2), [P, H, w]), ALU.mult).then_inc(sem("probs"), 1)
                if tt == 1:
                    v.wait_ge(sem("probs_T1"), l + 1)
                    v.tensor_copy(PT[:, 1, :, :], psPT[:, 1, :, :]).then_inc(sem("pT1_sb"), 1)
                v.wait_ge(sem("oT_H"), 3 * l + n + 2)
                q = slice(tt * P, (tt + 1) * P)
                v.tensor_tensor(hT_lo[:, 2:8, q], psO, hT_hi[:, 2:8, q].bitcast(F32), ALU.subtract) \
                    .then_inc(sem("oT_L"), 1)

        def dve_merge(v, cnt, l, lim):
            v.wait_ge(sem("gates"), l + 1)
            for j, name in enumerate(("pa", "pb", "pc")):
                s, nblk, per = slots_of(name, l)
                for b in range(nblk):
                    last = s + (b + 1) * per - 1
                    dve_split_to(v, cnt, min(last + RING, lim))
                    blk = blk0[name, l] + b
                    for i in range(TT):
                        if i == 0:
                            v.wait_ge(sem("tile0_done"), blk + 1)
                        else:
                            v.wait_ge(sem("mm_done"), last + 1)
                        g = gates[:, i, j * D + b * NB:j * D + (b + 1) * NB]
                        m = xn[:, i, b * NB:(b + 1) * NB]
                        prod = sc[:, 2048 + i * NB:2048 + (i + 1) * NB]
                        v.tensor_tensor(prod if j else m, ps[:, 4 + i, :], g, ALU.mult).then_inc(sem("evac"), 1)
                        v.drain()
                        if j:
                            ins = v.tensor_tensor(m, m, prod, ALU.add)
            ins.then_inc(sem("merged"), 1)

        def dve_cross(v, l):
            v.drain()
            sq_q, sq_k = sc[:, 5120:6144], sc[:, 0:1024]
            v.tensor_tensor(sq_q.rearrange("p (t d) -> p t d", t=TT), xq_n, xq_n, ALU.mult)
            v.tensor_tensor(sq_k.rearrange("p (t d) -> p t d", t=TT), xk_n, xk_n, ALU.mult)
            v.drain()
            v.tensor_reduce(ss[:, 0:8], sq_q.rearrange("p (h d) -> p h d", d=P), AX.X, ALU.add)
            v.tensor_reduce(ss[:, 8:16], sq_k.rearrange("p (h d) -> p h d", d=P), AX.X, ALU.add)
            dve_rsqrt(v, "xqk", l, P)
            v.drain()
            v.wait_ge(sem("xgain_in"), 32 * (l + 1))
            for j, (src, dst) in enumerate(((xq_n, xq_h), (xk_n, xk_h))):
                for i in range(TT):
                    for h in range(4):
                        r = 8 * j + 4 * i + h
                        ins = v.scalar_tensor_tensor(dst[:, i, h * P:(h + 1) * P], src[:, i, h * P:(h + 1) * P],
                                                     rstd[:, r:r + 1], hgain[:, j * P:(j + 1) * P],
                                                     ALU.mult, ALU.mult)
            ins.then_inc(sem("x_heads_n"), 1)
            v.wait_ge(sem("x_heads_T"), l + 1)
            v.tensor_copy(headsT[:, 4:8, :].rearrange("p b s -> p (b s)"), psf[:, 4 * S:8 * S]) \
                .then_inc(sem("x_kT"), 1)
            v.wait_ge(sem("x_scores"), l + 1)
            v.tensor_reduce(mx[:, 0:8], psX, AX.X, ALU.max)
            v.drain()
            v.tensor_scalar(negm[:, 0:8], mx[:, 0:8], -XS, None, ALU.mult).then_inc(sem("x_max"), 1)
            v.wait_ge(sem("x_exps"), l + 1)
            v.reciprocal(mx[:, 0:8], rsum[:, 0:8])
            v.drain()
            v.tensor_tensor(xP, xP, bc(mx[:, 0:8].unsqueeze(2), [P, 8, S]), ALU.mult).then_inc(sem("x_probs"), 1)
            v.wait_ge(sem("x_probs_T"), 2 * l + 2)
            v.tensor_copy(xPT[:, 1, :, :], psXT[:, 1, :, :]).then_inc(sem("x_pT1"), 1)
            dve_lo(v, "xo", l, psXO, 4)

        def dve_norm(v, name, l, srcs):
            v.drain()
            for j, src in enumerate(srcs):
                dve_sumsq(v, src, sc[:, 2048:3072], 2 * j)
            dve_rsqrt(v, name, l, D).then_inc(sem(name + "_rs"), 1)

        def dve_router(v):
            v.wait_ge(sem("logits"), 1)
            v.tensor_copy(logits, ps[:, 4, 0:16].rearrange("p (t e) -> p t e", t=TT))
            v.drain()
            for i in range(TT):
                v.max(top8[:, i, :], logits[:, i, :])
            v.drain()
            for i in range(TT):
                v.max_index(idx8[:, i, :], top8[:, i, :], logits[:, i, :])
            v.drain()
            v.tensor_copy(topi, idx8[:, :, :])
            v.drain()
            for j in range(2):
                for i in range(TT):
                    v.tensor_scalar(oh[:, j, i, :], iota[:, 0:8], topi[:, i, j:j + 1], None, ALU.is_equal)
            for i in range(TT):
                ins = v.tensor_tensor(g2[:, i:i + 1], top8[:, i, 1:2], top8[:, i, 0:1], ALU.subtract)
            ins.then_inc(sem("top_two"), 1)
            v.drain()
            v.tensor_tensor(chosen, oh[:, 0], oh[:, 1], ALU.add).then_inc(sem("chosen"), 1)
            v.wait_ge(sem("gate_exp"), 1)
            v.tensor_scalar(g2[:, 2:4], g2[:, 0:2], 1.0, None, ALU.add)
            v.drain()
            v.reciprocal(g2[:, 4:6], g2[:, 2:4])
            v.drain()
            v.tensor_tensor(g2[:, 6:8], g2[:, 4:6], g2[:, 0:2], ALU.mult)
            v.drain()
            for i in range(TT):
                for r in range(2):
                    v.tensor_scalar(gate16[:, i, r, :], oh[:, 0, i, :], g2[:, 4 + i:5 + i], None, ALU.mult)
            v.drain()
            for i in range(TT):
                for r in range(2):
                    v.scalar_tensor_tensor(gate16[:, i, r, :], oh[:, 1, i, :], g2[:, 6 + i:7 + i],
                                           gate16[:, i, r, :], ALU.mult, ALU.add)
            v.wait_ge(sem("ranks"), 1)
            v.tensor_scalar(chosen, chosen, -1e4, 1e4, ALU.mult, ALU.add)
            v.drain()
            v.tensor_tensor(rank16[:, :, 0, :], ps[:, 5, 0:16].rearrange("p (t e) -> p t e", t=TT), chosen, ALU.add)
            v.drain()
            v.tensor_scalar(rank16[:, :, 1, :], rank16[:, :, 0, :], -float(P), None, ALU.add)
            v.tensor_reduce(n_f[:, 0:1], ps[:, 5, 16:24], AX.X, ALU.max)
            v.drain()
            v.tensor_scalar(n_f[:, 1:2], n_f[:, 0:1], float(P), float(N_EXP), ALU.is_gt, ALU.mult)
            v.drain()
            v.tensor_scalar(n_f[:, 2:3], n_f[:, 1:2], float(N_EXP), None, ALU.add)
            v.drain()
            v.tensor_copy(n_iter[0:1, 0:1], n_f[0:1, 2:3]).then_inc(sem("routed"), 1)

        def dve_program(v):
            cnt = Count()
            v.wait_ge(sem("x_in"), 16)
            for l in range(L):
                lim = FFN0[l]
                v.wait_ge(sem("mem_in"), 16 * (l + 1))
                dve_norm(v, "mix", l, (x_sb, mem_n))
                if l == 0:
                    v.wait_ge(sem("gains"), 1)
                dve_gain(v, "mix", l)
                dve_lo(v, "mix", l, hTf)
                dve_win(v, l, cnt, end_of("in", l) + 2)
                v.drain().then_inc(sem("z_done"), 1)
                dve_gain(v, "mem", l)
                dve_lo(v, "mem", l, hTf)

                def take_kv(b, i):
                    return v.tensor_copy(mem_kv[:, b, i * NB:(i + 1) * NB], ps[:, 4 + i, :])
                dve_linear(v, cnt, "xkv", l, take_kv, lim)
                dve_mixers(v, l)
                dve_merge(v, cnt, l, lim)
                dve_lo(v, "mrg", l, psT)
                dve_linear(v, cnt, "out", l, add_to_x(v), lim)
                dve_norm(v, "x", l, (x_sb,))
                dve_gain(v, "x", l)
                dve_lo(v, "x", l, hTf)

                def take_q(b, i):
                    return v.tensor_copy(xq_n[:, i, :], ps[:, 4 + i, :])
                dve_linear(v, cnt, "xq", l, take_q, lim)
                dve_cross(v, l)
                dve_linear(v, cnt, "xo", l, add_to_x(v), lim)
                dve_norm(v, "ffn", l, (x_sb,))
                dve_gain(v, "ffn", l)
                dve_lo(v, "ffn", l, hTf)
                if l == 0:
                    dve_ffn(v, FFN0[0], 0, 0, TT, N_DENSE)
                    cnt.n = FFN0[0] + 3 * N_DENSE
                    v.wait_ge(sem("mm_done"), FFN0[0] + 3 * N_DENSE)
                    v.tensor_tensor(x_sb[:, :, :].rearrange("p t d -> p (t d)"), psf[:, 0:2048],
                                    x_sb[:, :, :].rearrange("p t d -> p (t d)"), ALU.add) \
                        .then_inc(sem("ffn_added"), 1)
            dve_router(v)
            v.drain()
            n_it = v.value_load(n_iter[0:1, 0:1], min_val=N_EXP, max_val=2 * N_EXP)
            g0 = GAIN["ffn"] * L * KC + (L - 1) * KC
            with v.Fori(0, n_it) as it:
                v.drain()
                for k, src in enumerate((rank16, gate16)):
                    v.tensor_copy(now[:, k, :].unsqueeze(2),
                                  src.rearrange("p t r e -> p t (r e)")[:, :, bass.ds(it, 1)])
                v.drain()
                for i in range(TT):
                    ins = v.tensor_scalar(PTe[:, i, :], iota, now[:, 0, i:i + 1], None, ALU.is_equal)
                ins.then_inc(sem("one_hot"), 1)
                v.wait_ge(sem("gathered"), it + 1)
                v.tensor_tensor(hTg, psG, bc(gains[:, g0:g0 + KC].unsqueeze(2), [P, KC, P]), ALU.mult) \
                    .then_inc(sem("hg_F"), 1)
                v.wait_ge(sem("hg_H"), it + 1)
                v.tensor_tensor(hT_lo[:, :, 0:P], hTg, hT_hi[:, :, 0:P].bitcast(F32), ALU.subtract) \
                    .then_inc(sem("hg_L"), 1)
                dve_ffn(v, FFN0[1], it * (3 * N_MOE), it * N_MOE + N_DENSE, 1, N_MOE)
                v.wait_ge(sem("scattered"), it + 1)
                for i in range(TT):
                    v.scalar_tensor_tensor(x_sb[:, i, :], psf[:, (2 + 2 * i) * NB:(4 + 2 * i) * NB],
                                           now[:, 1, i:i + 1], x_sb[:, i, :], ALU.mult, ALU.add)
            v.drain().then_inc(sem("x_final"), 1)

        block = ctx.enter_context(nc.Block())

        @block.sync
        def _(sp):
            sp_program(sp)

        @block.gpsimd
        def _(pool):
            pool_program(pool)

        @block.scalar
        def _(act):
            act_program(act)

        @block.vector
        def _(v):
            dve_program(v)

        @block.tensor
        def _(pe):
            pe_program(pe)


_INS = ["x", "mem", "rel_bias", "norm_mix", "w_in", "b_gate", "qn_dsa", "kn_dsa", "qn_swa", "kn_swa", "sinks",
        "w_pa", "w_pb", "w_pc", "w_out", "norm_x", "norm_mem", "w_xq", "w_xkv", "w_xo", "qn_x", "kn_x",
        "norm_ffn", "w_gu_dense", "w_down_dense", "w_router", "w_gu_moe", "w_down_moe"]


def shape_constants():
    import numpy as np
    a, b = np.arange(P)[:, None], np.arange(P)[None, :]
    tiles = np.stack([a == b, a > b, a >= 0 * b, a < b, b + 0 * a, np.where(b <= a, 0.0, -BIG)]).astype(np.float32)
    tiles[2] = 1.0
    rel = np.arange(P)[:, None] + P - np.arange(2 * P)[None, :]
    window = np.where((rel >= 0) & (rel < P), 0.0, -BIG).astype(np.float32)
    n = np.maximum(255 - np.arange(3 * P), 0)
    nf = np.maximum(n, 1).astype(np.float32)
    large = 16 + (np.log(nf / np.float32(16)) / np.float32(math.log(8)) * np.float32(16)).astype(np.int32)
    bucket = np.where(n < 16, n, np.minimum(large, 31))
    return tiles, window, (np.arange(32)[:, None] == bucket[None, :]).astype(np.float32)


def kernel(**inputs):
    import numpy as np
    import concourse.bacc as bacc
    from concourse.bass_utils import run_bass_kernel_spmd

    nc = bacc.Bacc("TRN2", target_bir_lowering=False, num_devices=1)
    arrays, t = {}, {}
    for name in _INS:
        arrays[f"in_{name}"] = np.ascontiguousarray(inputs[name])
    arrays["in_c_tiles"], arrays["in_c_window"], arrays["in_c_bucket"] = shape_constants()
    for name, a in arrays.items():
        t[name[3:]] = nc.dram_tensor(name, a.shape, mybir.dt.from_np(a.dtype), kind="ExternalInput").ap()
    shape = inputs["x"].shape
    out = nc.dram_tensor("out_x", shape, F32, kind="ExternalOutput").ap()
    build(nc, t, out)
    r = run_bass_kernel_spmd(nc, [arrays], core_ids=[0])
    return r.results[0]["out_x"]
```

```python
import math
from contextlib import ExitStack

import concourse.bass as bass
from concourse import mybir

F32 = mybir.dt.float32
F32R = mybir.dt.float32r
I32 = mybir.dt.int32
U32 = mybir.dt.uint32
ALU = mybir.AluOpType
ACT = mybir.ActivationFunctionType
AX = mybir.AxisListType

P = 128
EPS = 1e-6
BIG = 1e30
TAKEN = -3e38
HD = 64
TOPK = 64
SLOT = 2048
RING = 3
FC = 256
NB = 512
COL = dict(qa=0, ka=256, va=512, qb=768, kb=1024, vb=1088, qi=1152, ki=1408, wi=1472, qc=1476, kc=1988,
           vc=2116, g=2244)


def build(nc, t, out):
    L, D, N_IN = t["w_in"].shape
    S = t["x"].shape[1]
    TT = S // P
    KC = D // P
    F_DENSE = t["w_down_dense"].shape[1]
    N_EXP, F_MOE = t["w_down_moe"].shape[1:3]
    H = 12
    N_DENSE, N_MOE = F_DENSE // FC, F_MOE // FC
    assert (S, D, TT, KC) == (256, 1024, 2, 8)

    plan = []

    def add_block(w, row0, kcs, c0, n):
        v = w[row0:row0 + P * kcs, c0:c0 + n].rearrange("(k p) n -> p k n", p=P)
        plan.append((v, kcs, n))

    blocks = {}

    def add_linear(name, l, w, k, n):
        blocks[name, l] = len(plan)
        for c0 in range(0, n, NB):
            for r0 in range(0, k, 4 * P):
                add_block(w, r0, min(4, (k - r0) // P), c0, min(NB, n - c0))

    FFN0 = {}
    for l in range(L):
        add_linear("in", l, t["w_in"][l], D, N_IN)
        add_linear("xkv", l, t["w_xkv"][l], D, 1024)
        add_linear("pa", l, t["w_pa"][l], 256, D)
        add_linear("pb", l, t["w_pb"][l], 256, D)
        add_linear("pc", l, t["w_pc"][l], 512, D)
        add_linear("out", l, t["w_out"][l], D, D)
        add_linear("xq", l, t["w_xq"][l], D, 512)
        add_linear("xo", l, t["w_xo"][l], 512, D)
        FFN0[l] = len(plan)
        if l == 0:
            plan.extend([(None, 4, NB)] * (3 * (F_DENSE // FC)))
    n_in_blocks = -(-N_IN // NB)
    order = [("in", n_in_blocks), ("xkv", 2), ("pa", 2), ("pb", 2), ("pc", 2), ("out", 2), ("xq", 1), ("xo", 2)]
    per_layer = sum(n for _, n in order)
    blk0 = {}
    for l in range(L):
        at = l * per_layer
        for name, n in order:
            blk0[name, l] = at
            at += n

    ctx = ExitStack()
    with ctx:
        def sb(name, shape, dt=F32):
            return ctx.enter_context(nc.sbuf_tensor(name, shape, dt))

        sems = {}

        def sem(name):
            if name not in sems:
                sems[name] = ctx.enter_context(nc.semaphore(name))
            return sems[name]

        raw = sb("raw", [P, RING, SLOT])
        w_hi = sb("w_hi", [P, RING, SLOT], F32R)
        w_lo = sb("w_lo", [P, RING, SLOT], F32R)
        x_sb = sb("x_sb", [P, TT, D])
        z = sb("z", [P, TT, N_IN])
        scratch = sb("scratch", [P, 6144])
        hT_hi = sb("hT_hi", [P, KC, S], F32R)
        hT_lo = sb("hT_lo", [P, KC, S], F32R)
        headsT = sb("headsT", [P, 15, S])
        mem_kv = sb("mem_kv", [P, 2, 1024])
        bias = sb("bias", [P, H, 2 * P])
        aT_hi = sb("aT_hi", [P, 2, S], F32R)
        aT_lo = sb("aT_lo", [P, 2, S], F32R)
        consts = sb("consts", [P, 6, P])
        gains = sb("gains", [P, 64])
        hgain = sb("hgain", [P, 256])
        sel_add = sb("sel_add", [P, 3 * P])
        sink = sb("sink", [P, 8])
        w_router = sb("w_router", [P, KC, N_EXP])
        st = sb("st", [P, 176])
        n_iter = sb("n_iter", [1, 2], I32)
        idx8 = sb("idx8", [P, TT, 8], U32)
        ident, after_tri, ones, before_tri, iota, causal_add = (consts[:, i, :] for i in range(6))

        ps = ctx.enter_context(nc.psum_tensor("ps", [P, 8, NB], F32))
        psf = ps[:, :, :].rearrange("p b n -> p (b n)")
        scratch_dram = nc.dram_tensor("bias_by_distance", (H, P, 3 * P), F32, kind="Internal").ap()

        sc = scratch[:, :]
        xn = sc[:, 0:2048].rearrange("p (t d) -> p t d", t=TT)
        hTf = sc[:, 2048:4096].rearrange("p (k s) -> p k s", k=KC)
        mem_n = sc[:, 4096:6144].rearrange("p (t d) -> p t d", t=TT)
        heads_n = sc[:, 1920:4224].rearrange("p (t d) -> p t d", t=TT)
        gates = z[:, :, COL["g"]:]
        ss, var, rstd, tmp = st[:, 0:32], st[:, 32:64], st[:, 64:96], st[:, 96:128]
        mx, negm, rsum = st[:, 128:140], st[:, 140:152], st[:, 152:164]
        s8 = st[:, 164:176]

        def bc(ap, shape):
            return ap.to_broadcast(shape)

        def raw_val(s):
            return 32 * (s // RING + 1)

        def load_slot(sp, s):
            src, kcs, n = plan[s]
            dst = raw[:, s % RING, 0:kcs * n].rearrange("p (k n) -> p k n", k=kcs)
            h = kcs // 2
            sp.dma_start(dst[:, 0:h, :], src[:, 0:h, :]).then_inc(sem(f"raw_full{s % RING}"), 16)
            sp.dma_start(dst[:, h:, :], src[:, h:, :]).then_inc(sem(f"raw_full{s % RING}"), 16)

        def load_gu(sp, buf, full, w, c, half, F):
            dst = buf.rearrange("p (k n) -> p k n", k=4)
            rows = w[half * 4 * P:(half + 1) * 4 * P]
            for i in range(2):
                src = rows[:, bass.ds(c * FC + i * F, FC)].rearrange("(k p) n -> p k n", p=P)
                sp.dma_start(dst[:, :, i * FC:(i + 1) * FC], src).then_inc(sem(full), 16)

        def load_down(sp, buf, full, w, row):
            dst = buf.rearrange("p (k n) -> p k n", k=2)
            for k in range(2):
                sp.dma_start(dst[:, k, :], w[bass.ds(row + k * P, P), :]).then_inc(sem(full), 16)

        def sp_dense(sp, s0, w_gu, w_down, F, n):
            def place(s, c=0):
                sp.wait_ge(sem("lo_done"), c * 3 + (s - RING + 1))
                return raw[:, s % RING, :], f"raw_full{s % RING}"
            for half in range(2):
                load_gu(sp, *place(s0 + half), w_gu, 0, half, F)
            with sp.Fori(1, n) as c:
                for half in range(2):
                    load_gu(sp, *place(s0 - 1 + half, c), w_gu, c, half, F)
                load_down(sp, *place(s0 + 1, c), w_down, c * FC - FC)
            load_down(sp, *place(s0 + 3 * n - 1), w_down, (n - 1) * FC)

        MOE, MOE0 = 3 * N_MOE, FFN0[L - 1]
        z_flat = z[:, :, :].rearrange("p t n -> p (t n)")

        def moe_raw(p):
            return z_flat[:, p * SLOT:(p + 1) * SLOT] if p < RING else raw[:, (MOE0 + p) % RING, :]

        def moe_ring(k):
            return (MOE0 + k) % RING

        def sp_moe(sp, wg, wd):
            def chunks(it, u, first=False):
                w_e = wg[bass.ds((it % N_EXP) * D, D), :]
                for d in range(2):
                    for k in range(3):
                        p = 3 * d + k
                        if not first:
                            sp.wait_ge(sem("lo_done"), it * MOE + (u * 6 + (MOE0 + p - 5)))
                        elif p >= RING:
                            sp.wait_ge(sem("lo_done"), MOE0 + p - 5)
                        if k < 2:
                            load_gu(sp, moe_raw(p), f"moe_full{p}", w_e, u * 2 + d, k, F_MOE)
                        else:
                            row = it * F_MOE + (u * (2 * FC) + (d * FC + N_EXP * F_MOE - FC))
                            load_down(sp, moe_raw(p), f"moe_full{p}", wd, row % (N_EXP * F_MOE))
            sp.wait_ge(sem("merged"), L)
            chunks(0, 0, first=True)
            with sp.Fori(1, N_MOE // 2) as u:
                chunks(0, u)
            sp.wait_ge(sem("routed"), 1)
            n_it = sp.value_load(n_iter[0:1, 0:1], min_val=N_EXP, max_val=2 * N_EXP)
            with sp.Fori(1, n_it) as it:
                with sp.Fori(0, N_MOE // 2) as u:
                    chunks(it, u)
            sp.wait_ge(sem("lo_done"), n_it * MOE + (MOE0 - 5))
            load_down(sp, moe_raw(0), "moe_full0", wd, N_EXP * F_MOE - FC)

        def sp_program(sp):
            for l in range(L):
                for s in range(blocks["in", l], FFN0[l]):
                    if s >= RING:
                        sp.wait_ge(sem("lo_done"), s - RING + 1)
                    load_slot(sp, s)
                if l == 0:
                    sp_dense(sp, FFN0[0], t["w_gu_dense"][0], t["w_down_dense"][0], F_DENSE, N_DENSE)
            sp_moe(sp, t["w_gu_moe"][0].rearrange("e d f -> (e d) f"),
                   t["w_down_moe"][0].rearrange("e f d -> (e f) d"))
            sp.wait_ge(sem("x_final"), 1)
            sp.dma_start(out[0].rearrange("(t p) d -> p t d", p=P), x_sb[:, :, :]).then_inc(sem("stored"), 16)
            sp.wait_ge(sem("stored"), 16)

        set_up = headsT[:, 0:4, :].rearrange("p b s -> p (b s)")
        gain_rows, rel_rows = set_up[0:64, 0:P], set_up[0:32, P:P + H]
        bucket_rows, dist_rows = set_up[0:32, 2 * P:5 * P], set_up[0:H, 5 * P:8 * P]
        window = sel_add[:, 0:2 * P]

        def preset_z(pool, l):
            pool.memset(z[:, :, 0:COL["g"]], 0.0).then_inc(sem("z_zero"), 1)
            bg = t["b_gate"][l:l + 1].rearrange("a b d -> a (b d)")
            for i in range(TT):
                pool.dma_start(z[:, i, COL["g"]:], bg.to_broadcast([P, N_IN - COL["g"]])).then_inc(sem("z_bias"), 16)

        def load_memory(pool):
            pool.dma_start(mem_n, t["mem"][0].rearrange("(t p) d -> p t d", p=P)).then_inc(sem("mem_in"), 16)

        def load_head_gains(pool, l):
            pool.dma_start(sink[:, :], t["sinks"][l:l + 1].to_broadcast([P, 8])).then_inc(sem("hgain_in"), 16)
            for i, name in enumerate(("qn_dsa", "kn_dsa", "qn_swa", "kn_swa")):
                pool.dma_start(hgain[:, HD * i:HD * (i + 1)], t[name][l:l + 1].to_broadcast([P, HD])) \
                    .then_inc(sem("hgain_in"), 16)

        def load_cross_gains(pool, l):
            pool.wait_ge(sem("heads_n"), l + 1)
            for i, name in enumerate(("qn_x", "kn_x")):
                pool.dma_start(hgain[:, P * i:P * i + P], t[name][l:l + 1].to_broadcast([P, P])) \
                    .then_inc(sem("xgain_in"), 16)

        def pool_program(pool):
            load_memory(pool)
            pool.dma_start(consts[:, :, :], t["c_tiles"].rearrange("i p n -> p i n")).then_inc(sem("const_in"), 16)
            for i, name in enumerate(("norm_mix", "norm_mem", "norm_x", "norm_ffn")):
                pool.dma_start(gain_rows[16 * i:16 * i + 16, :], t[name].rearrange("l (c p) -> (l c) p", p=P)) \
                    .then_inc(sem("gain_in"), 16)
            pool.dma_start(rel_rows, t["rel_bias"]).then_inc(sem("gain_in"), 16)
            pool.dma_start(bucket_rows, t["c_bucket"]).then_inc(sem("gain_in"), 16)
            preset_z(pool, 0)
            load_head_gains(pool, 0)
            pool.wait_ge(sem("dist_sb"), 1)
            pool.dma_start(scratch_dram, dist_rows.unsqueeze(1).to_broadcast([H, P, 3 * P])) \
                .then_inc(sem("dist_out"), 16)
            pool.dma_start(window, t["c_window"]).then_inc(sem("bias_in"), 16)
            pool.dma_start(w_router[:, :, :], t["w_router"][0].rearrange("(k p) e -> p k e", p=P)) \
                .then_inc(sem("router_in"), 16)
            pool.wait_ge(sem("dist_out"), 16)
            for i, h in enumerate([0, 2, 1, 3] + list(range(4, H))):
                src = bass.AP(scratch_dram.tensor, h * 3 * P * P + P - 1, [[3 * P - 1, P], [1, 2 * P]])
                pool.dma_start(bias[:, i, :], src).then_inc(sem("bias_in"), 16)
            load_cross_gains(pool, 0)
            for l in range(1, L):
                pool.wait_ge(sem("merged"), l)
                preset_z(pool, l)
                pool.wait_ge(sem("x_heads_n"), l)
                load_head_gains(pool, l)
                pool.wait_ge(sem("ffn_added"), l)
                load_memory(pool)
                load_cross_gains(pool, l)

        class Count:
            def __init__(self):
                self.n = 0

        def act_split(act, ring, width, raw_v, free_v):
            act.wait_ge(sem(f"raw_full{ring}"), raw_v)
            if free_v is not None:
                act.wait_ge(sem("mm_done"), free_v)
            act.activation(w_hi[:, ring, 0:width], raw[:, ring, 0:width], ACT.Copy).then_inc(sem("hi_done"), 1)

        def dve_split(v, ring, width, hi_v):
            v.wait_ge(sem("hi_done"), hi_v)
            v.tensor_tensor(w_lo[:, ring, 0:width], raw[:, ring, 0:width], w_hi[:, ring, 0:width].bitcast(F32),
                            ALU.subtract).then_inc(sem("lo_done"), 1)

        def act_split_to(act, cnt, end):
            while cnt.n < end:
                s = cnt.n
                _, kcs, n = plan[s]
                act_split(act, s % RING, kcs * n, raw_val(s), s - RING + 1 if s >= RING else None)
                cnt.n += 1

        def dve_split_to(v, cnt, end):
            while cnt.n < end:
                s = cnt.n
                _, kcs, n = plan[s]
                dve_split(v, s % RING, kcs * n, s + 1)
                cnt.n += 1

        def slots_of(name, l):
            nblk = dict(order)[name]
            k2 = 2 if name in ("in", "xkv", "out", "xq") else 1
            return blocks[name, l], nblk, k2

        def ahead(split_to, eng, cnt, last, limit):
            split_to(eng, cnt, min(last + RING, limit))

        RS = {"mix": 0, "heads": 1, "x": 2, "xqk": 3, "ffn": 4}
        RS_N = {"mix": 4, "heads": 30, "x": 2, "xqk": 16, "ffn": 2}

        def act_rsqrt(act, name, l):
            n, k = RS_N[name], len(RS) * l + RS[name]
            act.wait_ge(sem("var"), k + 1)
            act.activation(tmp[:, 0:n], var[:, 0:n], ACT.Ln)
            act.drain()
            act.activation(rstd[:, 0:n], tmp[:, 0:n], ACT.Exp, scale=-0.5).then_inc(sem("rs0"), 1)

        def dve_rsqrt(v, name, l, width):
            n, k = RS_N[name], len(RS) * l + RS[name]
            v.drain()
            v.tensor_scalar(var[:, 0:n], ss[:, 0:n], 1.0 / width, EPS, ALU.mult, ALU.add).then_inc(sem("var"), 1)
            v.wait_ge(sem("rs0"), k + 1)
            v.tensor_tensor(tmp[:, 0:n], rstd[:, 0:n], rstd[:, 0:n], ALU.mult)
            v.drain()
            v.tensor_tensor(tmp[:, 0:n], tmp[:, 0:n], var[:, 0:n], ALU.mult)
            v.drain()
            v.tensor_scalar(tmp[:, 0:n], tmp[:, 0:n], -0.5, 1.5, ALU.mult, ALU.add)
            v.drain()
            return v.tensor_tensor(rstd[:, 0:n], rstd[:, 0:n], tmp[:, 0:n], ALU.mult)

        def dve_sumsq(v, src, junk, col):
            for i in range(TT):
                v.tensor_tensor_reduce(junk, src[:, i, :], src[:, i, :], 1.0, 0.0, ALU.mult, ALU.add,
                                       ss[:, col + i:col + i + 1])
                v.drain()

        def pe_turn(pe, name, src, nchunk=KC):
            for half in range(2):
                ks = range(half * nchunk // 2, (half + 1) * nchunk // 2)
                for k in ks:
                    for i in range(TT):
                        ins = pe.transpose(psf[:, k * S + i * P:k * S + (i + 1) * P], src[:, i, k * P:(k + 1) * P],
                                           ident)
                ins.then_inc(sem(name + "_T"), 1)

        def halves(nchunk=KC):
            return [(i, slice(i * nchunk // 2, (i + 1) * nchunk // 2)) for i in range(2)]

        psT = psf[:, 0:KC * S].rearrange("p (k s) -> p k s", k=KC)
        GAIN = {"mix": 0, "mem": 1, "x": 2, "ffn": 3}

        def dve_gain(v, name, l):
            g0 = (GAIN[name] * L + l) * KC
            for i, ks in halves():
                v.wait_ge(sem(name + "_T"), 2 * l + i + 1)
                g = gains[:, g0 + ks.start:g0 + ks.stop].unsqueeze(2)
                v.tensor_tensor(hTf[:, ks, :], psT[:, ks, :], bc(g, [P, KC // 2, S]), ALU.mult) \
                    .then_inc(sem(name + "_F"), 1)

        def act_hi(act, name, l, src, ready, nchunk=KC, mm=None):
            if mm is not None:
                act.wait_ge(sem("mm_done"), mm)
            for i, ks in halves(nchunk):
                act.wait_ge(sem(ready), 2 * l + i + 1)
                act.activation(hT_hi[:, ks, :], src[:, ks, :], ACT.Copy).then_inc(sem(name + "_H"), 1)

        def dve_lo(v, name, l, src, nchunk=KC):
            for i, ks in halves(nchunk):
                v.wait_ge(sem(name + "_H"), 2 * l + i + 1)
                v.tensor_tensor(hT_lo[:, ks, :], src[:, ks, :], hT_hi[:, ks, :].bitcast(F32), ALU.subtract) \
                    .then_inc(sem(name + "_L"), 1)

        def pe_products(pe, acc, hk, wk, start, stop, hi=hT_hi, lo=hT_lo):
            for j, ((k, cols), (wh, wl)) in enumerate(zip(hk, wk)):
                a, b = hi[:, k, cols], lo[:, k, cols]
                last = j == len(hk) - 1
                pe.matmul(acc, a, wh, start=start and j == 0, stop=False)
                pe.matmul(acc, b, wh, start=False, stop=False)
                ins = pe.matmul(acc, a, wl, start=False, stop=stop and last)
            return ins

        def pe_block_slot(pe, ring, kcs, n, k0, lo_v, first, final, blk_v, tile_done=True):
            pe.wait_ge(sem("lo_done"), lo_v)
            wh = w_hi[:, ring, 0:kcs * n].rearrange("p (k n) -> p k n", k=kcs)
            wl = w_lo[:, ring, 0:kcs * n].rearrange("p (k n) -> p k n", k=kcs)
            for i in range(TT):
                if first and blk_v[i] is not None:
                    pe.wait_ge(sem("evac"), blk_v[i])
                cols = slice(i * P, (i + 1) * P)
                ins = pe_products(pe, ps[:, 4 + i, 0:n], [(k0 + k, cols) for k in range(kcs)],
                                  [(wh[:, k, :], wl[:, k, :]) for k in range(kcs)], first, final)
                if i == 0 and final:
                    ins.then_inc(sem("tile0_done"), 1)
            ins.then_inc(sem("mm_done"), 1)

        def pe_linear(pe, name, l, k0=0, b0=0, nblk=None):
            s, nb_all, per = slots_of(name, l)
            nblk = nblk or nb_all
            for b in range(b0, nblk):
                blk = blk0[name, l] + b
                for h in range(per):
                    ss_ = s + b * per + h
                    _, kcs, n = plan[ss_]
                    evs = [2 * blk - 1 + i if blk else None for i in range(TT)]
                    pe_block_slot(pe, ss_ % RING, kcs, n, k0 + 4 * h, ss_ + 1, h == 0, h == per - 1, evs)

        def dve_linear(v, cnt, name, l, take, limit, b0=0):
            s, nblk, per = slots_of(name, l)
            for b in range(b0, nblk):
                last = s + (b + 1) * per - 1
                ahead(dve_split_to, v, cnt, last, limit)
                blk = blk0[name, l] + b
                v.wait_ge(sem("tile0_done"), blk + 1)
                take(b, 0).then_inc(sem("evac"), 1)
                v.wait_ge(sem("mm_done"), last + 1)
                take(b, 1).then_inc(sem("evac"), 1)

        IN_LOOP = 3

        def pe_win(pe, l):
            s0, b00 = blocks["in", l], blk0["in", l]
            if l == 0:
                pe_linear(pe, "in", l, nblk=3)
            it0 = 1 if l == 0 else 0
            with pe.Fori(it0, IN_LOOP) as i:
                for j in range(6):
                    s = i * 6 + (s0 + j)
                    b = i * 3 + (b00 + j // 2)
                    evs = [b * 2 + (q - 1) for q in range(TT)]
                    pe_block_slot(pe, (s0 + j) % RING, 4, NB, 4 * (j % 2), s + 1, j % 2 == 0, j % 2 == 1, evs)
            pe_linear(pe, "in", l, b0=9)

        def act_win(act, l, cnt, limit):
            s0 = blocks["in", l]
            act_split_to(act, cnt, s0 + 3)
            with act.Fori(0, IN_LOOP) as i:
                for j in range(6):
                    s = i * 6 + (s0 + 3 + j)
                    base = s0 + 3 + j
                    act_split(act, base % RING, SLOT, i * 64 + raw_val(base), s - RING + 1)
            cnt.n = s0 + 21
            act_split_to(act, cnt, limit)

        def dve_win(v, l, cnt, limit):
            s0, b00 = blocks["in", l], blk0["in", l]
            dve_split_to(v, cnt, s0 + 2)
            v.wait_ge(sem("z_zero"), l + 1)
            v.wait_ge(sem("z_bias"), 32 * (l + 1))
            with v.Fori(0, IN_LOOP) as i:
                for j in range(3):
                    for h in range(2):
                        s = i * 6 + (s0 + 2 + 2 * j + h)
                        dve_split(v, (s0 + 2 + 2 * j + h) % RING, SLOT, s + 1)
                    b = i * 3 + j
                    dst = z[:, :, bass.ds(b * NB, NB)]
                    v.wait_ge(sem("tile0_done"), b + (b00 + 1))
                    v.tensor_tensor(dst[:, 0, :], ps[:, 4, :], dst[:, 0, :], ALU.add).then_inc(sem("evac"), 1)
                    v.wait_ge(sem("mm_done"), i * 6 + (s0 + 2 * j + 2))
                    v.tensor_tensor(dst[:, 1, :], ps[:, 5, :], dst[:, 1, :], ALU.add).then_inc(sem("evac"), 1)
            cnt.n = s0 + 20

            def take(b, i):
                n = min(NB, N_IN - b * NB)
                dst = z[:, i, b * NB:b * NB + n]
                return v.tensor_tensor(dst, ps[:, 4 + i, 0:n], dst, ALU.add)
            dve_linear(v, cnt, "in", l, take, limit, b0=9)

        a_sb = headsT[:, 0:2, :]
        silu_sb = headsT[:, 2:4, :]

        def psA(T):
            return ps[:, 6, 0:2 * T * P].rearrange("p (f s) -> p f s", f=2)

        def pe_dense(pe, s0, n):
            def gate_up(c, half):
                s, ring = c * 3 + (s0 - 1 + half), (s0 - 1 + half) % RING
                if isinstance(c, int) and c == 0:
                    s, ring = s0 + half, (s0 + half) % RING
                pe.wait_ge(sem("lo_done"), s + 1)
                wh = w_hi[:, ring, :].rearrange("p (k n) -> p k n", k=4)
                wl = w_lo[:, ring, :].rearrange("p (k n) -> p k n", k=4)
                for i in range(TT):
                    ins = pe_products(pe, ps[:, 4 + i, :], [(4 * half + k, slice(i * P, (i + 1) * P)) for k in range(4)],
                                      [(wh[:, k, :], wl[:, k, :]) for k in range(4)], half == 0, half == 1)
                ins.then_inc(sem("mm_done"), 1)

            def turn(c):
                pe.wait_ge(sem("act_done"), c + 1)
                for i in range(TT):
                    for f in range(2):
                        ins = pe.transpose(ps[:, 6, (f * TT + i) * P:(f * TT + i + 1) * P],
                                           a_sb[:, i, f * P:(f + 1) * P], ident)
                ins.then_inc(sem("aT_turned"), 1)

            def down(c, s, ring, first, last):
                pe.wait_ge(sem("lo_done"), s + 1)
                pe.wait_ge(sem("aT_split"), c + 1)
                wh = w_hi[:, ring, :].rearrange("p (k n) -> p k n", k=2)
                wl = w_lo[:, ring, :].rearrange("p (k n) -> p k n", k=2)
                for i in range(TT):
                    for h in range(2):
                        cols = slice(h * NB, (h + 1) * NB)
                        ins = pe_products(pe, ps[:, 2 * i + h, :], [(f, slice(i * P, (i + 1) * P)) for f in range(2)],
                                          [(wh[:, f, cols], wl[:, f, cols]) for f in range(2)], first, last,
                                          hi=aT_hi, lo=aT_lo)
                ins.then_inc(sem("mm_done"), 1)

            def chunk(c, first):
                pe.wait_ge(sem("act_done"), c)
                gate_up(c, 0)
                turn(c - 1)
                gate_up(c, 1)
                down(c - 1, c * 3 + (s0 + 1), (s0 + 1) % RING, first, False)

            gate_up(0, 0)
            gate_up(0, 1)
            chunk(1, True)
            with pe.Fori(2, n) as c:
                chunk(c, False)
            turn(n - 1)
            down(n - 1, s0 + 3 * n - 1, (s0 + 3 * n - 1) % RING, False, True)

        def split_order(split, act_of, aT_of, s0, n, fori):
            split(0, s0)
            split(0, s0 + 1)
            split(0, s0 + 2)
            act_of(0, s0 + 1)
            split(0, s0 + 3)
            with fori(1, n - 1) as c:
                split(c, s0 + 1)
                aT_of(c - 1)
                split(c, s0 + 2)
                act_of(c, s0)
                split(c, s0 + 3)
            split(n - 1, s0 + 1)
            aT_of(n - 2)
            act_of(n - 1, s0)
            split(n - 1, s0 + 2)
            aT_of(n - 1)

        def act_dense(act, s0, n):
            def split(c, base):
                act_split(act, base % RING, SLOT, c * 32 + raw_val(base),
                          c * 3 + (base - RING + 1))

            def silu(c, base):
                act.wait_ge(sem("mm_done"), c * 3 + (base + 1))
                act.activation(silu_sb[:, :, :], ps[:, 4:4 + TT, 0:FC], ACT.Silu).then_inc(sem("silu"), 1)

            def aT(c):
                act.wait_ge(sem("aT_turned"), c + 1)
                act.activation(aT_hi[:, :, :], psA(TT), ACT.Copy).then_inc(sem("aT_hi"), 1)
            split_order(split, silu, aT, s0, n, act.Fori)

        def dve_dense(v, s0, n):
            def split(c, base):
                dve_split(v, base % RING, SLOT, c * 3 + (base + 1))

            def gated(c, base):
                v.wait_ge(sem("silu"), c + 1)
                v.tensor_tensor(a_sb[:, :, :], ps[:, 4:4 + TT, FC:], silu_sb[:, :, :], ALU.mult) \
                    .then_inc(sem("act_done"), 1)

            def aT(c):
                v.wait_ge(sem("aT_hi"), c + 1)
                v.tensor_tensor(aT_lo[:, :, :], psA(TT), aT_hi[:, :, :].bitcast(F32), ALU.subtract) \
                    .then_inc(sem("aT_split"), 1)
            split_order(split, gated, aT, s0, n, v.Fori)

        def at(ip, par, per):
            return ip * (2 * per) + par * per

        def col_of(par):
            return slice(par * P, (par + 1) * P)

        def pe_turn_chunk(pe):
            for f in range(2):
                ins = pe.transpose(ps[:, 6, f * P:(f + 1) * P], a_sb[:, 0, f * P:(f + 1) * P], ident)
            ins.then_inc(sem("aT_turned"), 1)

        def pe_moe_down(pe, first, last):
            ring = moe_ring(2)
            wh = w_hi[:, ring, :].rearrange("p (k n) -> p k n", k=2)
            wl = w_lo[:, ring, :].rearrange("p (k n) -> p k n", k=2)
            for h in range(2):
                cols = slice(h * NB, (h + 1) * NB)
                ins = pe_products(pe, ps[:, h, :], [(f, slice(0, P)) for f in range(2)],
                                  [(wh[:, f, cols], wl[:, f, cols]) for f in range(2)], first, last,
                                  hi=aT_hi, lo=aT_lo)
            ins.then_inc(sem("mm_done"), 1)

        def pe_moe_chunk(pe, ip, par, c):
            off, coff = at(ip, par, MOE), at(ip, par, N_MOE)
            pe.wait_ge(sem("act_done"), coff + (c + N_DENSE + 1))
            for k in range(2):
                pe.wait_ge(sem("lo_done"), off + (c * 3 + (MOE0 + k + 1)))
                ring = moe_ring(k)
                wh = w_hi[:, ring, :].rearrange("p (k n) -> p k n", k=4)
                wl = w_lo[:, ring, :].rearrange("p (k n) -> p k n", k=4)
                pe_products(pe, ps[:, 4, :], [(4 * k + q, col_of(par)) for q in range(4)],
                            [(wh[:, q, :], wl[:, q, :]) for q in range(4)], k == 0, k == 1) \
                    .then_inc(sem("mm_done"), 1)
                if k == 0:
                    pe_turn_chunk(pe)
            pe.wait_ge(sem("lo_done"), off + (c * 3 + (MOE0 + 3)))
            pe.wait_ge(sem("aT_split"), coff + (c + N_DENSE + 1))
            static = isinstance(c, int)
            if static and c == 1:
                pe.wait_ge(sem("y_sb"), at(ip, par, 1) + 1)
            pe_moe_down(pe, static and c == 1, static and c == 0)

        def pe_gather(pe, n):
            pe.wait_ge(sem("one_hot"), n)
            for i in range(TT):
                pe.transpose(ps[:, 7, i * P:(i + 1) * P], PTe[:, i, :], ident)
            for k in range(KC):
                for i in range(TT):
                    ins = pe.matmul(psG[:, k, :], xn[:, i, k * P:(k + 1) * P], PTe[:, i, :], start=i == 0, stop=i == 1)
            ins.then_inc(sem("gathered"), 1)

        def pe_scatter(pe, n, par):
            pe.wait_ge(sem("y_sb"), n)
            for i in range(TT):
                for h in range(2):
                    ins = pe.matmul(ps[:, SCATTER[i][h], :], Pe[par][:, i * P:(i + 1) * P],
                                    y_sb[:, h * NB:(h + 1) * NB], start=True, stop=True)
            ins.then_inc(sem("scattered"), 1)

        def pe_moe(pe):
            pe.wait_ge(sem("routed"), 1)
            n_pair = pe.value_load(n_iter[0:1, 1:2], min_val=N_EXP // 2, max_val=N_EXP)
            for h in range(2):
                pe.matmul(ps[:, h, :], Pe[1][:, 0:P], consts[:, 0:4, :].rearrange("p i n -> p (i n)"),
                          start=True, stop=False)
            pe_gather(pe, 1)
            with pe.Fori(0, n_pair) as ip:
                for par in range(2):
                    n = at(ip, par, 1) + 1
                    pe.wait_ge(sem("hg_L"), n)
                    pe_moe_chunk(pe, ip, par, 0)
                    pe_moe_chunk(pe, ip, par, 1)
                    pe_scatter(pe, n, 1 - par)
                    pe_moe_chunk(pe, ip, par, 2)
                    pe.wait_ge(sem("x_added"), n)
                    pe_gather(pe, n + 1)
                    with pe.Fori(3, N_MOE) as c:
                        pe_moe_chunk(pe, ip, par, c)
            pe.wait_ge(sem("act_done"), n_pair * (2 * N_MOE) + (N_DENSE + 1))
            pe_turn_chunk(pe)
            pe.wait_ge(sem("lo_done"), n_pair * (2 * MOE) + (MOE0 + 1))
            pe.wait_ge(sem("aT_split"), n_pair * (2 * N_MOE) + (N_DENSE + 1))
            wh = w_hi[:, moe_ring(0), :].rearrange("p (k n) -> p k n", k=2)
            wl = w_lo[:, moe_ring(0), :].rearrange("p (k n) -> p k n", k=2)
            for h in range(2):
                cols = slice(h * NB, (h + 1) * NB)
                ins = pe_products(pe, ps[:, h, :], [(f, slice(0, P)) for f in range(2)],
                                  [(wh[:, f, cols], wl[:, f, cols]) for f in range(2)], False, True,
                                  hi=aT_hi, lo=aT_lo)
            ins.then_inc(sem("mm_done"), 1)
            pe_scatter(pe, n_pair * 2 + 1, 1)

        def moe_order(split, act_of, aT_of, hook, ip, par, fori):
            def chunk(u, d, between=None):
                split(u, 3 * d)
                act_of(u, d)
                split(u, 3 * d + 1)
                if between is not None:
                    hook(between)
                split(u, 3 * d + 2)
                aT_of(u, d)
            chunk(0, 0)
            chunk(0, 1, "rows")
            chunk(1, 0, "scatter")
            chunk(1, 1, "gather")
            with fori(2, N_MOE // 2) as u:
                chunk(u, 0)
                chunk(u, 1)

        def act_moe_split(act, p, full_v, free_v):
            act.wait_ge(sem(f"moe_full{p}"), full_v)
            act.wait_ge(sem("mm_done"), free_v)
            act.activation(w_hi[:, moe_ring(p), :], moe_raw(p), ACT.Copy).then_inc(sem("hi_done"), 1)

        def act_silu(act, mm_v):
            act.wait_ge(sem("mm_done"), mm_v)
            act.activation(silu_sb[:, 0, :], ps[:, 4, 0:FC], ACT.Silu).then_inc(sem("silu"), 1)

        def act_aT(act, n):
            act.wait_ge(sem("aT_turned"), n)
            act.activation(aT_hi[:, :, 0:P], psA(1), ACT.Copy).then_inc(sem("aT_hi"), 1)

        def act_gather(act, n, par):
            act.wait_ge(sem("gathered"), n)
            act.activation(Pe[par], ps[:, 7, 0:2 * P], ACT.Copy)
            act.wait_ge(sem("hg_F"), n)
            act.activation(hT_hi[:, :, col_of(par)], hTg, ACT.Copy).then_inc(sem("hg_H"), 1)

        def act_rows(act, mm_v):
            act.wait_ge(sem("mm_done"), mm_v)
            act.activation(y_sb, psf[:, 0:1024], ACT.Copy).then_inc(sem("y_sb"), 1)

        def act_moe(act):
            act.wait_ge(sem("routed"), 1)
            n_pair = act.value_load(n_iter[0:1, 1:2], min_val=N_EXP // 2, max_val=N_EXP)
            act_gather(act, 1, 0)
            with act.Fori(0, n_pair) as ip:
                for par in range(2):
                    off, coff, full = at(ip, par, MOE), at(ip, par, N_MOE), at(ip, par, MOE // 6 * 32)

                    def split(u, p):
                        act_moe_split(act, p, full + (u * 32 + 32), off + (u * 6 + (MOE0 + p - 2)))

                    def silu(u, d):
                        act_silu(act, off + (u * 6 + (3 * d + MOE0 - 1)))

                    def aT(u, d):
                        act_aT(act, coff + (u * 2 + (d + N_DENSE + 1)))

                    def hook(what):
                        if what == "rows":
                            act_rows(act, off + (MOE0 + 3))
                        elif what == "gather":
                            act_gather(act, at(ip, par, 1) + 2, 1 - par)
                    moe_order(split, silu, aT, hook, ip, par, act.Fori)
            act_silu(act, n_pair * (2 * MOE) + (MOE0 - 1))
            act_moe_split(act, 0, n_pair * (MOE // 3 * 32) + 32, n_pair * (2 * MOE) + (MOE0 - 2))
            act_aT(act, n_pair * (2 * N_MOE) + (N_DENSE + 1))
            act_rows(act, n_pair * (2 * MOE) + (MOE0 + 1))

        def dve_moe_split(v, p, hi_v):
            v.wait_ge(sem("hi_done"), hi_v)
            v.tensor_tensor(w_lo[:, moe_ring(p), :], moe_raw(p), w_hi[:, moe_ring(p), :].bitcast(F32), ALU.subtract) \
                .then_inc(sem("lo_done"), 1)

        def dve_gated(v, n):
            v.wait_ge(sem("silu"), n)
            v.tensor_tensor(a_sb[:, 0, :], ps[:, 4, FC:], silu_sb[:, 0, :], ALU.mult).then_inc(sem("act_done"), 1)

        def dve_aT(v, n):
            v.wait_ge(sem("aT_hi"), n)
            v.tensor_tensor(aT_lo[:, :, 0:P], psA(1), aT_hi[:, :, 0:P].bitcast(F32), ALU.subtract) \
                .then_inc(sem("aT_split"), 1)

        def dve_one_hot(v, it, par):
            v.drain()
            for k, src in enumerate((rank17, gate17)):
                v.tensor_copy(now[par][:, k, :].unsqueeze(2), src[:, :, bass.ds(it, 1)])
            v.drain()
            for i in range(TT):
                ins = v.tensor_scalar(PTe[:, i, :], iota, now[par][:, 0, i:i + 1], None, ALU.is_equal)
            ins.then_inc(sem("one_hot"), 1)

        def dve_gather(v, n, par):
            g0 = (GAIN["ffn"] * L + L - 1) * KC
            v.wait_ge(sem("gathered"), n)
            v.tensor_tensor(hTg, psG, bc(gains[:, g0:g0 + KC].unsqueeze(2), [P, KC, P]), ALU.mult) \
                .then_inc(sem("hg_F"), 1)
            v.wait_ge(sem("hg_H"), n)
            v.tensor_tensor(hT_lo[:, :, col_of(par)], hTg, hT_hi[:, :, col_of(par)].bitcast(F32), ALU.subtract) \
                .then_inc(sem("hg_L"), 1)

        def dve_add_rows(v, n, par):
            v.wait_ge(sem("scattered"), n)
            for i in range(TT):
                for h in range(2):
                    dst = x_sb[:, i, h * NB:(h + 1) * NB]
                    ins = v.scalar_tensor_tensor(dst, ps[:, SCATTER[i][h], :], now[par][:, 1, i:i + 1], dst,
                                                 ALU.mult, ALU.add)
            ins.then_inc(sem("x_added"), 1)

        def dve_moe(v):
            v.drain()
            n_pair = v.value_load(n_iter[0:1, 1:2], min_val=N_EXP // 2, max_val=N_EXP)
            dve_one_hot(v, 0, 0)
            dve_gather(v, 1, 0)
            with v.Fori(0, n_pair) as ip:
                for par in range(2):
                    off, coff = at(ip, par, MOE), at(ip, par, N_MOE)

                    def split(u, p):
                        dve_moe_split(v, p, off + (u * 6 + (MOE0 + p + 1)))

                    def gated(u, d):
                        dve_gated(v, coff + (u * 2 + (d + N_DENSE + 1)))

                    def aT(u, d):
                        dve_aT(v, coff + (u * 2 + (d + N_DENSE + 1)))

                    def hook(what):
                        if what == "scatter":
                            dve_add_rows(v, at(ip, par, 1) + 1, 1 - par)
                            dve_one_hot(v, at(ip, par, 1) + 1, 1 - par)
                        elif what == "gather":
                            dve_gather(v, at(ip, par, 1) + 2, 1 - par)
                    moe_order(split, gated, aT, hook, ip, par, v.Fori)
            dve_gated(v, n_pair * (2 * N_MOE) + (N_DENSE + 1))
            dve_moe_split(v, 0, n_pair * (2 * MOE) + (MOE0 + 1))
            dve_aT(v, n_pair * (2 * N_MOE) + (N_DENSE + 1))
            dve_add_rows(v, n_pair * 2 + 1, 1)

        def add_to_x(v):
            def take(b, i):
                dst = x_sb[:, i, b * NB:(b + 1) * NB]
                return v.tensor_tensor(dst, ps[:, 4 + i, :], dst, ALU.add)
            return take

        QA, KA, QI, KI, QB, KB, QC, KCC = 0, 2, 4, 6, 7, 9, 10, 14
        T1, T2, T3 = sc[:, 0:1536], sc[:, 1536:3072], sc[:, 3072:4608]
        IDX = {1: sc[:, 4608:5632].rearrange("p (h s) -> p h s", h=4),
               0: sc[:, 5632:6144].rearrange("p (h s) -> p h s", h=4)}
        W = {0: P, 1: 2 * P}
        SEL = {1: sel_add[:, 0:2 * P], 0: sel_add[:, 2 * P:3 * P]}
        psS = psf[:, 0:H * 2 * P].rearrange("p (h s) -> p h s", h=H)
        psPT = psf[:, 0:2 * H * P].rearrange("p (s h q) -> p s h q", s=2, h=H)
        PT = sc[:, 3072:6144].rearrange("p (s h q) -> p s h q", s=2, h=H)
        psO = psf[:, 6 * NB:6 * NB + 6 * P].rearrange("p (c q) -> p c q", c=6)

        def probs(tt):
            return sc[:, 0:H * W[tt]].rearrange("p (h s) -> p h s", h=H)

        def diag(ap, n):
            return [ap[:, 0:1024].rearrange("p (h s) -> p h s", h=4)[:, :, 0:P],
                    ap[:, 1024:1536].rearrange("p (h s) -> p h s", h=4)]

        def za_parts(ap):
            return ap[:, 0:1024], ap[:, 1024:1536]

        ps_za = (psf[:, 0:1024], ps[:, 2:4, 0:256])

        def part2(ap):
            return ap.rearrange("p (b n) -> p b n", b=2)

        xq_n = sc[:, 4096:5120].rearrange("p (t d) -> p t d", t=TT)
        xq_h = sc[:, 5120:6144].rearrange("p (t d) -> p t d", t=TT)
        xk_h = sc[:, 0:1024].rearrange("p (t d) -> p t d", t=TT)
        xk_n = mem_kv[:, 0, :].rearrange("p (t d) -> p t d", t=TT)
        xv_n = mem_kv[:, 1, :].rearrange("p (t d) -> p t d", t=TT)
        xP = sc[:, 0:2048].rearrange("p (g s) -> p g s", g=8)
        xPT = sc[:, 2048:4096].rearrange("p (m h q) -> p m h q", m=2, h=4)
        psX = psf[:, 2048:4096].rearrange("p (g s) -> p g s", g=8)
        psXT = psf[:, 0:2048].rearrange("p (m h q) -> p m h q", m=2, h=4)
        psXO = psf[:, 2048:3072].rearrange("p (h q) -> p h q", h=4)
        XS = float(P) ** -0.5

        PTe = sc[:, 2048:2304].rearrange("p (t s) -> p t s", t=TT)
        Pe = [sc[:, 2304:2560], sc[:, 3584:3840]]
        y_sb = sc[:, 2560:3584]
        hTg = sc[:, 4096:5120].rearrange("p (k s) -> p k s", k=KC)
        psG = psf[:, 1024:2048].rearrange("p (k s) -> p k s", k=KC)
        rt = headsT[:, 8, 0:192]
        logits = rt[:, 0:16].rearrange("p (t e) -> p t e", t=TT)
        top8 = rt[:, 16:32].rearrange("p (t e) -> p t e", t=TT)
        topi = rt[:, 32:48].rearrange("p (t e) -> p t e", t=TT)
        oh = rt[:, 48:80].rearrange("p (j t e) -> p j t e", j=2, t=TT)
        gate17 = rt[:, 80:114].rearrange("p (t c) -> p t c", t=TT)
        rank17 = rt[:, 114:148].rearrange("p (t c) -> p t c", t=TT)
        chosen = rt[:, 148:164].rearrange("p (t e) -> p t e", t=TT)
        g2 = rt[:, 164:172]
        now = [rt[:, 172 + 4 * i:176 + 4 * i].rearrange("p (k t) -> p k t", k=2) for i in range(2)]
        n_f = rt[:, 180:184]
        SCATTER = ((2, 3), (5, 7))

        def pe_mixers(pe, l):
            pe.wait_ge(sem("evac"), 2 * blk0["pa", l])
            for b, col in enumerate((COL["qa"], COL["qa"] + P, COL["ka"], COL["ka"] + P, COL["qi"], COL["qi"] + P)):
                for i in range(TT):
                    ins = pe.transpose(psf[:, b * S + i * P:b * S + (i + 1) * P], z[:, i, col:col + P], ident)
            ins.then_inc(sem("heads1_T"), 1)
            pe.wait_ge(sem("heads_n"), l + 1)
            pe.wait_ge(sem("ki_dup"), l + 1)
            for j, b in enumerate((QB, QB + 1, KB, KI, QC, QC + 1, QC + 2, QC + 3, KCC)):
                for i in range(TT):
                    ins = pe.transpose(psf[:, b * S + i * P:b * S + (i + 1) * P], heads_n[:, i, j * P:(j + 1) * P],
                                       ident)
            ins.then_inc(sem("heads2_T"), 1)
            pe.wait_ge(sem("heads1_sb"), l + 1)
            pe.wait_ge(sem("heads2_sb"), l + 1)
            pe.wait_ge(sem("heads3_sb"), l + 1)
            for i in range(2):
                for p in range(2):
                    r = slice(64 * p, 64 * p + 64)
                    q, k = headsT[r, QA + i, :], headsT[r, KA + i, :]
                    pe.matmul(ps[:, p, i * S:(i + 1) * S], k[:, 0:P], q, start=True, stop=True)
                    ins = pe.matmul(ps[:, 2 + p, i * P:(i + 1) * P], k[:, P:S], q[:, P:S], start=True, stop=True)
            ins.then_inc(sem("a_scores"), 1)
            for i in range(2):
                for p in range(2):
                    r = slice(64 * p, 64 * p + 64)
                    q, k = headsT[r, QI + i, :], headsT[r, KI, :]
                    pe.matmul(ps[:, 4 + p, i * S:(i + 1) * S], q[:, P:S], k, start=True, stop=True)
                    ins = pe.matmul(ps[:, 6 + p, i * P:(i + 1) * P], q[:, 0:P], k[:, 0:P], start=True, stop=True)
            ins.then_inc(sem("idx_scores"), 1)
            pe.wait_ge(sem("idx_relu"), l + 1)
            pe.wait_ge(sem("log_keep"), l + 1)
            for p in range(2):
                pe.matmul(ps[:, 4 + p, :], after_tri, T3[:, p * NB:(p + 1) * NB], start=True, stop=False)
                for i in range(2):
                    pe.matmul(ps[:, 4 + p, i * S + P:(i + 1) * S], ones,
                              T3[:, 1024 + (2 * p + i) * P:1024 + (2 * p + i + 1) * P], start=False, stop=i == 1)
            pe.matmul(ps[:, 6, :], after_tri, T3[:, 1024:1536], start=True, stop=True).then_inc(sem("later"), 1)
            pe.wait_ge(sem("a_att"), l + 1)
            for i in range(2):
                for p in range(2):
                    v0 = COL["va"] + (2 * i + p) * HD
                    o = ps[64 * p:64 * p + 64, 7, i * S:(i + 1) * S]
                    pe.matmul(o, z[:, 0, v0:v0 + HD], T1[:, p * NB + i * S:p * NB + (i + 1) * S],
                              start=True, stop=False)
                    ins = pe.matmul(o[:, P:S], z[:, 1, v0:v0 + HD],
                                    T1[:, 1024 + (2 * p + i) * P:1024 + (2 * p + i + 1) * P], start=False, stop=True)
            ins.then_inc(sem("a_out"), 1)
            for n, tt in enumerate((1, 0)):
                w, q = W[tt], slice(tt * P, (tt + 1) * P)
                for i in range(2):
                    for p in range(2):
                        r = slice(64 * p, 64 * p + 64)
                        pe.matmul(psS[:, 2 * p + i, 0:w], headsT[r, QB + i, q], headsT[r, KB, 0:w],
                                  start=True, stop=True)
                for i in range(4):
                    for g in range(2):
                        r = slice(64 * g, 64 * g + 64)
                        ins = pe.matmul(psS[:, 4 + 4 * g + i, 0:w], headsT[r, QC + i, q], headsT[r, KCC, 0:w],
                                        start=True, stop=True)
                ins.then_inc(sem("scores"), 1)
                pe.wait_ge(sem("probs"), 2 * l + n + 1)
                for s in range(w // P):
                    for h in range(H):
                        ins = pe.transpose(psPT[:, s, h, :], probs(tt)[:, h, s * P:(s + 1) * P], ident)
                    ins.then_inc(sem(f"probs_T{s}"), 1)
                pe.wait_ge(sem("pT0_sb"), 2 * l + n + 1)
                if tt == 1:
                    pe.wait_ge(sem("pT1_sb"), l + 1)
                pe.wait_ge(sem("oT_L"), 3 * l + n + 1)
                ns = w // P
                for p in range(2):
                    for s in range(ns):
                        pe.matmul(psO[64 * p:64 * p + 64, 0:2, :], z[:, s, COL["vb"]:COL["vb"] + HD],
                                  PT[:, s, 2 * p:2 * p + 2, :], start=s == 0, stop=s == ns - 1)
                for g in range(2):
                    for p in range(2):
                        v0 = COL["vc"] + g * HD
                        for s in range(ns):
                            ins = pe.matmul(psO[64 * p:64 * p + 64, 2 + 2 * g:4 + 2 * g, :], z[:, s, v0:v0 + HD],
                                            PT[:, s, 4 + 4 * g + p:4 + 4 * g + p + 3:2, :],
                                            start=s == 0, stop=s == ns - 1)
                ins.then_inc(sem("bc_out"), 1)

        def pe_cross(pe, l):
            pe.wait_ge(sem("x_heads_n"), l + 1)
            for j, src in enumerate((xq_h, xk_h)):
                for h in range(4):
                    for i in range(TT):
                        c = (4 * j + h) * S + i * P
                        ins = pe.transpose(psf[:, c:c + P], src[:, i, h * P:(h + 1) * P], ident)
            ins.then_inc(sem("x_heads_T"), 1)
            pe.wait_ge(sem("x_qT"), l + 1)
            pe.wait_ge(sem("x_kT"), l + 1)
            for i in range(TT):
                for h in range(4):
                    ins = pe.matmul(psX[:, 4 * i + h, :], headsT[:, h, i * P:(i + 1) * P], headsT[:, 4 + h, :],
                                    start=True, stop=True)
            ins.then_inc(sem("x_scores"), 1)
            pe.wait_ge(sem("x_probs"), l + 1)
            for m in range(2):
                for h in range(4):
                    for i in range(TT):
                        ins = pe.transpose(psXT[:, m, h, i * P:(i + 1) * P], xP[:, 4 * i + h, m * P:(m + 1) * P],
                                           ident)
                ins.then_inc(sem("x_probs_T"), 1)
            pe.wait_ge(sem("x_pT0"), l + 1)
            pe.wait_ge(sem("x_pT1"), l + 1)
            for h in range(4):
                for m in range(2):
                    ins = pe.matmul(psXO[:, h, :], xv_n[:, m, h * P:(h + 1) * P], xPT[:, m, h, :],
                                    start=m == 0, stop=m == 1)
                if h % 2:
                    ins.then_inc(sem("xo_T"), 1)

        def pe_program(pe):
            pe.wait_ge(sem("const_in"), 16)
            pe.wait_ge(sem("gain_in"), 96)
            pe.transpose(ps[:, 0, 0:64], gain_rows, ident[0:64, 0:64])
            pe.matmul(ps[0:H, 1, 0:3 * P], rel_rows, bucket_rows, start=True, stop=True) \
                .then_inc(sem("setup"), 1)
            for l in range(L):
                pe.wait_ge(sem("mix_xn"), l + 1)
                pe_turn(pe, "mix", xn)
                pe.wait_ge(sem("mix_L"), 2 * l + 2)
                pe_win(pe, l)
                pe.wait_ge(sem("mem_xn"), l + 1)
                pe_turn(pe, "mem", mem_n)
                pe.wait_ge(sem("mem_L"), 2 * l + 2)
                pe_linear(pe, "xkv", l)
                pe_mixers(pe, l)
                pe.wait_ge(sem("oT_L"), 3 * l + 3)
                pe_linear(pe, "pa", l)
                pe_linear(pe, "pb", l, k0=2)
                pe_linear(pe, "pc", l, k0=4)
                pe.wait_ge(sem("merged"), l + 1)
                pe_turn(pe, "mrg", xn)
                pe.wait_ge(sem("mrg_L"), 2 * l + 2)
                pe_linear(pe, "out", l)
                pe.wait_ge(sem("x_xn"), l + 1)
                pe_turn(pe, "x", xn)
                pe.wait_ge(sem("x_L"), 2 * l + 2)
                pe_linear(pe, "xq", l)
                pe_cross(pe, l)
                pe.wait_ge(sem("xo_L"), 2 * l + 2)
                pe_linear(pe, "xo", l)
                pe.wait_ge(sem("ffn_xn"), l + 1)
                pe_turn(pe, "ffn", xn)
                pe.wait_ge(sem("ffn_L"), 2 * l + 2)
                if l == 0:
                    pe_dense(pe, FFN0[0], N_DENSE)
            pe.wait_ge(sem("router_in"), 16)
            for i in range(TT):
                for k in range(KC):
                    ins = pe.matmul(ps[:, 4, 8 * i:8 * i + 8], hTf[:, k, i * P:(i + 1) * P], w_router[:, k, :],
                                    start=k == 0, stop=k == KC - 1)
            ins.then_inc(sem("logits"), 1)
            pe.wait_ge(sem("chosen"), 1)
            pe.matmul(ps[:, 5, 0:8], before_tri, chosen[:, 0, :], start=True, stop=True)
            pe.matmul(ps[:, 5, 8:16], ones, chosen[:, 0, :], start=True, stop=False)
            pe.matmul(ps[:, 5, 8:16], before_tri, chosen[:, 1, :], start=False, stop=True)
            pe.matmul(ps[:, 5, 16:24], ones, chosen[:, 0, :], start=True, stop=False)
            pe.matmul(ps[:, 5, 16:24], ones, chosen[:, 1, :], start=False, stop=True).then_inc(sem("ranks"), 1)
            pe_moe(pe)

        def act_norm(act, name, l, rows, src, dst, col):
            for i in range(TT):
                ins = act.activation(dst[:, i, :], src[:, i, :], ACT.Copy, scale=rstd[:, col + i:col + i + 1])
            ins.then_inc(sem(name + "_xn"), 1)

        def end_of(name, l):
            s, nblk, per = slots_of(name, l)
            return s + nblk * per

        def act_mixers(act, l):
            act.wait_ge(sem("z_done"), l + 1)
            act.activation(gates, gates, ACT.Sigmoid).then_inc(sem("gates"), 1)
            ki = z[:, :, COL["ki"]:COL["ki"] + HD].unsqueeze(2)
            act.wait_ge(sem("var"), len(RS) * l + RS["heads"] + 1)
            for i in range(TT):
                ins = act.activation(heads_n[:, i, 3 * P:4 * P].rearrange("p (r d) -> p r d", r=2),
                                     bc(ki[:, i], [P, 2, HD]), ACT.Copy)
            ins.then_inc(sem("ki_dup"), 1)
            act_rsqrt(act, "heads", l)
            if l == 0:
                act.wait_ge(sem("bias_in"), 16 * (H + 1))
            act.wait_ge(sem("heads1_T"), l + 1)
            act.activation(headsT[:, 0:6, :].rearrange("p b s -> p (b s)"), psf[:, 0:6 * S], ACT.Copy) \
                .then_inc(sem("heads1_sb"), 1)
            act.wait_ge(sem("heads2_T"), l + 1)
            act.activation(headsT[:, 6:10, :].rearrange("p b s -> p (b s)"), psf[:, 6 * S:10 * S], ACT.Copy) \
                .then_inc(sem("heads2_sb"), 1)
            act.wait_ge(sem("a_scores"), l + 1)
            t1 = za_parts(T1)
            act.activation(t1[0], ps_za[0], ACT.Abs, scale=0.125)
            act.activation(part2(t1[1]), ps_za[1], ACT.Abs, scale=0.125).then_inc(sem("a_abs"), 1)
            act.drain()
            act.activation(T1, T1, ACT.Exp, scale=-1.0)
            act.drain()
            act.activation(T1, T1, ACT.Ln, bias=1.0).then_inc(sem("softplus"), 1)
            act.wait_ge(sem("idx_scores"), l + 1)
            act.activation(IDX[1].rearrange("p h s -> p (h s)"), psf[:, 4 * NB:6 * NB], ACT.Relu, scale=0.125)
            act.activation(part2(IDX[0].rearrange("p h s -> p (h s)")), ps[:, 6:8, 0:256], ACT.Relu, scale=0.125) \
                .then_inc(sem("idx_relu"), 1)
            act.wait_ge(sem("a_logs"), l + 1)
            act.activation(T1, T2, ACT.Exp).then_inc(sem("a_exp"), 1)
            act.wait_ge(sem("a_out"), l + 1)
            act.wait_ge(sem("mm_done"), end_of("xkv", l))
            act.activation(hT_hi[:, 0:2, :], ps[:, 7, :].rearrange("p (c s) -> p c s", c=2), ACT.Copy) \
                .then_inc(sem("oT_H"), 1)
            for n, tt in enumerate((1, 0)):
                pr = probs(tt)
                act.wait_ge(sem("row_max"), 2 * l + n + 1)
                for h in range(H):
                    act.activation(pr[:, h, :], pr[:, h, :], ACT.Exp, bias=negm[:, h:h + 1],
                                   accum_out=rsum[:, h:h + 1])
                act.activation(s8[:, 0:8], s8[:, 0:8], ACT.Exp).then_inc(sem("exps"), 1)
                act.wait_ge(sem("probs_T0"), 2 * l + n + 1)
                act.activation(PT[:, 0, :, :], psPT[:, 0, :, :], ACT.Copy).then_inc(sem("pT0_sb"), 1)
                act.wait_ge(sem("bc_out"), 2 * l + n + 1)
                act.activation(hT_hi[:, 2:8, tt * P:(tt + 1) * P], psO, ACT.Copy).then_inc(sem("oT_H"), 1)

        def act_cross(act, l):
            act_rsqrt(act, "xqk", l)
            act.wait_ge(sem("x_heads_T"), l + 1)
            act.activation(headsT[:, 0:4, :].rearrange("p b s -> p (b s)"), psf[:, 0:4 * S], ACT.Copy) \
                .then_inc(sem("x_qT"), 1)
            act.wait_ge(sem("x_max"), l + 1)
            for g in range(8):
                ins = act.activation(xP[:, g, :], psX[:, g, :], ACT.Exp, bias=negm[:, g:g + 1], scale=XS,
                                     accum_out=rsum[:, g:g + 1])
            ins.then_inc(sem("x_exps"), 1)
            act.wait_ge(sem("x_probs_T"), 2 * l + 1)
            act.activation(xPT[:, 0, :, :], psXT[:, 0, :, :], ACT.Copy).then_inc(sem("x_pT0"), 1)
            act_hi(act, "xo", l, psXO, "xo_T", 4, end_of("xq", l))

        def act_program(act):
            cnt = Count()
            act.dma_start(x_sb[:, :, :], t["x"][0].rearrange("(t p) d -> p t d", p=P)).then_inc(sem("x_in"), 16)
            act.wait_ge(sem("setup"), 1)
            act.activation(gains[:, :], ps[:, 0, 0:64], ACT.Copy).then_inc(sem("gains"), 1)
            act.activation(dist_rows, ps[0:H, 1, 0:3 * P], ACT.Copy).then_inc(sem("dist_sb"), 1)
            for l in range(L):
                lim = FFN0[l]
                act_rsqrt(act, "mix", l)
                act.wait_ge(sem("mix_rs"), l + 1)
                act_norm(act, "mix", l, None, x_sb, xn, 0)
                act_norm(act, "mem", l, None, mem_n, mem_n, 2)
                act_hi(act, "mix", l, hTf, "mix_F")
                act_win(act, l, cnt, end_of("in", l) + 2)
                act_hi(act, "mem", l, hTf, "mem_F", mm=end_of("in", l))
                act_split_to(act, cnt, end_of("xkv", l) + 2)
                act_mixers(act, l)
                act_split_to(act, cnt, end_of("pc", l) + 2)
                act_hi(act, "mrg", l, psT, "mrg_T", mm=end_of("pc", l))
                act_split_to(act, cnt, end_of("out", l) + 2)
                act_rsqrt(act, "x", l)
                act.wait_ge(sem("x_rs"), l + 1)
                act_norm(act, "x", l, None, x_sb, xn, 0)
                act_hi(act, "x", l, hTf, "x_F", mm=end_of("out", l))
                act_split_to(act, cnt, end_of("xq", l) + 2)
                act_cross(act, l)
                act_split_to(act, cnt, lim)
                act_rsqrt(act, "ffn", l)
                act.wait_ge(sem("ffn_rs"), l + 1)
                act_norm(act, "ffn", l, None, x_sb, xn, 0)
                act_hi(act, "ffn", l, hTf, "ffn_F", mm=end_of("xo", l))
                if l == 0:
                    act_dense(act, FFN0[0], N_DENSE)
                    cnt.n = FFN0[0] + 3 * N_DENSE
            act.wait_ge(sem("top_two"), 1)
            act.activation(g2[:, 0:2], g2[:, 0:2], ACT.Exp).then_inc(sem("gate_exp"), 1)
            act_moe(act)

        def dve_topk(v, l, tt):
            acc = IDX[tt][:, 0, :]
            for j, h in enumerate((0, 2, 1, 3)):
                w = z[:, tt, COL["wi"] + j:COL["wi"] + j + 1]
                if j == 0:
                    v.tensor_scalar(acc, acc, w, None, ALU.mult)
                else:
                    v.scalar_tensor_tensor(acc, IDX[tt][:, h, :], w, acc, ALU.mult, ALU.add)
                v.drain()
            d = acc[:, tt * P:(tt + 1) * P]
            v.tensor_tensor(d, d, causal_add, ALU.add)
            v.drain()
            for _ in range(TOPK // 8):
                v.max(s8[:, 0:8], acc)
                v.drain()
                v.match_replace(acc, s8[:, 0:8], acc, TAKEN)
                v.drain()
            v.tensor_scalar(SEL[tt], acc, TAKEN / 1.5, -BIG, ALU.is_gt, ALU.mult)
            if tt == 0:
                v.drain()
                v.tensor_tensor(SEL[0], SEL[0], causal_add, ALU.add)

        def dve_mixers(v, l):
            if l == 0:
                v.wait_ge(sem("bias_in"), 16 * (H + 1))
                v.tensor_tensor(bias[:, 4:H, :], bias[:, 4:H, :], bc(window.unsqueeze(1), [P, 8, 2 * P]), ALU.add)
            v.drain()
            zb, zc = z[:, :, COL["qb"]:COL["vb"]], z[:, :, COL["qc"]:COL["vc"]]
            sqb, sqc = sc[:, 0:640], sc[:, 640:1920]
            v.tensor_tensor(sqb.rearrange("p (t d) -> p t d", t=TT), zb, zb, ALU.mult)
            v.tensor_tensor(sqc.rearrange("p (t d) -> p t d", t=TT), zc, zc, ALU.mult)
            v.drain()
            v.tensor_reduce(ss[:, 0:10], sqb.rearrange("p (h d) -> p h d", d=HD), AX.X, ALU.add)
            v.tensor_reduce(ss[:, 10:30], sqc.rearrange("p (h d) -> p h d", d=HD), AX.X, ALU.add)
            dve_rsqrt(v, "heads", l, HD)
            v.drain()
            v.wait_ge(sem("hgain_in"), 80 * (l + 1))
            v.wait_ge(sem("ki_dup"), l + 1)

            def head(i, col, r, g, dst):
                return v.scalar_tensor_tensor(heads_n[:, i, dst:dst + HD], z[:, i, col:col + HD], rstd[:, r:r + 1],
                                              hgain[:, g * HD:(g + 1) * HD], ALU.mult, ALU.mult)
            for i in range(TT):
                for h in range(4):
                    head(i, COL["qb"] + h * HD, 5 * i + h, 0, h * HD)
                for d in range(2):
                    head(i, COL["kb"], 5 * i + 4, 1, 2 * P + d * HD)
                for h in range(8):
                    head(i, COL["qc"] + h * HD, 10 + 10 * i + h, 2, 4 * P + (h % 4) * P + (h // 4) * HD)
                for g in range(2):
                    ins = head(i, COL["kc"] + g * HD, 10 + 10 * i + 8 + g, 3, 8 * P + g * HD)
            ins.then_inc(sem("heads_n"), 1)
            v.wait_ge(sem("heads2_T"), l + 1)
            v.tensor_copy(headsT[:, 10:15, :].rearrange("p b s -> p (b s)"), psf[:, 10 * S:15 * S]) \
                .then_inc(sem("heads3_sb"), 1)
            v.wait_ge(sem("a_abs"), l + 1)
            t2, t3 = za_parts(T2), za_parts(T3)
            v.tensor_scalar(t2[0], ps_za[0], 0.125, 0.0, ALU.mult, ALU.min)
            v.tensor_scalar(part2(t2[1]), ps_za[1], 0.125, 0.0, ALU.mult, ALU.min)
            v.wait_ge(sem("softplus"), l + 1)
            v.drain()
            v.tensor_tensor(T2, T2, T1, ALU.subtract)
            v.drain()
            v.scalar_tensor_tensor(t3[0], ps_za[0], -0.125, t2[0], ALU.mult, ALU.add)
            v.scalar_tensor_tensor(part2(t3[1]), ps_za[1], -0.125, part2(t2[1]), ALU.mult, ALU.add)
            v.drain()
            tri = bc(before_tri.unsqueeze(1), [P, 4, P])
            for d in diag(T3, 0):
                ins = v.tensor_tensor(d, d, tri, ALU.mult)
            ins.then_inc(sem("log_keep"), 1)
            v.wait_ge(sem("idx_relu"), l + 1)
            dve_topk(v, l, 1)
            v.wait_ge(sem("later"), l + 1)
            v.tensor_tensor(T2, psf[:, 4 * NB:7 * NB], T2, ALU.add).then_inc(sem("a_logs"), 1)
            dve_topk(v, l, 0)
            v.wait_ge(sem("a_exp"), l + 1)
            for d in diag(T1, 0):
                ins = v.tensor_tensor(d, d, tri, ALU.mult)
            ins.then_inc(sem("a_att"), 1)
            v.wait_ge(sem("oT_H"), 3 * l + 1)
            v.tensor_tensor(hT_lo[:, 0:2, :], ps[:, 7, :].rearrange("p (c s) -> p c s", c=2),
                            hT_hi[:, 0:2, :].bitcast(F32), ALU.subtract).then_inc(sem("oT_L"), 1)
            for n, tt in enumerate((1, 0)):
                pr, w = probs(tt), W[tt]
                v.wait_ge(sem("scores"), 2 * l + n + 1)
                v.scalar_tensor_tensor(pr, psS[:, :, 0:w], 0.125, bias[:, :, 2 * P - w:], ALU.mult, ALU.add)
                v.drain()
                v.tensor_tensor(pr[:, 0:4, :], pr[:, 0:4, :], bc(SEL[tt].unsqueeze(1), [P, 4, w]), ALU.add)
                v.drain()
                v.tensor_reduce(mx, pr, AX.X, ALU.max)
                v.drain()
                v.tensor_tensor(mx[:, 4:12], mx[:, 4:12], sink[:, :], ALU.max)
                v.drain()
                v.tensor_scalar(negm, mx, -1.0, None, ALU.mult)
                v.tensor_tensor(s8[:, 0:8], sink[:, :], mx[:, 4:12], ALU.subtract).then_inc(sem("row_max"), 1)
                v.wait_ge(sem("exps"), 2 * l + n + 1)
                v.tensor_tensor(rsum[:, 4:12], rsum[:, 4:12], s8[:, 0:8], ALU.add)
                v.drain()
                v.reciprocal(mx, rsum)
                v.drain()
                v.tensor_tensor(pr, pr, bc(mx.unsqueeze(2), [P, H, w]), ALU.mult).then_inc(sem("probs"), 1)
                if tt == 1:
                    v.wait_ge(sem("probs_T1"), l + 1)
                    v.tensor_copy(PT[:, 1, :, :], psPT[:, 1, :, :]).then_inc(sem("pT1_sb"), 1)
                v.wait_ge(sem("oT_H"), 3 * l + n + 2)
                q = slice(tt * P, (tt + 1) * P)
                v.tensor_tensor(hT_lo[:, 2:8, q], psO, hT_hi[:, 2:8, q].bitcast(F32), ALU.subtract) \
                    .then_inc(sem("oT_L"), 1)

        def dve_merge(v, cnt, l, lim):
            v.wait_ge(sem("gates"), l + 1)
            for j, name in enumerate(("pa", "pb", "pc")):
                s, nblk, per = slots_of(name, l)
                for b in range(nblk):
                    last = s + (b + 1) * per - 1
                    dve_split_to(v, cnt, min(last + RING, lim))
                    blk = blk0[name, l] + b
                    for i in range(TT):
                        if i == 0:
                            v.wait_ge(sem("tile0_done"), blk + 1)
                        else:
                            v.wait_ge(sem("mm_done"), last + 1)
                        g = gates[:, i, j * D + b * NB:j * D + (b + 1) * NB]
                        m = xn[:, i, b * NB:(b + 1) * NB]
                        prod = sc[:, 2048 + i * NB:2048 + (i + 1) * NB]
                        v.tensor_tensor(prod if j else m, ps[:, 4 + i, :], g, ALU.mult).then_inc(sem("evac"), 1)
                        v.drain()
                        if j:
                            ins = v.tensor_tensor(m, m, prod, ALU.add)
            ins.then_inc(sem("merged"), 1)

        def dve_cross(v, l):
            v.drain()
            sq_q, sq_k = sc[:, 5120:6144], sc[:, 0:1024]
            v.tensor_tensor(sq_q.rearrange("p (t d) -> p t d", t=TT), xq_n, xq_n, ALU.mult)
            v.tensor_tensor(sq_k.rearrange("p (t d) -> p t d", t=TT), xk_n, xk_n, ALU.mult)
            v.drain()
            v.tensor_reduce(ss[:, 0:8], sq_q.rearrange("p (h d) -> p h d", d=P), AX.X, ALU.add)
            v.tensor_reduce(ss[:, 8:16], sq_k.rearrange("p (h d) -> p h d", d=P), AX.X, ALU.add)
            dve_rsqrt(v, "xqk", l, P)
            v.drain()
            v.wait_ge(sem("xgain_in"), 32 * (l + 1))
            for j, (src, dst) in enumerate(((xq_n, xq_h), (xk_n, xk_h))):
                for i in range(TT):
                    for h in range(4):
                        r = 8 * j + 4 * i + h
                        ins = v.scalar_tensor_tensor(dst[:, i, h * P:(h + 1) * P], src[:, i, h * P:(h + 1) * P],
                                                     rstd[:, r:r + 1], hgain[:, j * P:(j + 1) * P],
                                                     ALU.mult, ALU.mult)
            ins.then_inc(sem("x_heads_n"), 1)
            v.wait_ge(sem("x_heads_T"), l + 1)
            v.tensor_copy(headsT[:, 4:8, :].rearrange("p b s -> p (b s)"), psf[:, 4 * S:8 * S]) \
                .then_inc(sem("x_kT"), 1)
            v.wait_ge(sem("x_scores"), l + 1)
            v.tensor_reduce(mx[:, 0:8], psX, AX.X, ALU.max)
            v.drain()
            v.tensor_scalar(negm[:, 0:8], mx[:, 0:8], -XS, None, ALU.mult).then_inc(sem("x_max"), 1)
            v.wait_ge(sem("x_exps"), l + 1)
            v.reciprocal(mx[:, 0:8], rsum[:, 0:8])
            v.drain()
            v.tensor_tensor(xP, xP, bc(mx[:, 0:8].unsqueeze(2), [P, 8, S]), ALU.mult).then_inc(sem("x_probs"), 1)
            v.wait_ge(sem("x_probs_T"), 2 * l + 2)
            v.tensor_copy(xPT[:, 1, :, :], psXT[:, 1, :, :]).then_inc(sem("x_pT1"), 1)
            dve_lo(v, "xo", l, psXO, 4)

        def dve_norm(v, name, l, srcs):
            v.drain()
            for j, src in enumerate(srcs):
                dve_sumsq(v, src, sc[:, 2048:3072], 2 * j)
            dve_rsqrt(v, name, l, D).then_inc(sem(name + "_rs"), 1)

        def dve_router(v):
            v.wait_ge(sem("logits"), 1)
            v.tensor_copy(logits, ps[:, 4, 0:16].rearrange("p (t e) -> p t e", t=TT))
            v.drain()
            for i in range(TT):
                v.max(top8[:, i, :], logits[:, i, :])
            v.drain()
            for i in range(TT):
                v.max_index(idx8[:, i, :], top8[:, i, :], logits[:, i, :])
            v.drain()
            v.tensor_copy(topi, idx8[:, :, :])
            v.drain()
            for j in range(2):
                for i in range(TT):
                    v.tensor_scalar(oh[:, j, i, :], iota[:, 0:8], topi[:, i, j:j + 1], None, ALU.is_equal)
            for i in range(TT):
                ins = v.tensor_tensor(g2[:, i:i + 1], top8[:, i, 1:2], top8[:, i, 0:1], ALU.subtract)
            ins.then_inc(sem("top_two"), 1)
            v.drain()
            v.tensor_tensor(chosen, oh[:, 0], oh[:, 1], ALU.add).then_inc(sem("chosen"), 1)
            v.wait_ge(sem("gate_exp"), 1)
            v.tensor_scalar(g2[:, 2:4], g2[:, 0:2], 1.0, None, ALU.add)
            v.drain()
            v.reciprocal(g2[:, 4:6], g2[:, 2:4])
            v.drain()
            v.tensor_tensor(g2[:, 6:8], g2[:, 4:6], g2[:, 0:2], ALU.mult)
            v.drain()
            for i in range(TT):
                for r in range(2):
                    v.tensor_scalar(gate17[:, i, r * N_EXP:(r + 1) * N_EXP], oh[:, 0, i, :], g2[:, 4 + i:5 + i], None, ALU.mult)
            v.drain()
            for i in range(TT):
                for r in range(2):
                    v.scalar_tensor_tensor(gate17[:, i, r * N_EXP:(r + 1) * N_EXP], oh[:, 1, i, :], g2[:, 6 + i:7 + i],
                                           gate17[:, i, r * N_EXP:(r + 1) * N_EXP], ALU.mult, ALU.add)
            v.wait_ge(sem("ranks"), 1)
            v.tensor_scalar(chosen, chosen, -1e4, 1e4, ALU.mult, ALU.add)
            v.drain()
            v.tensor_tensor(rank17[:, :, 0:N_EXP], ps[:, 5, 0:16].rearrange("p (t e) -> p t e", t=TT), chosen, ALU.add)
            v.drain()
            v.tensor_scalar(rank17[:, :, N_EXP:2 * N_EXP], rank17[:, :, 0:N_EXP], -float(P), None, ALU.add)
            v.tensor_reduce(n_f[:, 0:1], ps[:, 5, 16:24], AX.X, ALU.max)
            v.drain()
            v.tensor_scalar(n_f[:, 1:2], n_f[:, 0:1], float(P), float(N_EXP), ALU.is_gt, ALU.mult)
            v.drain()
            v.tensor_scalar(n_f[:, 2:3], n_f[:, 1:2], float(N_EXP), None, ALU.add)
            v.drain()
            v.tensor_scalar(n_f[:, 3:4], n_f[:, 2:3], 0.5, None, ALU.mult)
            for src in (rank17, gate17):
                v.memset(src[:, :, 2 * N_EXP:], 0.0)
            v.memset(ps[:, 4, :], 0.0)
            v.memset(Pe[1], 0.0)
            v.memset(now[1], 0.0)
            v.drain()
            v.tensor_copy(n_iter[0:1, 0:2], n_f[0:1, 2:4]).then_inc(sem("routed"), 1)

        def dve_program(v):
            cnt = Count()
            v.wait_ge(sem("x_in"), 16)
            for l in range(L):
                lim = FFN0[l]
                v.wait_ge(sem("mem_in"), 16 * (l + 1))
                dve_norm(v, "mix", l, (x_sb, mem_n))
                if l == 0:
                    v.wait_ge(sem("gains"), 1)
                dve_gain(v, "mix", l)
                dve_lo(v, "mix", l, hTf)
                dve_win(v, l, cnt, end_of("in", l) + 2)
                v.drain().then_inc(sem("z_done"), 1)
                dve_gain(v, "mem", l)
                dve_lo(v, "mem", l, hTf)

                def take_kv(b, i):
                    return v.tensor_copy(mem_kv[:, b, i * NB:(i + 1) * NB], ps[:, 4 + i, :])
                dve_linear(v, cnt, "xkv", l, take_kv, lim)
                dve_mixers(v, l)
                dve_merge(v, cnt, l, lim)
                dve_lo(v, "mrg", l, psT)
                dve_linear(v, cnt, "out", l, add_to_x(v), lim)
                dve_norm(v, "x", l, (x_sb,))
                dve_gain(v, "x", l)
                dve_lo(v, "x", l, hTf)

                def take_q(b, i):
                    return v.tensor_copy(xq_n[:, i, :], ps[:, 4 + i, :])
                dve_linear(v, cnt, "xq", l, take_q, lim)
                dve_cross(v, l)
                dve_linear(v, cnt, "xo", l, add_to_x(v), lim)
                dve_norm(v, "ffn", l, (x_sb,))
                dve_gain(v, "ffn", l)
                dve_lo(v, "ffn", l, hTf)
                if l == 0:
                    dve_dense(v, FFN0[0], N_DENSE)
                    cnt.n = FFN0[0] + 3 * N_DENSE
                    v.wait_ge(sem("mm_done"), FFN0[0] + 3 * N_DENSE)
                    v.tensor_tensor(x_sb[:, :, :].rearrange("p t d -> p (t d)"), psf[:, 0:2048],
                                    x_sb[:, :, :].rearrange("p t d -> p (t d)"), ALU.add) \
                        .then_inc(sem("ffn_added"), 1)
            dve_router(v)
            dve_moe(v)
            v.drain().then_inc(sem("x_final"), 1)

        block = ctx.enter_context(nc.Block())

        @block.sync
        def _(sp):
            sp_program(sp)

        @block.gpsimd
        def _(pool):
            pool_program(pool)

        @block.scalar
        def _(act):
            act_program(act)

        @block.vector
        def _(v):
            dve_program(v)

        @block.tensor
        def _(pe):
            pe_program(pe)


_INS = ["x", "mem", "rel_bias", "norm_mix", "w_in", "b_gate", "qn_dsa", "kn_dsa", "qn_swa", "kn_swa", "sinks",
        "w_pa", "w_pb", "w_pc", "w_out", "norm_x", "norm_mem", "w_xq", "w_xkv", "w_xo", "qn_x", "kn_x",
        "norm_ffn", "w_gu_dense", "w_down_dense", "w_router", "w_gu_moe", "w_down_moe"]


def shape_constants():
    import numpy as np
    a, b = np.arange(P)[:, None], np.arange(P)[None, :]
    tiles = np.stack([a == b, a > b, a >= 0 * b, a < b, b + 0 * a, np.where(b <= a, 0.0, -BIG)]).astype(np.float32)
    tiles[2] = 1.0
    rel = np.arange(P)[:, None] + P - np.arange(2 * P)[None, :]
    window = np.where((rel >= 0) & (rel < P), 0.0, -BIG).astype(np.float32)
    n = np.maximum(255 - np.arange(3 * P), 0)
    nf = np.maximum(n, 1).astype(np.float32)
    large = 16 + (np.log(nf / np.float32(16)) / np.float32(math.log(8)) * np.float32(16)).astype(np.int32)
    bucket = np.where(n < 16, n, np.minimum(large, 31))
    return tiles, window, (np.arange(32)[:, None] == bucket[None, :]).astype(np.float32)


def kernel(**inputs):
    import numpy as np
    import concourse.bacc as bacc
    from concourse.bass_utils import run_bass_kernel_spmd

    nc = bacc.Bacc("TRN2", target_bir_lowering=False, num_devices=1)
    arrays, t = {}, {}
    for name in _INS:
        arrays[f"in_{name}"] = np.ascontiguousarray(inputs[name])
    arrays["in_c_tiles"], arrays["in_c_window"], arrays["in_c_bucket"] = shape_constants()
    for name, a in arrays.items():
        t[name[3:]] = nc.dram_tensor(name, a.shape, mybir.dt.from_np(a.dtype), kind="ExternalInput").ap()
    shape = inputs["x"].shape
    out = nc.dram_tensor("out_x", shape, F32, kind="ExternalOutput").ap()
    build(nc, t, out)
    r = run_bass_kernel_spmd(nc, [arrays], core_ids=[0])
    return r.results[0]["out_x"]
```

```python
import math
from contextlib import ExitStack

import concourse.bass as bass
from concourse import mybir

F32 = mybir.dt.float32
F32R = mybir.dt.float32r
I32 = mybir.dt.int32
U32 = mybir.dt.uint32
ALU = mybir.AluOpType
ACT = mybir.ActivationFunctionType
AX = mybir.AxisListType

P = 128
EPS = 1e-6
BIG = 1e30
TAKEN = -3e38
HD = 64
TOPK = 64
SLOT = 2048
RING = 3
FC = 256
NB = 512
LIN = 6
COL = dict(qa=0, ka=256, va=512, qb=768, kb=1024, vb=1088, qi=1152, ki=1408, wi=1472, qc=1476, kc=1988,
           vc=2116, g=2244)


def build(nc, t, out):
    L, D, N_IN = t["w_in"].shape
    S = t["x"].shape[1]
    TT = S // P
    KC = D // P
    F_DENSE = t["w_down_dense"].shape[1]
    N_EXP, F_MOE = t["w_down_moe"].shape[1:3]
    H = 12
    N_DENSE, N_MOE = F_DENSE // FC, F_MOE // FC
    assert (S, D, TT, KC) == (256, 1024, 2, 8)

    plan = []

    def add_block(w, row0, kcs, c0, n):
        v = w[row0:row0 + P * kcs, c0:c0 + n].rearrange("(k p) n -> p k n", p=P)
        plan.append((v, kcs, n))

    blocks = {}

    def add_linear(name, l, w, k, n):
        blocks[name, l] = len(plan)
        for c0 in range(0, n, NB):
            step = min(KC, SLOT // min(NB, n - c0))
            for r0 in range(0, k, step * P):
                add_block(w, r0, min(step, (k - r0) // P), c0, min(NB, n - c0))

    FFN0 = {}
    for l in range(L):
        add_linear("xkv", l, t["w_xkv"][l], D, 1024)
        add_linear("in", l, t["w_in"][l], D, N_IN)
        add_linear("pa", l, t["w_pa"][l], 256, D)
        add_linear("pb", l, t["w_pb"][l], 256, D)
        add_linear("pc", l, t["w_pc"][l], 512, D)
        add_linear("out", l, t["w_out"][l], D, D)
        add_linear("xq", l, t["w_xq"][l], D, 512)
        add_linear("xo", l, t["w_xo"][l], 512, D)
        FFN0[l] = len(plan)
        if l == 0:
            plan.extend([(None, 4, NB)] * (3 * (F_DENSE // FC)))
    n_in_blocks = -(-N_IN // NB)
    order = [("xkv", 2), ("in", n_in_blocks), ("pa", 2), ("pb", 2), ("pc", 2), ("out", 2), ("xq", 1), ("xo", 2)]
    GB0 = -(-COL["g"] // NB)
    N_GB = n_in_blocks - GB0
    N_GATE = 2 * N_GB - 1
    gate0 = {l: blocks["in", l] + 2 * GB0 for l in range(L)}

    def is_gate(s):
        return any(g <= s < g + N_GATE for g in gate0.values())

    def split_no(s):
        return s - sum(min(max(s - g, 0), N_GATE) for g in gate0.values())

    place, full, before = [], [], []
    last_use, n_use = [None] * RING, [0] * RING
    for s in range(len(plan)):
        g = max((g for g in gate0.values() if g <= s), default=0)
        p = (split_no(g) + (s - g + 1) % 2 if is_gate(s) else split_no(s)) % RING
        n_use[p] += 1
        place.append(p)
        full.append(32 * n_use[p])
        before.append(last_use[p])
        last_use[p] = s
    split_slots = [s for s in range(len(plan)) if not is_gate(s)]

    per_layer = sum(n for _, n in order)
    blk0 = {}
    for l in range(L):
        at = l * per_layer
        for name, n in order:
            blk0[name, l] = at
            at += n

    ctx = ExitStack()
    with ctx:
        def sb(name, shape, dt=F32):
            return ctx.enter_context(nc.sbuf_tensor(name, shape, dt))

        sems = {}

        def sem(name):
            if name not in sems:
                sems[name] = ctx.enter_context(nc.semaphore(name))
            return sems[name]

        raw = sb("raw", [P, RING, SLOT])
        w_hi = sb("w_hi", [P, RING, SLOT], F32R)
        w_lo = sb("w_lo", [P, RING, SLOT], F32R)
        x_sb = sb("x_sb", [P, TT, D])
        z = sb("z", [P, TT, N_IN])
        scratch = sb("scratch", [P, 6144])
        hT_hi = sb("hT_hi", [P, KC, S], F32R)
        hT_lo = sb("hT_lo", [P, KC, S], F32R)
        headsT = sb("headsT", [P, 15, S])
        mem_kv = sb("mem_kv", [P, 2, 1024])
        bias = sb("bias", [P, H, 2 * P])
        aT_hi = sb("aT_hi", [P, 2, S], F32R)
        aT_lo = sb("aT_lo", [P, 2, S], F32R)
        consts = sb("consts", [P, 6, P])
        gains = sb("gains", [P, 64])
        hgain = sb("hgain", [P, 256])
        sel_add = sb("sel_add", [P, 3 * P])
        sink = sb("sink", [P, 8])
        w_router = sb("w_router", [P, KC, N_EXP])
        st = sb("st", [P, 184])
        n_iter = sb("n_iter", [1, 2], I32)
        idx8 = sb("idx8", [P, TT, 8], U32)
        ident, after_tri, ones, before_tri, iota, causal_add = (consts[:, i, :] for i in range(6))

        ps = ctx.enter_context(nc.psum_tensor("ps", [P, 8, NB], F32))
        psf = ps[:, :, :].rearrange("p b n -> p (b n)")
        scratch_dram = nc.dram_tensor("bias_by_distance", (H, P, 3 * P), F32, kind="Internal").ap()

        sc = scratch[:, :]
        xn = sc[:, 0:2048].rearrange("p (t d) -> p t d", t=TT)
        hTf = sc[:, 2048:4096].rearrange("p (k s) -> p k s", k=KC)
        mem_n = sc[:, 4096:6144].rearrange("p (t d) -> p t d", t=TT)
        heads_n = sc[:, 1920:4224].rearrange("p (t d) -> p t d", t=TT)
        gates = z[:, :, COL["g"]:]
        ss, var, rstd, tmp = st[:, 0:32], st[:, 32:64], st[:, 64:96], st[:, 96:128]
        mx, negm, rsum = st[:, 128:140], st[:, 140:152], st[:, 152:164]
        s8 = st[:, 164:176]
        norm_rs = st[:, 176:184]

        def bc(ap, shape):
            return ap.to_broadcast(shape)

        def load_slot(sp, s):
            src, kcs, n = plan[s]
            dst = raw[:, place[s], 0:kcs * n].rearrange("p (k n) -> p k n", k=kcs)
            h = kcs // 2
            sp.dma_start(dst[:, 0:h, :], src[:, 0:h, :]).then_inc(sem(f"raw_full{place[s]}"), 16)
            sp.dma_start(dst[:, h:, :], src[:, h:, :]).then_inc(sem(f"raw_full{place[s]}"), 16)

        def load_gu(sp, buf, full, w, c, half, F):
            dst = buf.rearrange("p (k n) -> p k n", k=4)
            rows = w[half * 4 * P:(half + 1) * 4 * P]
            for i in range(2):
                src = rows[:, bass.ds(c * FC + i * F, FC)].rearrange("(k p) n -> p k n", p=P)
                sp.dma_start(dst[:, :, i * FC:(i + 1) * FC], src).then_inc(sem(full), 16)

        def load_down(sp, buf, full, w, row):
            dst = buf.rearrange("p (k n) -> p k n", k=2)
            for k in range(2):
                sp.dma_start(dst[:, k, :], w[bass.ds(row + k * P, P), :]).then_inc(sem(full), 16)

        def sp_dense(sp, s0, w_gu, w_down, F, n):
            def free(s, c=0):
                sp.wait_ge(sem("lo_done"), c * 3 + (split_no(s) - RING + 1))
                return raw[:, place[s], :], f"raw_full{place[s]}"
            for half in range(2):
                load_gu(sp, *free(s0 + half), w_gu, 0, half, F)
            with sp.Fori(1, n) as c:
                for half in range(2):
                    load_gu(sp, *free(s0 - 1 + half, c), w_gu, c, half, F)
                load_down(sp, *free(s0 + 1, c), w_down, c * FC - FC)
            load_down(sp, *free(s0 + 3 * n - 1), w_down, (n - 1) * FC)

        MOE, MOE0 = 3 * N_MOE, FFN0[L - 1]
        SPL0 = split_no(MOE0)
        z_flat = z[:, :, :].rearrange("p t n -> p (t n)")

        def moe_raw(p):
            return z_flat[:, p * SLOT:(p + 1) * SLOT] if p < RING else raw[:, (SPL0 + p) % RING, :]

        def moe_ring(k):
            return (SPL0 + k) % RING

        def sp_moe(sp, wg, wd):
            def chunks(it, u, first=False):
                w_e = wg[bass.ds((it % N_EXP) * D, D), :]
                for d in range(2):
                    for k in range(3):
                        p = 3 * d + k
                        if not first:
                            sp.wait_ge(sem("lo_done"), it * MOE + (u * 6 + (SPL0 + p - 5)))
                        elif p >= RING:
                            sp.wait_ge(sem("lo_done"), SPL0 + p - 5)
                        if k < 2:
                            load_gu(sp, moe_raw(p), f"moe_full{p}", w_e, u * 2 + d, k, F_MOE)
                        else:
                            row = it * F_MOE + (u * (2 * FC) + (d * FC + N_EXP * F_MOE - FC))
                            load_down(sp, moe_raw(p), f"moe_full{p}", wd, row % (N_EXP * F_MOE))
            sp.wait_ge(sem("merged"), L)
            chunks(0, 0, first=True)
            with sp.Fori(1, N_MOE // 2) as u:
                chunks(0, u)
            sp.wait_ge(sem("routed"), 1)
            n_it = sp.value_load(n_iter[0:1, 0:1], min_val=N_EXP, max_val=2 * N_EXP)
            with sp.Fori(1, n_it) as it:
                with sp.Fori(0, N_MOE // 2) as u:
                    chunks(it, u)
            sp.wait_ge(sem("lo_done"), n_it * MOE + (SPL0 - 5))
            load_down(sp, moe_raw(0), "moe_full0", wd, N_EXP * F_MOE - FC)

        def gate_x_place(l):
            return (split_no(gate0[l]) + 2) % RING

        def sp_program(sp):
            sp.dma_start(consts[:, :, :], t["c_tiles"].rearrange("i p n -> p i n")).then_inc(sem("const_in"), 16)
            load_memory(sp, 0)
            for l in range(L):
                for s in range(blocks["xkv", l], FFN0[l]):
                    u = before[s]
                    if s >= gate0[l] + N_GATE and place[s] == gate_x_place(l) and u < gate0[l]:
                        sp.wait_ge(sem("mm_done"), gate0[l] + N_GATE)
                    elif u is not None and is_gate(u):
                        sp.wait_ge(sem("mm_done"), u + 1)
                    elif u is not None:
                        sp.wait_ge(sem("lo_done"), split_no(u) + 1)
                    load_slot(sp, s)
                if l == 0:
                    sp_dense(sp, FFN0[0], t["w_gu_dense"][0], t["w_down_dense"][0], F_DENSE, N_DENSE)
            sp_moe(sp, t["w_gu_moe"][0].rearrange("e d f -> (e d) f"),
                   t["w_down_moe"][0].rearrange("e f d -> (e f) d"))
            sp.wait_ge(sem("x_final"), 1)
            sp.dma_start(out[0].rearrange("(t p) d -> p t d", p=P), x_sb[:, :, :]).then_inc(sem("stored"), 16)
            sp.wait_ge(sem("stored"), 16)

        set_up = headsT[:, 0:4, :].rearrange("p b s -> p (b s)")
        gain_rows, rel_rows = set_up[0:64, 0:P], set_up[0:32, P:P + H]
        bucket_rows, dist_rows = set_up[0:32, 2 * P:5 * P], set_up[0:H, 5 * P:8 * P]
        window = sel_add[:, 0:2 * P]

        def clear_z(pool):
            pool.memset(z[:, :, 0:COL["g"]], 0.0).then_inc(sem("z_zero"), 1)

        def load_gate_bias(pool, l):
            bg = t["b_gate"][l:l + 1].rearrange("a b d -> a (b d)")
            for i in range(TT):
                pool.dma_start(z[:, i, COL["g"]:], bg.to_broadcast([P, N_IN - COL["g"]])).then_inc(sem("z_bias"), 16)

        def load_memory(eng, l):
            eng.dma_start(mem_n, t["mem"][0].rearrange("(t p) d -> p t d", p=P)).then_inc(sem(f"mem{l}_in"), 16)

        def load_head_gains(pool, l):
            pool.dma_start(sink[:, :], t["sinks"][l:l + 1].to_broadcast([P, 8])).then_inc(sem("hgain_in"), 16)
            for i, name in enumerate(("qn_dsa", "kn_dsa", "qn_swa", "kn_swa")):
                pool.dma_start(hgain[:, HD * i:HD * (i + 1)], t[name][l:l + 1].to_broadcast([P, HD])) \
                    .then_inc(sem("hgain_in"), 16)

        def load_cross_gains(pool, l):
            pool.wait_ge(sem("heads_n"), l + 1)
            for i, name in enumerate(("qn_x", "kn_x")):
                pool.dma_start(hgain[:, P * i:P * i + P], t[name][l:l + 1].to_broadcast([P, P])) \
                    .then_inc(sem("xgain_in"), 16)

        def pool_program(pool):
            pool.dma_start(rel_rows, t["rel_bias"]).then_inc(sem("tables_in"), 16)
            pool.dma_start(bucket_rows, t["c_bucket"]).then_inc(sem("tables_in"), 16)
            clear_z(pool)
            load_head_gains(pool, 0)
            pool.wait_ge(sem("dist_sb"), 1)
            pool.wait_ge(sem("mm_done"), 2)
            pool.dma_start(scratch_dram, dist_rows.unsqueeze(1).to_broadcast([H, P, 3 * P])) \
                .then_inc(sem("dist_out"), 16)
            pool.dma_start(window, t["c_window"]).then_inc(sem("bias_in"), 16)
            pool.dma_start(w_router[:, :, :], t["w_router"][0].rearrange("(k p) e -> p k e", p=P)) \
                .then_inc(sem("router_in"), 16)
            pool.wait_ge(sem("dist_out"), 16)
            for i, h in enumerate([0, 2, 1, 3] + list(range(4, H))):
                src = bass.AP(scratch_dram.tensor, h * 3 * P * P + P - 1, [[3 * P - 1, P], [1, 2 * P]])
                pool.dma_start(bias[:, i, :], src).then_inc(sem("bias_in"), 16)
            load_gate_bias(pool, 0)
            load_cross_gains(pool, 0)
            for l in range(1, L):
                pool.wait_ge(sem("merged"), l)
                clear_z(pool)
                load_gate_bias(pool, l)
                pool.wait_ge(sem("k_normed"), l)
                load_head_gains(pool, l)
                pool.wait_ge(sem("x_max"), 2 * l)
                load_memory(pool, l)
                load_cross_gains(pool, l)

        class Count:
            def __init__(self):
                self.n = 0

        def act_split(act, ring, width, raw_v, free_v):
            act.wait_ge(sem(f"raw_full{ring}"), raw_v)
            if free_v is not None:
                act.wait_ge(sem("mm_done"), free_v)
            act.activation(w_hi[:, ring, 0:width], raw[:, ring, 0:width], ACT.Copy).then_inc(sem("hi_done"), 1)

        def dve_split(v, ring, width, hi_v):
            v.wait_ge(sem("hi_done"), hi_v)
            v.tensor_tensor(w_lo[:, ring, 0:width], raw[:, ring, 0:width], w_hi[:, ring, 0:width].bitcast(F32),
                            ALU.subtract).then_inc(sem("lo_done"), 1)

        def act_split_to(act, cnt, end):
            while cnt.n < end:
                s = cnt.n
                _, kcs, n = plan[s]
                if not is_gate(s):
                    k = split_no(s)
                    act_split(act, place[s], kcs * n, full[s], split_slots[k - RING] + 1 if k >= RING else None)
                cnt.n += 1

        def dve_split_to(v, cnt, end):
            while cnt.n < end:
                s = cnt.n
                _, kcs, n = plan[s]
                if not is_gate(s):
                    dve_split(v, place[s], kcs * n, split_no(s) + 1)
                cnt.n += 1

        def slots_of(name, l):
            nblk = dict(order)[name]
            k2 = 2 if name in ("in", "xkv", "out", "xq") else 1
            return blocks[name, l], nblk, k2

        def ahead(split_to, eng, cnt, last, limit):
            split_to(eng, cnt, min(last + RING, limit))

        RS = {"mem": 0, "mix": 1, "heads": 2, "xk": 3, "x": 4, "xq": 5, "ffn": 6}
        RS_N = {"mem": 2, "mix": 2, "heads": 30, "xk": 8, "x": 2, "xq": 8, "ffn": 2}

        def act_rsqrt(act, name, l):
            n, k = RS_N[name], len(RS) * l + RS[name]
            act.wait_ge(sem("var"), k + 1)
            act.activation(tmp[:, 0:n], var[:, 0:n], ACT.Ln)
            act.drain()
            act.activation(rstd[:, 0:n], tmp[:, 0:n], ACT.Exp, scale=-0.5).then_inc(sem("rs0"), 1)

        def dve_var(v, name, width):
            n = RS_N[name]
            v.drain()
            v.tensor_scalar(var[:, 0:n], ss[:, 0:n], 1.0 / width, EPS, ALU.mult, ALU.add).then_inc(sem("var"), 1)

        def dve_newton(v, name, l, dst=None):
            n, k = RS_N[name], len(RS) * l + RS[name]
            v.wait_ge(sem("rs0"), k + 1)
            v.tensor_tensor(tmp[:, 0:n], rstd[:, 0:n], rstd[:, 0:n], ALU.mult)
            v.drain()
            v.tensor_tensor(tmp[:, 0:n], tmp[:, 0:n], var[:, 0:n], ALU.mult)
            v.drain()
            v.tensor_scalar(tmp[:, 0:n], tmp[:, 0:n], -0.5, 1.5, ALU.mult, ALU.add)
            v.drain()
            return v.tensor_tensor(rstd[:, 0:n] if dst is None else dst, rstd[:, 0:n], tmp[:, 0:n], ALU.mult)

        def dve_rsqrt(v, name, l, width):
            dve_var(v, name, width)
            return dve_newton(v, name, l)

        def dve_sumsq(v, src, i, col):
            v.tensor_tensor_reduce(sc[:, 0:1024], src[:, i, :], src[:, i, :], 1.0, 0.0, ALU.mult, ALU.add,
                                   ss[:, col + i:col + i + 1])
            v.drain()

        def pe_turn(pe, name, src, nchunk=KC, blk=None):
            for half in range(2):
                if blk is not None:
                    pe.wait_ge(sem("evac"), 2 * (blk + half + 1))
                ks = range(half * nchunk // 2, (half + 1) * nchunk // 2)
                for k in ks:
                    for i in range(TT):
                        ins = pe.transpose(psf[:, k * S + i * P:k * S + (i + 1) * P], src[:, i, k * P:(k + 1) * P],
                                           ident)
                ins.then_inc(sem(name + "_T"), 1)

        def halves(nchunk=KC):
            return [(i, slice(i * nchunk // 2, (i + 1) * nchunk // 2)) for i in range(2)]

        psT = psf[:, 0:KC * S].rearrange("p (k s) -> p k s", k=KC)
        GAIN = {"mix": 0, "mem": 1, "x": 2, "ffn": 3}

        def dve_gain(v, name, l):
            g0 = (GAIN[name] * L + l) * KC
            for i, ks in halves():
                v.wait_ge(sem(name + "_T"), 2 * l + i + 1)
                g = gains[:, g0 + ks.start:g0 + ks.stop].unsqueeze(2)
                v.tensor_tensor(hTf[:, ks, :], psT[:, ks, :], bc(g, [P, KC // 2, S]), ALU.mult) \
                    .then_inc(sem(name + "_F"), 1)

        def act_hi(act, name, l, src, ready, nchunk=KC, mm=None):
            if mm is not None:
                act.wait_ge(sem("mm_done"), mm)
            for i, ks in halves(nchunk):
                act.wait_ge(sem(ready), 2 * l + i + 1)
                act.activation(hT_hi[:, ks, :], src[:, ks, :], ACT.Copy).then_inc(sem(name + "_H"), 1)

        def dve_lo(v, name, l, src, nchunk=KC):
            for i, ks in halves(nchunk):
                v.wait_ge(sem(name + "_H"), 2 * l + i + 1)
                v.tensor_tensor(hT_lo[:, ks, :], src[:, ks, :], hT_hi[:, ks, :].bitcast(F32), ALU.subtract) \
                    .then_inc(sem(name + "_L"), 1)

        def pe_products(pe, acc, hk, wk, start, stop, hi=hT_hi, lo=hT_lo):
            for j, ((k, cols), (wh, wl)) in enumerate(zip(hk, wk)):
                a, b = hi[:, k, cols], lo[:, k, cols]
                last = j == len(hk) - 1
                pe.matmul(acc, a, wh, start=start and j == 0, stop=False)
                pe.matmul(acc, b, wh, start=False, stop=False)
                ins = pe.matmul(acc, a, wl, start=False, stop=stop and last)
            return ins

        def pe_block_slot(pe, ring, kcs, n, k0, lo_v, first, final, blk_v):
            pe.wait_ge(sem("lo_done"), lo_v)
            wh = w_hi[:, ring, 0:kcs * n].rearrange("p (k n) -> p k n", k=kcs)
            wl = w_lo[:, ring, 0:kcs * n].rearrange("p (k n) -> p k n", k=kcs)
            for i in range(TT):
                if first and blk_v[i] is not None:
                    pe.wait_ge(sem("evac"), blk_v[i])
                cols = slice(i * P, (i + 1) * P)
                ins = pe_products(pe, ps[:, LIN + i, 0:n], [(k0 + k, cols) for k in range(kcs)],
                                  [(wh[:, k, :], wl[:, k, :]) for k in range(kcs)], first, final)
                if i == 0 and final:
                    ins.then_inc(sem("tile0_done"), 1)
            ins.then_inc(sem("mm_done"), 1)

        def pe_linear(pe, name, l, k0=0, b0=0, nblk=None, h_ready=None):
            s, nb_all, per = slots_of(name, l)
            nblk = nblk or nb_all
            for b in range(b0, nblk):
                blk = blk0[name, l] + b
                for h in range(per):
                    ss_ = s + b * per + h
                    _, kcs, n = plan[ss_]
                    evs = [2 * blk - 1 + i if blk else None for i in range(TT)]
                    if h_ready and b == b0:
                        pe.wait_ge(sem(h_ready), 2 * l + h + 1)
                    pe_block_slot(pe, place[ss_], kcs, n, k0 + 4 * h, split_no(ss_) + 1, h == 0, h == per - 1, evs)

        def dve_linear(v, cnt, name, l, take, limit, b0=0, b1=None):
            s, nblk, per = slots_of(name, l)
            for b in range(b0, b1 or nblk):
                last = s + (b + 1) * per - 1
                ahead(dve_split_to, v, cnt, last, limit)
                blk = blk0[name, l] + b
                v.wait_ge(sem("tile0_done"), blk + 1)
                take(b, 0).then_inc(sem("evac"), 1)
                v.wait_ge(sem("mm_done"), last + 1)
                take(b, 1).then_inc(sem("evac"), 1)

        def gate_x(l):
            return raw[:, gate_x_place(l), :].rearrange("p (k s) -> p k s", k=KC)

        def pe_gates(pe, l, a, b):
            for j in range(a, b):
                s = gate0[l] + j
                _, kcs, n = plan[s]
                blk = blk0["in", l] + GB0 + j // 2
                w = raw[:, place[s], 0:kcs * n].rearrange("p (k n) -> p k n", k=kcs)
                pe.wait_ge(sem(f"raw_full{place[s]}"), full[s])
                if j == 0:
                    pe.wait_ge(sem("gate_x"), l + 1)
                for i in range(TT):
                    if j % 2 == 0:
                        pe.wait_ge(sem("evac"), 2 * blk - 1 + i)
                    for k in range(kcs):
                        kk = (j % 2) * 4 + k
                        ins = pe.matmul(ps[:, LIN + i, 0:n], gate_x(l)[:, kk, i * P:(i + 1) * P], w[:, k, :],
                                        start=kk == 0, stop=kk == KC - 1)
                    if i == 0 and kk == KC - 1:
                        ins.then_inc(sem("tile0_done"), 1)
                ins.then_inc(sem("mm_done"), 1)

        def take_in(v):
            def take(b, i):
                n = min(NB, N_IN - b * NB)
                dst = z[:, i, b * NB:b * NB + n]
                return v.scalar_tensor_tensor(dst, ps[:, LIN + i, 0:n], norm_rs[:, i:i + 1], dst, ALU.mult, ALU.add)
            return take

        def dve_gates(v, l, a, b):
            for j in range(a, b):
                blk = blk0["in", l] + GB0 + j
                v.wait_ge(sem("tile0_done"), blk + 1)
                take_in(v)(GB0 + j, 0).then_inc(sem("evac"), 1)
                v.wait_ge(sem("mm_done"), gate0[l] + min(2 * j + 2, N_GATE))
                take_in(v)(GB0 + j, 1).then_inc(sem("evac"), 1)

        a_sb = headsT[:, 0:2, :]
        silu_sb = headsT[:, 2:4, :]

        def psA(T):
            return ps[:, 6, 0:2 * T * P].rearrange("p (f s) -> p f s", f=2)

        def pe_dense(pe, s0, n):
            def gate_up(c, half):
                s, ring = c * 3 + (s0 - 1 + half), place[s0 + 2 + half]
                if isinstance(c, int) and c == 0:
                    s, ring = s0 + half, place[s0 + half]
                pe.wait_ge(sem("lo_done"), s + (1 - N_GATE))
                wh = w_hi[:, ring, :].rearrange("p (k n) -> p k n", k=4)
                wl = w_lo[:, ring, :].rearrange("p (k n) -> p k n", k=4)
                for i in range(TT):
                    cols = slice(i * P, (i + 1) * P)
                    ins = pe_products(pe, ps[:, 4 + i, :], [(4 * half + k, cols) for k in range(4)],
                                      [(wh[:, k, :], wl[:, k, :]) for k in range(4)], half == 0, half == 1)
                ins.then_inc(sem("mm_done"), 1)

            def turn(c):
                pe.wait_ge(sem("act_done"), c + 1)
                for i in range(TT):
                    for f in range(2):
                        ins = pe.transpose(ps[:, 6, (f * TT + i) * P:(f * TT + i + 1) * P],
                                           a_sb[:, i, f * P:(f + 1) * P], ident)
                ins.then_inc(sem("aT_turned"), 1)

            def down(c, s, ring, first, last):
                pe.wait_ge(sem("lo_done"), s + (1 - N_GATE))
                pe.wait_ge(sem("aT_split"), c + 1)
                wh = w_hi[:, ring, :].rearrange("p (k n) -> p k n", k=2)
                wl = w_lo[:, ring, :].rearrange("p (k n) -> p k n", k=2)
                for i in range(TT):
                    for h in range(2):
                        cols = slice(h * NB, (h + 1) * NB)
                        ins = pe_products(pe, ps[:, 2 * i + h, :], [(f, slice(i * P, (i + 1) * P)) for f in range(2)],
                                          [(wh[:, f, cols], wl[:, f, cols]) for f in range(2)], first, last,
                                          hi=aT_hi, lo=aT_lo)
                ins.then_inc(sem("mm_done"), 1)

            def chunk(c, first):
                pe.wait_ge(sem("act_done"), c)
                gate_up(c, 0)
                turn(c - 1)
                gate_up(c, 1)
                down(c - 1, c * 3 + (s0 + 1), place[s0 + 1], first, False)

            for half in range(2):
                pe.wait_ge(sem("ffn_L"), half + 1)
                gate_up(0, half)
            chunk(1, True)
            with pe.Fori(2, n) as c:
                chunk(c, False)
            turn(n - 1)
            down(n - 1, s0 + 3 * n - 1, place[s0 + 3 * n - 1], False, True)

        def split_order(split, act_of, aT_of, s0, n, fori):
            split(0, s0 + 2)
            act_of(0, s0 + 1)
            split(0, s0 + 3)
            with fori(1, n - 1) as c:
                split(c, s0 + 1)
                aT_of(c - 1)
                split(c, s0 + 2)
                act_of(c, s0)
                split(c, s0 + 3)
            split(n - 1, s0 + 1)
            aT_of(n - 2)
            act_of(n - 1, s0)
            split(n - 1, s0 + 2)
            aT_of(n - 1)

        def act_dense(act, s0, n):
            def split(c, base):
                act_split(act, place[base], SLOT, c * 32 + full[base],
                          c * 3 + (base - RING + 1))

            def silu(c, base):
                act.wait_ge(sem("mm_done"), c * 3 + (base + 1))
                for i in range(TT):
                    ins = act.activation(silu_sb[:, i, :], ps[:, 4 + i, 0:FC], ACT.Silu,
                                         scale=norm_rs[:, 6 + i:7 + i])
                ins.then_inc(sem("silu"), 1)

            def aT(c):
                act.wait_ge(sem("aT_turned"), c + 1)
                act.activation(aT_hi[:, :, :], psA(TT), ACT.Copy).then_inc(sem("aT_hi"), 1)
            split_order(split, silu, aT, s0, n, act.Fori)

        def dve_dense(v, s0, n):
            def split(c, base):
                dve_split(v, place[base], SLOT, c * 3 + (split_no(base) + 1))

            def gated(c, base):
                v.wait_ge(sem("silu"), c + 1)
                for i in range(TT):
                    ins = v.scalar_tensor_tensor(a_sb[:, i, :], ps[:, 4 + i, FC:], norm_rs[:, 6 + i:7 + i],
                                                 silu_sb[:, i, :], ALU.mult, ALU.mult)
                ins.then_inc(sem("act_done"), 1)

            def aT(c):
                v.wait_ge(sem("aT_hi"), c + 1)
                v.tensor_tensor(aT_lo[:, :, :], psA(TT), aT_hi[:, :, :].bitcast(F32), ALU.subtract) \
                    .then_inc(sem("aT_split"), 1)
            split_order(split, gated, aT, s0, n, v.Fori)

        def at(ip, par, per):
            return ip * (2 * per) + par * per

        def col_of(par):
            return slice(par * P, (par + 1) * P)

        def pe_turn_chunk(pe):
            for f in range(2):
                ins = pe.transpose(ps[:, 6, f * P:(f + 1) * P], a_sb[:, 0, f * P:(f + 1) * P], ident)
            ins.then_inc(sem("aT_turned"), 1)

        def pe_moe_down(pe, first, last):
            ring = moe_ring(2)
            wh = w_hi[:, ring, :].rearrange("p (k n) -> p k n", k=2)
            wl = w_lo[:, ring, :].rearrange("p (k n) -> p k n", k=2)
            for h in range(2):
                cols = slice(h * NB, (h + 1) * NB)
                ins = pe_products(pe, ps[:, h, :], [(f, slice(0, P)) for f in range(2)],
                                  [(wh[:, f, cols], wl[:, f, cols]) for f in range(2)], first, last,
                                  hi=aT_hi, lo=aT_lo)
            ins.then_inc(sem("mm_done"), 1)

        def pe_moe_chunk(pe, ip, par, c):
            off, coff = at(ip, par, MOE), at(ip, par, N_MOE)
            pe.wait_ge(sem("act_done"), coff + (c + N_DENSE + 1))
            for k in range(2):
                pe.wait_ge(sem("lo_done"), off + (c * 3 + (SPL0 + k + 1)))
                ring = moe_ring(k)
                wh = w_hi[:, ring, :].rearrange("p (k n) -> p k n", k=4)
                wl = w_lo[:, ring, :].rearrange("p (k n) -> p k n", k=4)
                pe_products(pe, ps[:, 4, :], [(4 * k + q, col_of(par)) for q in range(4)],
                            [(wh[:, q, :], wl[:, q, :]) for q in range(4)], k == 0, k == 1) \
                    .then_inc(sem("mm_done"), 1)
                if k == 0:
                    pe_turn_chunk(pe)
            pe.wait_ge(sem("lo_done"), off + (c * 3 + (SPL0 + 3)))
            pe.wait_ge(sem("aT_split"), coff + (c + N_DENSE + 1))
            static = isinstance(c, int)
            if static and c == 1:
                pe.wait_ge(sem("y_sb"), at(ip, par, 1) + 1)
            pe_moe_down(pe, static and c == 1, static and c == 0)

        def pe_gather(pe, n):
            pe.wait_ge(sem("one_hot"), n)
            for i in range(TT):
                pe.transpose(ps[:, 7, i * P:(i + 1) * P], PTe[:, i, :], ident)
            for k in range(KC):
                for i in range(TT):
                    ins = pe.matmul(psG[:, k, :], xn[:, i, k * P:(k + 1) * P], PTe[:, i, :], start=i == 0, stop=i == 1)
            ins.then_inc(sem("gathered"), 1)

        def pe_scatter(pe, n, par):
            pe.wait_ge(sem("y_sb"), n)
            for i in range(TT):
                for h in range(2):
                    ins = pe.matmul(ps[:, SCATTER[i][h], :], Pe[par][:, i * P:(i + 1) * P],
                                    y_sb[:, h * NB:(h + 1) * NB], start=True, stop=True)
            ins.then_inc(sem("scattered"), 1)

        def pe_moe(pe):
            pe.wait_ge(sem("routed"), 1)
            n_pair = pe.value_load(n_iter[0:1, 1:2], min_val=N_EXP // 2, max_val=N_EXP)
            for h in range(2):
                pe.matmul(ps[:, h, :], Pe[1][:, 0:P], consts[:, 0:4, :].rearrange("p i n -> p (i n)"),
                          start=True, stop=False)
            pe_gather(pe, 1)
            with pe.Fori(0, n_pair) as ip:
                for par in range(2):
                    n = at(ip, par, 1) + 1
                    pe.wait_ge(sem("hg_L"), n)
                    pe_moe_chunk(pe, ip, par, 0)
                    pe_moe_chunk(pe, ip, par, 1)
                    pe_scatter(pe, n, 1 - par)
                    pe_moe_chunk(pe, ip, par, 2)
                    pe.wait_ge(sem("x_added"), n)
                    pe_gather(pe, n + 1)
                    with pe.Fori(3, N_MOE) as c:
                        pe_moe_chunk(pe, ip, par, c)
            pe.wait_ge(sem("act_done"), n_pair * (2 * N_MOE) + (N_DENSE + 1))
            pe_turn_chunk(pe)
            pe.wait_ge(sem("lo_done"), n_pair * (2 * MOE) + (SPL0 + 1))
            pe.wait_ge(sem("aT_split"), n_pair * (2 * N_MOE) + (N_DENSE + 1))
            wh = w_hi[:, moe_ring(0), :].rearrange("p (k n) -> p k n", k=2)
            wl = w_lo[:, moe_ring(0), :].rearrange("p (k n) -> p k n", k=2)
            for h in range(2):
                cols = slice(h * NB, (h + 1) * NB)
                ins = pe_products(pe, ps[:, h, :], [(f, slice(0, P)) for f in range(2)],
                                  [(wh[:, f, cols], wl[:, f, cols]) for f in range(2)], False, True,
                                  hi=aT_hi, lo=aT_lo)
            ins.then_inc(sem("mm_done"), 1)
            pe_scatter(pe, n_pair * 2 + 1, 1)

        def moe_order(split, act_of, aT_of, hook, ip, par, fori):
            def chunk(u, d, between=None):
                split(u, 3 * d)
                act_of(u, d)
                split(u, 3 * d + 1)
                if between is not None:
                    hook(between)
                split(u, 3 * d + 2)
                aT_of(u, d)
            chunk(0, 0)
            chunk(0, 1, "rows")
            chunk(1, 0, "scatter")
            chunk(1, 1, "gather")
            with fori(2, N_MOE // 2) as u:
                chunk(u, 0)
                chunk(u, 1)

        def act_moe_split(act, p, full_v, free_v):
            act.wait_ge(sem(f"moe_full{p}"), full_v)
            act.wait_ge(sem("mm_done"), free_v)
            act.activation(w_hi[:, moe_ring(p), :], moe_raw(p), ACT.Copy).then_inc(sem("hi_done"), 1)

        def act_silu(act, mm_v):
            act.wait_ge(sem("mm_done"), mm_v)
            act.activation(silu_sb[:, 0, :], ps[:, 4, 0:FC], ACT.Silu).then_inc(sem("silu"), 1)

        def act_aT(act, n):
            act.wait_ge(sem("aT_turned"), n)
            act.activation(aT_hi[:, :, 0:P], psA(1), ACT.Copy).then_inc(sem("aT_hi"), 1)

        def act_gather(act, n, par):
            act.wait_ge(sem("gathered"), n)
            act.activation(Pe[par], ps[:, 7, 0:2 * P], ACT.Copy)
            act.wait_ge(sem("hg_F"), n)
            act.activation(hT_hi[:, :, col_of(par)], hTg, ACT.Copy).then_inc(sem("hg_H"), 1)

        def act_rows(act, mm_v):
            act.wait_ge(sem("mm_done"), mm_v)
            act.activation(y_sb, psf[:, 0:1024], ACT.Copy).then_inc(sem("y_sb"), 1)

        def act_moe(act):
            act.wait_ge(sem("routed"), 1)
            n_pair = act.value_load(n_iter[0:1, 1:2], min_val=N_EXP // 2, max_val=N_EXP)
            act_gather(act, 1, 0)
            with act.Fori(0, n_pair) as ip:
                for par in range(2):
                    off, coff, full = at(ip, par, MOE), at(ip, par, N_MOE), at(ip, par, MOE // 6 * 32)

                    def split(u, p):
                        act_moe_split(act, p, full + (u * 32 + 32), off + (u * 6 + (MOE0 + p - 2)))

                    def silu(u, d):
                        act_silu(act, off + (u * 6 + (3 * d + MOE0 - 1)))

                    def aT(u, d):
                        act_aT(act, coff + (u * 2 + (d + N_DENSE + 1)))

                    def hook(what):
                        if what == "rows":
                            act_rows(act, off + (MOE0 + 3))
                        elif what == "gather":
                            act_gather(act, at(ip, par, 1) + 2, 1 - par)
                    moe_order(split, silu, aT, hook, ip, par, act.Fori)
            act_silu(act, n_pair * (2 * MOE) + (MOE0 - 1))
            act_moe_split(act, 0, n_pair * (MOE // 3 * 32) + 32, n_pair * (2 * MOE) + (MOE0 - 2))
            act_aT(act, n_pair * (2 * N_MOE) + (N_DENSE + 1))
            act_rows(act, n_pair * (2 * MOE) + (MOE0 + 1))

        def dve_moe_split(v, p, hi_v):
            v.wait_ge(sem("hi_done"), hi_v)
            v.tensor_tensor(w_lo[:, moe_ring(p), :], moe_raw(p), w_hi[:, moe_ring(p), :].bitcast(F32), ALU.subtract) \
                .then_inc(sem("lo_done"), 1)

        def dve_gated(v, n):
            v.wait_ge(sem("silu"), n)
            v.tensor_tensor(a_sb[:, 0, :], ps[:, 4, FC:], silu_sb[:, 0, :], ALU.mult).then_inc(sem("act_done"), 1)

        def dve_aT(v, n):
            v.wait_ge(sem("aT_hi"), n)
            v.tensor_tensor(aT_lo[:, :, 0:P], psA(1), aT_hi[:, :, 0:P].bitcast(F32), ALU.subtract) \
                .then_inc(sem("aT_split"), 1)

        def dve_one_hot(v, it, par):
            v.drain()
            for k, src in enumerate((rank17, gate17)):
                v.tensor_copy(now[par][:, k, :].unsqueeze(2), src[:, :, bass.ds(it, 1)])
            v.drain()
            for i in range(TT):
                ins = v.tensor_scalar(PTe[:, i, :], iota, now[par][:, 0, i:i + 1], None, ALU.is_equal)
            ins.then_inc(sem("one_hot"), 1)

        def dve_gather(v, n, par):
            g0 = (GAIN["ffn"] * L + L - 1) * KC
            v.wait_ge(sem("gathered"), n)
            v.tensor_tensor(hTg, psG, bc(gains[:, g0:g0 + KC].unsqueeze(2), [P, KC, P]), ALU.mult) \
                .then_inc(sem("hg_F"), 1)
            v.wait_ge(sem("hg_H"), n)
            v.tensor_tensor(hT_lo[:, :, col_of(par)], hTg, hT_hi[:, :, col_of(par)].bitcast(F32), ALU.subtract) \
                .then_inc(sem("hg_L"), 1)

        def dve_add_rows(v, n, par):
            v.wait_ge(sem("scattered"), n)
            for i in range(TT):
                for h in range(2):
                    dst = x_sb[:, i, h * NB:(h + 1) * NB]
                    ins = v.scalar_tensor_tensor(dst, ps[:, SCATTER[i][h], :], now[par][:, 1, i:i + 1], dst,
                                                 ALU.mult, ALU.add)
            ins.then_inc(sem("x_added"), 1)

        def dve_moe(v):
            v.drain()
            n_pair = v.value_load(n_iter[0:1, 1:2], min_val=N_EXP // 2, max_val=N_EXP)
            dve_one_hot(v, 0, 0)
            dve_gather(v, 1, 0)
            with v.Fori(0, n_pair) as ip:
                for par in range(2):
                    off, coff = at(ip, par, MOE), at(ip, par, N_MOE)

                    def split(u, p):
                        dve_moe_split(v, p, off + (u * 6 + (SPL0 + p + 1)))

                    def gated(u, d):
                        dve_gated(v, coff + (u * 2 + (d + N_DENSE + 1)))

                    def aT(u, d):
                        dve_aT(v, coff + (u * 2 + (d + N_DENSE + 1)))

                    def hook(what):
                        if what == "scatter":
                            dve_add_rows(v, at(ip, par, 1) + 1, 1 - par)
                            dve_one_hot(v, at(ip, par, 1) + 1, 1 - par)
                        elif what == "gather":
                            dve_gather(v, at(ip, par, 1) + 2, 1 - par)
                    moe_order(split, gated, aT, hook, ip, par, v.Fori)
            dve_gated(v, n_pair * (2 * N_MOE) + (N_DENSE + 1))
            dve_moe_split(v, 0, n_pair * (2 * MOE) + (SPL0 + 1))
            dve_aT(v, n_pair * (2 * N_MOE) + (N_DENSE + 1))
            dve_add_rows(v, n_pair * 2 + 1, 1)

        def add_to_x(v):
            def take(b, i):
                dst = x_sb[:, i, b * NB:(b + 1) * NB]
                return v.tensor_tensor(dst, ps[:, LIN + i, :], dst, ALU.add)
            return take

        QA, KA, QI, KI, QB, KB, QC, KCC = 0, 2, 4, 6, 7, 9, 10, 14
        T1, T2, T3 = sc[:, 0:1536], sc[:, 1536:3072], sc[:, 3072:4608]
        IDX = {1: sc[:, 4608:5632].rearrange("p (h s) -> p h s", h=4),
               0: sc[:, 5632:6144].rearrange("p (h s) -> p h s", h=4)}
        W = {0: P, 1: 2 * P}
        SEL = {1: sel_add[:, 0:2 * P], 0: sel_add[:, 2 * P:3 * P]}
        psS = psf[:, 0:H * 2 * P].rearrange("p (h s) -> p h s", h=H)
        psPT = psf[:, 0:2 * H * P].rearrange("p (s h q) -> p s h q", s=2, h=H)
        PT = sc[:, 3072:6144].rearrange("p (s h q) -> p s h q", s=2, h=H)
        psO = psf[:, 4 * NB:4 * NB + 6 * P].rearrange("p (c q) -> p c q", c=6)

        GATES = [(0, 3), (3, 4), (4, 5), (5, 7), (7, 9), (9, N_GATE)]
        GA = (GB0 + 4) * NB

        def probs(tt):
            return sc[:, 0:H * W[tt]].rearrange("p (h s) -> p h s", h=H)

        def diag(ap, n):
            return [ap[:, 0:1024].rearrange("p (h s) -> p h s", h=4)[:, :, 0:P],
                    ap[:, 1024:1536].rearrange("p (h s) -> p h s", h=4)]

        def za_parts(ap):
            return ap[:, 0:1024], ap[:, 1024:1536]

        ps_za = (psf[:, 0:1024], ps[:, 2:4, 0:256])

        def part2(ap):
            return ap.rearrange("p (b n) -> p b n", b=2)

        xq_n = sc[:, 4096:5120].rearrange("p (t d) -> p t d", t=TT)
        xk_n = mem_kv[:, 0, :].rearrange("p (t d) -> p t d", t=TT)
        xv_n = mem_kv[:, 1, :].rearrange("p (t d) -> p t d", t=TT)
        xP = sc[:, 0:2048].rearrange("p (g s) -> p g s", g=8)
        xPT = sc[:, 2048:4096].rearrange("p (m h q) -> p m h q", m=2, h=4)
        psX = psf[:, 2048:4096].rearrange("p (g s) -> p g s", g=8)
        psXT = psf[:, 0:2048].rearrange("p (m h q) -> p m h q", m=2, h=4)
        psXO = psf[:, 2048:3072].rearrange("p (h q) -> p h q", h=4)
        XS = float(P) ** -0.5

        PTe = sc[:, 2048:2304].rearrange("p (t s) -> p t s", t=TT)
        Pe = [sc[:, 2304:2560], sc[:, 3584:3840]]
        y_sb = sc[:, 2560:3584]
        hTg = sc[:, 4096:5120].rearrange("p (k s) -> p k s", k=KC)
        psG = psf[:, 1024:2048].rearrange("p (k s) -> p k s", k=KC)
        rt = headsT[:, 8, 0:192]
        logits = rt[:, 0:16].rearrange("p (t e) -> p t e", t=TT)
        top8 = rt[:, 16:32].rearrange("p (t e) -> p t e", t=TT)
        topi = rt[:, 32:48].rearrange("p (t e) -> p t e", t=TT)
        oh = rt[:, 48:80].rearrange("p (j t e) -> p j t e", j=2, t=TT)
        gate17 = rt[:, 80:114].rearrange("p (t c) -> p t c", t=TT)
        rank17 = rt[:, 114:148].rearrange("p (t c) -> p t c", t=TT)
        chosen = rt[:, 148:164].rearrange("p (t e) -> p t e", t=TT)
        g2 = rt[:, 164:172]
        now = [rt[:, 172 + 4 * i:176 + 4 * i].rearrange("p (k t) -> p k t", k=2) for i in range(2)]
        n_f = rt[:, 180:184]
        SCATTER = ((2, 3), (5, 7))

        def pe_mixers(pe, l):
            pe.wait_ge(sem("evac"), 2 * (blk0["in", l] + GB0))
            for b, col in enumerate((COL["qa"], COL["qa"] + P, COL["ka"], COL["ka"] + P, COL["qi"], COL["qi"] + P)):
                for i in range(TT):
                    ins = pe.transpose(psf[:, b * S + i * P:b * S + (i + 1) * P], z[:, i, col:col + P], ident)
            ins.then_inc(sem("heads1_T"), 1)
            pe_gates(pe, l, *GATES[0])
            pe.wait_ge(sem("heads_n"), l + 1)
            pe.wait_ge(sem("ki_dup"), l + 1)
            for j, b in enumerate((QB, QB + 1, KB, KI, QC, QC + 1, QC + 2, QC + 3, KCC)):
                if b == QC + 2:
                    ins.then_inc(sem("heads2_T"), 1)
                    pe.wait_ge(sem("heads1_sb"), l + 1)
                c = (b - QC - 2 if b >= QC + 2 else b) * S
                for i in range(TT):
                    ins = pe.transpose(psf[:, c + i * P:c + (i + 1) * P], heads_n[:, i, j * P:(j + 1) * P], ident)
            ins.then_inc(sem("heads3_T"), 1)
            pe.wait_ge(sem("heads2_sb"), l + 1)
            pe.wait_ge(sem("heads3_sb"), l + 1)
            for i in range(2):
                for p in range(2):
                    r = slice(64 * p, 64 * p + 64)
                    q, k = headsT[r, QA + i, :], headsT[r, KA + i, :]
                    pe.matmul(ps[:, p, i * S:(i + 1) * S], k[:, 0:P], q, start=True, stop=True)
                    ins = pe.matmul(ps[:, 2 + p, i * P:(i + 1) * P], k[:, P:S], q[:, P:S], start=True, stop=True)
            ins.then_inc(sem("a_scores"), 1)
            for tt in range(TT):
                for i in range(2):
                    for p in range(2):
                        r = slice(64 * p, 64 * p + 64)
                        q, k = headsT[r, QI + i, tt * P:(tt + 1) * P], headsT[r, KI, 0:W[tt]]
                        o = ps[:, 4 + p, i * S:(i + 1) * S] if tt else ps[:, 2 + p, S + i * P:S + (i + 1) * P]
                        ins = pe.matmul(o, q, k, start=True, stop=True)
                ins.then_inc(sem(f"idx{tt}_scores"), 1)
            pe_gates(pe, l, *GATES[1])
            pe.wait_ge(sem("idx_relu"), l + 1)
            pe.wait_ge(sem("log_keep"), l + 1)
            for p in range(2):
                pe.matmul(ps[:, p, :], after_tri, T3[:, p * NB:(p + 1) * NB], start=True, stop=False)
                for i in range(2):
                    pe.matmul(ps[:, p, i * S + P:(i + 1) * S], ones,
                              T3[:, 1024 + (2 * p + i) * P:1024 + (2 * p + i + 1) * P], start=False, stop=i == 1)
            pe.matmul(ps[:, 2, :], after_tri, T3[:, 1024:1536], start=True, stop=True).then_inc(sem("later"), 1)
            pe_gates(pe, l, *GATES[2])
            pe.wait_ge(sem("a_att"), l + 1)
            for i in range(2):
                for p in range(2):
                    v0 = COL["va"] + (2 * i + p) * HD
                    o = ps[64 * p:64 * p + 64, 5, i * S:(i + 1) * S]
                    pe.matmul(o, z[:, 0, v0:v0 + HD], T1[:, p * NB + i * S:p * NB + (i + 1) * S],
                              start=True, stop=False)
                    ins = pe.matmul(o[:, P:S], z[:, 1, v0:v0 + HD],
                                    T1[:, 1024 + (2 * p + i) * P:1024 + (2 * p + i + 1) * P], start=False, stop=True)
            ins.then_inc(sem("a_out"), 1)
            for n, tt in enumerate((1, 0)):
                w, q = W[tt], slice(tt * P, (tt + 1) * P)
                for i in range(2):
                    for p in range(2):
                        r = slice(64 * p, 64 * p + 64)
                        pe.matmul(psS[:, 2 * p + i, 0:w], headsT[r, QB + i, q], headsT[r, KB, 0:w],
                                  start=True, stop=True)
                pe.wait_ge(sem("oT_L"), 3 * l + n + 1)
                for i in range(4):
                    for g in range(2):
                        r = slice(64 * g, 64 * g + 64)
                        ins = pe.matmul(psS[:, 4 + 4 * g + i, 0:w], headsT[r, QC + i, q], headsT[r, KCC, 0:w],
                                        start=True, stop=True)
                ins.then_inc(sem("scores"), 1)
                pe_gates(pe, l, *GATES[3 + n])
                pe.wait_ge(sem("probs"), 2 * l + n + 1)
                for s in range(w // P):
                    for h in range(H):
                        ins = pe.transpose(psPT[:, s, h, :], probs(tt)[:, h, s * P:(s + 1) * P], ident)
                    ins.then_inc(sem(f"probs_T{s}"), 1)
                pe.wait_ge(sem("pT0_sb"), 2 * l + n + 1)
                if tt == 1:
                    pe.wait_ge(sem("pT1_sb"), l + 1)
                ns = w // P
                for p in range(2):
                    for s in range(ns):
                        pe.matmul(psO[64 * p:64 * p + 64, 0:2, :], z[:, s, COL["vb"]:COL["vb"] + HD],
                                  PT[:, s, 2 * p:2 * p + 2, :], start=s == 0, stop=s == ns - 1)
                for g in range(2):
                    for p in range(2):
                        v0 = COL["vc"] + g * HD
                        for s in range(ns):
                            ins = pe.matmul(psO[64 * p:64 * p + 64, 2 + 2 * g:4 + 2 * g, :], z[:, s, v0:v0 + HD],
                                            PT[:, s, 4 + 4 * g + p:4 + 4 * g + p + 3:2, :],
                                            start=s == 0, stop=s == ns - 1)
                ins.then_inc(sem("bc_out"), 1)
            pe_gates(pe, l, *GATES[5])

        def pe_cross_keys(pe, l):
            pe.wait_ge(sem("k_normed"), l + 1)
            for h in range(4):
                for i in range(TT):
                    c = (8 + h) * S + i * P
                    ins = pe.transpose(psf[:, c:c + P], xk_n[:, i, h * P:(h + 1) * P], ident)
            ins.then_inc(sem("x_keys_T"), 1)

        def pe_cross(pe, l):
            pe.wait_ge(sem("evac"), 2 * (blk0["xq", l] + 1))
            for h in range(4):
                for i in range(TT):
                    c = h * S + i * P
                    ins = pe.transpose(psf[:, c:c + P], xq_n[:, i, h * P:(h + 1) * P], ident)
            ins.then_inc(sem("x_queries_T"), 1)
            pe.wait_ge(sem("x_qT"), l + 1)
            pe.wait_ge(sem("x_kT"), l + 1)
            for i in range(TT):
                for h in range(4):
                    ins = pe.matmul(psX[:, 4 * i + h, :], headsT[:, h, i * P:(i + 1) * P], headsT[:, 4 + h, :],
                                    start=True, stop=True)
                ins.then_inc(sem("x_scores"), 1)
            for i in range(TT):
                pe.wait_ge(sem("x_probs"), 2 * l + i + 1)
                for m in range(2):
                    for h in range(4):
                        ins = pe.transpose(psXT[:, m, h, i * P:(i + 1) * P], xP[:, 4 * i + h, m * P:(m + 1) * P],
                                           ident)
                    if i == TT - 1:
                        ins.then_inc(sem("x_probs_T"), 1)
            pe.wait_ge(sem("x_pT0"), l + 1)
            pe.wait_ge(sem("x_pT1"), l + 1)
            for h in range(4):
                for m in range(2):
                    ins = pe.matmul(psXO[:, h, :], xv_n[:, m, h * P:(h + 1) * P], xPT[:, m, h, :],
                                    start=m == 0, stop=m == 1)
                if h % 2:
                    ins.then_inc(sem("xo_T"), 1)

        def pe_program(pe):
            pe.wait_ge(sem("const_in"), 16)
            pe.wait_ge(sem("gain_in"), 64)
            pe.transpose(ps[:, 4, 0:64], gain_rows, ident[0:64, 0:64]).then_inc(sem("gains_T"), 1)
            for l in range(L):
                if l:
                    pe.wait_ge(sem("ffn_added"), l)
                pe.wait_ge(sem(f"mem{l}_in"), 16)
                pe_turn(pe, "mem", mem_n)
                if l == 0:
                    pe.wait_ge(sem("tables_in"), 32)
                    pe.matmul(ps[0:H, 5, 0:3 * P], rel_rows, bucket_rows, start=True, stop=True) \
                        .then_inc(sem("dist_ps"), 1)
                pe_linear(pe, "xkv", l, nblk=1, h_ready="mem_L")
                if l == 0:
                    pe.wait_ge(sem("x_in"), 16)
                pe_turn(pe, "mix", x_sb)
                pe_linear(pe, "xkv", l, b0=1)
                pe_linear(pe, "in", l, nblk=GB0, h_ready="mix_L")
                pe_mixers(pe, l)
                pe.wait_ge(sem("oT_L"), 3 * l + 3)
                pe_linear(pe, "pa", l)
                pe_linear(pe, "pb", l, k0=2)
                pe_linear(pe, "pc", l, k0=4)
                pe.wait_ge(sem("merged"), l + 1)
                pe_turn(pe, "mrg", xn)
                pe_linear(pe, "out", l, h_ready="mrg_L")
                pe_turn(pe, "x", x_sb, blk=blk0["out", l])
                pe_cross_keys(pe, l)
                pe_linear(pe, "xq", l, h_ready="x_L")
                pe_cross(pe, l)
                pe.wait_ge(sem("xo_L"), 2 * l + 2)
                pe_linear(pe, "xo", l)
                if l < L - 1:
                    pe_turn(pe, "ffn", x_sb, blk=blk0["xo", l])
                else:
                    pe.wait_ge(sem("ffn_xn"), 1)
                    pe_turn(pe, "ffn", xn)
                if l == 0:
                    pe_dense(pe, FFN0[0], N_DENSE)
            pe.wait_ge(sem("ffn_L"), 2 * L)
            pe.wait_ge(sem("router_in"), 16)
            for i in range(TT):
                for k in range(KC):
                    ins = pe.matmul(ps[:, 4, 8 * i:8 * i + 8], hTf[:, k, i * P:(i + 1) * P], w_router[:, k, :],
                                    start=k == 0, stop=k == KC - 1)
            ins.then_inc(sem("logits"), 1)
            pe.wait_ge(sem("chosen"), 1)
            pe.matmul(ps[:, 5, 0:8], before_tri, chosen[:, 0, :], start=True, stop=True)
            pe.matmul(ps[:, 5, 8:16], ones, chosen[:, 0, :], start=True, stop=False)
            pe.matmul(ps[:, 5, 8:16], before_tri, chosen[:, 1, :], start=False, stop=True)
            pe.matmul(ps[:, 5, 16:24], ones, chosen[:, 0, :], start=True, stop=False)
            pe.matmul(ps[:, 5, 16:24], ones, chosen[:, 1, :], start=False, stop=True).then_inc(sem("ranks"), 1)
            pe_moe(pe)

        def act_norm(act, name, src, dst, col):
            for i in range(TT):
                ins = act.activation(dst[:, i, :], src[:, i, :], ACT.Copy, scale=norm_rs[:, col + i:col + i + 1])
            ins.then_inc(sem(name + "_xn"), 1)

        def end_of(name, l):
            s, nblk, per = slots_of(name, l)
            return gate0[l] + N_GATE if name == "in" else s + nblk * per

        def act_mixers(act, cnt, l):
            act.wait_ge(sem("lo_done"), split_no(gate0[l]))
            act.activation(gate_x(l), hTf, ACT.Copy).then_inc(sem("gate_x"), 1)
            ki = z[:, :, COL["ki"]:COL["ki"] + HD].unsqueeze(2)
            act.drain()
            act.wait_ge(sem("var"), len(RS) * l + RS["heads"] + 1)
            for i in range(TT):
                ins = act.activation(heads_n[:, i, 3 * P:4 * P].rearrange("p (r d) -> p r d", r=2),
                                     bc(ki[:, i], [P, 2, HD]), ACT.Copy)
            ins.then_inc(sem("ki_dup"), 1)
            act_rsqrt(act, "heads", l)
            if l == 0:
                act.wait_ge(sem("bias_in"), 16 * (H + 1))
            act.wait_ge(sem("heads1_T"), l + 1)
            act.activation(headsT[:, 0:6, :].rearrange("p b s -> p (b s)"), psf[:, 0:6 * S], ACT.Copy) \
                .then_inc(sem("heads1_sb"), 1)
            act.wait_ge(sem("heads2_T"), l + 1)
            act.activation(headsT[:, 6:10, :].rearrange("p b s -> p (b s)"), psf[:, 6 * S:10 * S], ACT.Copy) \
                .then_inc(sem("heads2_sb"), 1)
            act.wait_ge(sem("a_scores"), l + 1)
            t1 = za_parts(T1)
            act.activation(t1[0], ps_za[0], ACT.Abs, scale=0.125)
            act.wait_ge(sem("idx0_scores"), l + 1)
            act.activation(part2(IDX[0].rearrange("p h s -> p (h s)")), ps[:, 2:4, 256:512], ACT.Relu, scale=0.125)
            act.activation(part2(t1[1]), ps_za[1], ACT.Abs, scale=0.125).then_inc(sem("a_abs"), 1)
            act.drain()
            act.activation(T1, T1, ACT.Exp, scale=-1.0)
            act.drain()
            act.activation(T1, T1, ACT.Ln, bias=1.0).then_inc(sem("softplus"), 1)
            act.wait_ge(sem("idx1_scores"), l + 1)
            act.activation(IDX[1].rearrange("p h s -> p (h s)"), psf[:, 4 * NB:6 * NB], ACT.Relu, scale=0.125) \
                .then_inc(sem("idx_relu"), 1)
            act.wait_ge(sem("a_logs"), l + 1)
            act.activation(T1, T2, ACT.Exp).then_inc(sem("a_exp"), 1)
            act.wait_ge(sem("a_out"), l + 1)
            act.activation(hT_hi[:, 0:2, :], ps[:, 5, :].rearrange("p (c s) -> p c s", c=2), ACT.Copy) \
                .then_inc(sem("oT_H"), 1)
            for n, tt in enumerate((1, 0)):
                pr = probs(tt)
                act.wait_ge(sem("row_max"), 2 * l + n + 1)
                for h in range(H):
                    act.activation(pr[:, h, :], pr[:, h, :], ACT.Exp, bias=negm[:, h:h + 1],
                                   accum_out=rsum[:, h:h + 1])
                act.activation(s8[:, 0:8], s8[:, 0:8], ACT.Exp).then_inc(sem("exps"), 1)
                if tt == 0:
                    act.wait_ge(sem("z_done"), 2 * l + 1)
                    g = z[:, :, COL["g"]:GA]
                    act.activation(g, g, ACT.Sigmoid).then_inc(sem("gates"), 1)
                act.wait_ge(sem("probs_T0"), 2 * l + n + 1)
                act.activation(PT[:, 0, :, :], psPT[:, 0, :, :], ACT.Copy).then_inc(sem("pT0_sb"), 1)
                act.wait_ge(sem("bc_out"), 2 * l + n + 1)
                act.activation(hT_hi[:, 2:8, tt * P:(tt + 1) * P], psO, ACT.Copy).then_inc(sem("oT_H"), 1)
            act_split_to(act, cnt, end_of("in", l) + 2)
            act.wait_ge(sem("z_done"), 2 * l + 2)
            act.activation(z[:, :, GA:], z[:, :, GA:], ACT.Sigmoid).then_inc(sem("gates"), 1)

        def act_cross(act, l):
            act.wait_ge(sem("x_queries_T"), l + 1)
            act.activation(headsT[:, 0:4, :].rearrange("p b s -> p (b s)"), psf[:, 0:4 * S], ACT.Copy) \
                .then_inc(sem("x_qT"), 1)
            act_rsqrt(act, "xq", l)
            for g in range(8):
                if g % 4 == 0:
                    act.wait_ge(sem("x_max"), 2 * l + g // 4 + 1)
                ins = act.activation(xP[:, g, :], psX[:, g, :], ACT.Exp, bias=negm[:, g:g + 1], scale=rstd[:, g:g + 1],
                                     accum_out=rsum[:, g:g + 1])
                if g % 4 == 3:
                    ins.then_inc(sem("x_exps"), 1)
            act.wait_ge(sem("x_probs_T"), 2 * l + 1)
            act.activation(xPT[:, 0, :, :], psXT[:, 0, :, :], ACT.Copy).then_inc(sem("x_pT0"), 1)
            act_hi(act, "xo", l, psXO, "xo_T", 4, end_of("xq", l))

        def act_program(act):
            cnt = Count()
            for i, name in enumerate(("norm_mix", "norm_mem", "norm_x", "norm_ffn")):
                act.dma_start(gain_rows[16 * i:16 * i + 16, :], t[name].rearrange("l (c p) -> (l c) p", p=P)) \
                    .then_inc(sem("gain_in"), 16)
            act.dma_start(x_sb[:, :, :], t["x"][0].rearrange("(t p) d -> p t d", p=P)).then_inc(sem("x_in"), 16)
            act.wait_ge(sem("gains_T"), 1)
            act.activation(gains[:, :], ps[:, 4, 0:64], ACT.Copy).then_inc(sem("gains"), 1)
            for l in range(L):
                lim = FFN0[l]
                s0 = blocks["xkv", l]
                act_split_to(act, cnt, s0 + (1 if l == 0 else RING))
                act_hi(act, "mem", l, hTf, "mem_F")
                act_split_to(act, cnt, s0 + RING)
                if l == 0:
                    act.wait_ge(sem("dist_ps"), 1)
                    act.activation(dist_rows, ps[0:H, 5, 0:3 * P], ACT.Copy).then_inc(sem("dist_sb"), 1)
                act_rsqrt(act, "mem", l)
                act_split_to(act, cnt, end_of("xkv", l) + 2)
                act_hi(act, "mix", l, hTf, "mix_F", mm=end_of("xkv", l))
                act_rsqrt(act, "mix", l)
                act_split_to(act, cnt, gate0[l])
                act_mixers(act, cnt, l)
                act_split_to(act, cnt, end_of("pc", l) + 2)
                act_hi(act, "mrg", l, psT, "mrg_T", mm=end_of("pc", l))
                act_rsqrt(act, "xk", l)
                act_split_to(act, cnt, end_of("out", l) + 2)
                act_hi(act, "x", l, hTf, "x_F", mm=end_of("out", l))
                act.wait_ge(sem("x_keys_T"), l + 1)
                act.activation(headsT[:, 4:8, :].rearrange("p b s -> p (b s)"), psf[:, 8 * S:12 * S], ACT.Copy) \
                    .then_inc(sem("x_kT"), 1)
                act_rsqrt(act, "x", l)
                act_split_to(act, cnt, end_of("xq", l) + 2)
                act_cross(act, l)
                act_split_to(act, cnt, lim + (2 if l == 0 else 0))
                if l < L - 1:
                    act_hi(act, "ffn", l, hTf, "ffn_F", mm=end_of("xo", l))
                    act_rsqrt(act, "ffn", l)
                    act.wait_ge(sem("ffn_rs"), l + 1)
                else:
                    act_rsqrt(act, "ffn", l)
                    act.wait_ge(sem("ffn_rs"), l + 1)
                    act_norm(act, "ffn", x_sb, xn, 6)
                    act_hi(act, "ffn", l, hTf, "ffn_F", mm=end_of("xo", l))
                if l == 0:
                    act_dense(act, FFN0[0], N_DENSE)
                    cnt.n = FFN0[0] + 3 * N_DENSE
            act.wait_ge(sem("top_two"), 1)
            act.activation(g2[:, 0:2], g2[:, 0:2], ACT.Exp).then_inc(sem("gate_exp"), 1)
            act_moe(act)

        def dve_topk(v, l, tt):
            acc = IDX[tt][:, 0, :]
            for j, h in enumerate((0, 2, 1, 3)):
                w = z[:, tt, COL["wi"] + j:COL["wi"] + j + 1]
                if j == 0:
                    v.tensor_scalar(acc, acc, w, None, ALU.mult)
                else:
                    v.scalar_tensor_tensor(acc, IDX[tt][:, h, :], w, acc, ALU.mult, ALU.add)
                v.drain()
            d = acc[:, tt * P:(tt + 1) * P]
            v.tensor_tensor(d, d, causal_add, ALU.add)
            v.drain()
            for _ in range(TOPK // 8):
                v.max(s8[:, 0:8], acc)
                v.drain()
                v.match_replace(acc, s8[:, 0:8], acc, TAKEN)
                v.drain()
            v.tensor_scalar(SEL[tt], acc, TAKEN / 1.5, -BIG, ALU.is_gt, ALU.mult)
            if tt == 0:
                v.drain()
                v.tensor_tensor(SEL[0], SEL[0], causal_add, ALU.add)

        def dve_mixers(v, cnt, l):
            if l == 0:
                v.wait_ge(sem("bias_in"), 16 * (H + 1))
                v.tensor_tensor(bias[:, 4:H, :], bias[:, 4:H, :], bc(window.unsqueeze(1), [P, 8, 2 * P]), ALU.add)
            v.drain()
            zb, zc = z[:, :, COL["qb"]:COL["vb"]], z[:, :, COL["qc"]:COL["vc"]]
            sqb, sqc = sc[:, 0:640], sc[:, 640:1920]
            v.tensor_tensor(sqb.rearrange("p (t d) -> p t d", t=TT), zb, zb, ALU.mult)
            v.tensor_tensor(sqc.rearrange("p (t d) -> p t d", t=TT), zc, zc, ALU.mult)
            v.drain()
            v.tensor_reduce(ss[:, 0:10], sqb.rearrange("p (h d) -> p h d", d=HD), AX.X, ALU.add)
            v.tensor_reduce(ss[:, 10:30], sqc.rearrange("p (h d) -> p h d", d=HD), AX.X, ALU.add)
            dve_rsqrt(v, "heads", l, HD)
            v.drain()
            v.wait_ge(sem("hgain_in"), 80 * (l + 1))
            v.wait_ge(sem("ki_dup"), l + 1)

            def head(i, col, r, g, dst):
                return v.scalar_tensor_tensor(heads_n[:, i, dst:dst + HD], z[:, i, col:col + HD], rstd[:, r:r + 1],
                                              hgain[:, g * HD:(g + 1) * HD], ALU.mult, ALU.mult)
            for i in range(TT):
                for h in range(4):
                    head(i, COL["qb"] + h * HD, 5 * i + h, 0, h * HD)
                for d in range(2):
                    head(i, COL["kb"], 5 * i + 4, 1, 2 * P + d * HD)
                for h in range(8):
                    head(i, COL["qc"] + h * HD, 10 + 10 * i + h, 2, 4 * P + (h % 4) * P + (h // 4) * HD)
                for g in range(2):
                    ins = head(i, COL["kc"] + g * HD, 10 + 10 * i + 8 + g, 3, 8 * P + g * HD)
            ins.then_inc(sem("heads_n"), 1)
            dve_gates(v, l, 0, 1)
            v.wait_ge(sem("heads2_T"), l + 1)
            v.tensor_copy(headsT[:, 10:12, :].rearrange("p b s -> p (b s)"), psf[:, 10 * S:12 * S])
            v.wait_ge(sem("heads3_T"), l + 1)
            v.tensor_copy(headsT[:, 12:15, :].rearrange("p b s -> p (b s)"), psf[:, 0:3 * S]) \
                .then_inc(sem("heads3_sb"), 1)
            v.wait_ge(sem("a_abs"), l + 1)
            t2, t3 = za_parts(T2), za_parts(T3)
            v.tensor_scalar(t2[0], ps_za[0], 0.125, 0.0, ALU.mult, ALU.min)
            v.tensor_scalar(part2(t2[1]), ps_za[1], 0.125, 0.0, ALU.mult, ALU.min)
            v.wait_ge(sem("softplus"), l + 1)
            v.drain()
            v.tensor_tensor(T2, T2, T1, ALU.subtract)
            v.drain()
            v.scalar_tensor_tensor(t3[0], ps_za[0], -0.125, t2[0], ALU.mult, ALU.add)
            v.scalar_tensor_tensor(part2(t3[1]), ps_za[1], -0.125, part2(t2[1]), ALU.mult, ALU.add)
            v.drain()
            tri = bc(before_tri.unsqueeze(1), [P, 4, P])
            for d in diag(T3, 0):
                ins = v.tensor_tensor(d, d, tri, ALU.mult)
            ins.then_inc(sem("log_keep"), 1)
            v.wait_ge(sem("idx_relu"), l + 1)
            dve_topk(v, l, 1)
            v.wait_ge(sem("later"), l + 1)
            v.tensor_tensor(T2, psf[:, 0:3 * NB], T2, ALU.add).then_inc(sem("a_logs"), 1)
            dve_gates(v, l, 1, 2)
            dve_topk(v, l, 0)
            v.wait_ge(sem("a_exp"), l + 1)
            for d in diag(T1, 0):
                ins = v.tensor_tensor(d, d, tri, ALU.mult)
            ins.then_inc(sem("a_att"), 1)
            v.wait_ge(sem("oT_H"), 3 * l + 1)
            v.tensor_tensor(hT_lo[:, 0:2, :], ps[:, 5, :].rearrange("p (c s) -> p c s", c=2),
                            hT_hi[:, 0:2, :].bitcast(F32), ALU.subtract).then_inc(sem("oT_L"), 1)
            for n, tt in enumerate((1, 0)):
                pr, w = probs(tt), W[tt]
                v.wait_ge(sem("scores"), 2 * l + n + 1)
                v.scalar_tensor_tensor(pr, psS[:, :, 0:w], 0.125, bias[:, :, 2 * P - w:], ALU.mult, ALU.add)
                v.drain()
                v.tensor_tensor(pr[:, 0:4, :], pr[:, 0:4, :], bc(SEL[tt].unsqueeze(1), [P, 4, w]), ALU.add)
                v.drain()
                v.tensor_reduce(mx, pr, AX.X, ALU.max)
                v.drain()
                v.tensor_tensor(mx[:, 4:12], mx[:, 4:12], sink[:, :], ALU.max)
                v.drain()
                v.tensor_scalar(negm, mx, -1.0, None, ALU.mult)
                v.tensor_tensor(s8[:, 0:8], sink[:, :], mx[:, 4:12], ALU.subtract).then_inc(sem("row_max"), 1)
                dve_gates(v, l, 2 + n, 3 + n)
                if tt == 0:
                    v.drain().then_inc(sem("z_done"), 1)
                v.wait_ge(sem("exps"), 2 * l + n + 1)
                v.tensor_tensor(rsum[:, 4:12], rsum[:, 4:12], s8[:, 0:8], ALU.add)
                v.drain()
                v.reciprocal(mx, rsum)
                v.drain()
                v.tensor_tensor(pr, pr, bc(mx.unsqueeze(2), [P, H, w]), ALU.mult).then_inc(sem("probs"), 1)
                if tt == 1:
                    v.wait_ge(sem("probs_T1"), l + 1)
                    v.tensor_copy(PT[:, 1, :, :], psPT[:, 1, :, :]).then_inc(sem("pT1_sb"), 1)
                v.wait_ge(sem("oT_H"), 3 * l + n + 2)
                q = slice(tt * P, (tt + 1) * P)
                v.tensor_tensor(hT_lo[:, 2:8, q], psO, hT_hi[:, 2:8, q].bitcast(F32), ALU.subtract) \
                    .then_inc(sem("oT_L"), 1)
            dve_gates(v, l, 4, 5)
            dve_split_to(v, cnt, end_of("in", l) + 1)
            dve_gates(v, l, 5, N_GB)
            v.drain().then_inc(sem("z_done"), 1)

        def dve_merge(v, cnt, l, lim):
            for j, name in enumerate(("pa", "pb", "pc")):
                s, nblk, per = slots_of(name, l)
                v.wait_ge(sem("gates"), 2 * l + (2 if COL["g"] + (j + 1) * D > GA else 1))
                for b in range(nblk):
                    last = s + (b + 1) * per - 1
                    dve_split_to(v, cnt, min(last + (RING if j else 1), lim))
                    blk = blk0[name, l] + b
                    for i in range(TT):
                        if i == 0:
                            v.wait_ge(sem("tile0_done"), blk + 1)
                        else:
                            v.wait_ge(sem("mm_done"), last + 1)
                        g = gates[:, i, j * D + b * NB:j * D + (b + 1) * NB]
                        m = xn[:, i, b * NB:(b + 1) * NB]
                        prod = sc[:, 2048 + i * NB:2048 + (i + 1) * NB]
                        v.tensor_tensor(prod if j else m, ps[:, LIN + i, :], g, ALU.mult).then_inc(sem("evac"), 1)
                        v.drain()
                        if j:
                            ins = v.tensor_tensor(m, m, prod, ALU.add)
            ins.then_inc(sem("merged"), 1)

        def dve_cross_keys_ss(v):
            v.drain()
            sq = sc[:, 0:1024]
            v.tensor_tensor(sq.rearrange("p (t d) -> p t d", t=TT), xk_n, xk_n, ALU.mult)
            v.drain()
            v.tensor_reduce(ss[:, 0:8], sq.rearrange("p (h d) -> p h d", d=P), AX.X, ALU.add)
            dve_var(v, "xk", P)

        def dve_cross_keys(v, l):
            v.wait_ge(sem("xgain_in"), 32 * (l + 1))
            v.tensor_tensor(hgain[:, P:2 * P], hgain[:, 0:P], hgain[:, P:2 * P], ALU.mult)
            dve_newton(v, "xk", l)
            v.drain()
            for i in range(TT):
                for h in range(4):
                    k = xk_n[:, i, h * P:(h + 1) * P]
                    ins = v.scalar_tensor_tensor(k, k, rstd[:, 4 * i + h:4 * i + h + 1], hgain[:, P:2 * P],
                                                 ALU.mult, ALU.mult)
            ins.then_inc(sem("k_normed"), 1)

        def dve_cross(v, cnt, l):
            v.drain()
            sq = sc[:, 5120:6144]
            v.tensor_tensor(sq.rearrange("p (t d) -> p t d", t=TT), xq_n, xq_n, ALU.mult)
            v.drain()
            v.tensor_reduce(ss[:, 0:8], sq.rearrange("p (h d) -> p h d", d=P), AX.X, ALU.add)
            dve_var(v, "xq", P)
            dve_split_to(v, cnt, end_of("xq", l) + 2)
            dve_newton(v, "xq", l)
            v.drain()
            v.tensor_scalar(rstd[:, 0:8], rstd[:, 0:8], XS, None, ALU.mult)
            tiles = [slice(0, 4), slice(4, 8)]
            for i, g in enumerate(tiles):
                v.wait_ge(sem("x_scores"), 2 * l + i + 1)
                v.tensor_reduce(mx[:, g], psX[:, g, :], AX.X, ALU.max)
                v.drain()
                v.scalar_tensor_tensor(negm[:, g], mx[:, g], -1.0, rstd[:, g], ALU.mult, ALU.mult) \
                    .then_inc(sem("x_max"), 1)
            for i, g in enumerate(tiles):
                v.wait_ge(sem("x_exps"), 2 * l + i + 1)
                v.reciprocal(mx[:, g], rsum[:, g])
                v.drain()
                v.tensor_tensor(xP[:, g, :], xP[:, g, :], bc(mx[:, g].unsqueeze(2), [P, 4, S]), ALU.mult) \
                    .then_inc(sem("x_probs"), 1)
            v.wait_ge(sem("x_probs_T"), 2 * l + 2)
            v.tensor_copy(xPT[:, 1, :, :], psXT[:, 1, :, :]).then_inc(sem("x_pT1"), 1)
            dve_lo(v, "xo", l, psXO, 4)

        def dve_hT(v, name, l):
            v.drain()
            dve_gain(v, name, l)
            dve_lo(v, name, l, hTf)
            for i in range(TT):
                dve_sumsq(v, x_sb, i, 0)
            dve_var(v, name, D)

        def dve_router(v):
            v.wait_ge(sem("logits"), 1)
            v.tensor_copy(logits, ps[:, 4, 0:16].rearrange("p (t e) -> p t e", t=TT))
            v.drain()
            for i in range(TT):
                v.max(top8[:, i, :], logits[:, i, :])
            v.drain()
            for i in range(TT):
                v.max_index(idx8[:, i, :], top8[:, i, :], logits[:, i, :])
            v.drain()
            v.tensor_copy(topi, idx8[:, :, :])
            v.drain()
            for j in range(2):
                for i in range(TT):
                    v.tensor_scalar(oh[:, j, i, :], iota[:, 0:8], topi[:, i, j:j + 1], None, ALU.is_equal)
            for i in range(TT):
                ins = v.tensor_tensor(g2[:, i:i + 1], top8[:, i, 1:2], top8[:, i, 0:1], ALU.subtract)
            ins.then_inc(sem("top_two"), 1)
            v.drain()
            v.tensor_tensor(chosen, oh[:, 0], oh[:, 1], ALU.add).then_inc(sem("chosen"), 1)
            v.wait_ge(sem("gate_exp"), 1)
            v.tensor_scalar(g2[:, 2:4], g2[:, 0:2], 1.0, None, ALU.add)
            v.drain()
            v.reciprocal(g2[:, 4:6], g2[:, 2:4])
            v.drain()
            v.tensor_tensor(g2[:, 6:8], g2[:, 4:6], g2[:, 0:2], ALU.mult)
            v.drain()
            for i in range(TT):
                for r in range(2):
                    v.tensor_scalar(gate17[:, i, r * N_EXP:(r + 1) * N_EXP], oh[:, 0, i, :], g2[:, 4 + i:5 + i],
                                    None, ALU.mult)
            v.drain()
            for i in range(TT):
                for r in range(2):
                    v.scalar_tensor_tensor(gate17[:, i, r * N_EXP:(r + 1) * N_EXP], oh[:, 1, i, :], g2[:, 6 + i:7 + i],
                                           gate17[:, i, r * N_EXP:(r + 1) * N_EXP], ALU.mult, ALU.add)
            v.wait_ge(sem("ranks"), 1)
            v.tensor_scalar(chosen, chosen, -1e4, 1e4, ALU.mult, ALU.add)
            v.drain()
            v.tensor_tensor(rank17[:, :, 0:N_EXP], ps[:, 5, 0:16].rearrange("p (t e) -> p t e", t=TT), chosen, ALU.add)
            v.drain()
            v.tensor_scalar(rank17[:, :, N_EXP:2 * N_EXP], rank17[:, :, 0:N_EXP], -float(P), None, ALU.add)
            v.tensor_reduce(n_f[:, 0:1], ps[:, 5, 16:24], AX.X, ALU.max)
            v.drain()
            v.tensor_scalar(n_f[:, 1:2], n_f[:, 0:1], float(P), float(N_EXP), ALU.is_gt, ALU.mult)
            v.drain()
            v.tensor_scalar(n_f[:, 2:3], n_f[:, 1:2], float(N_EXP), None, ALU.add)
            v.drain()
            v.tensor_scalar(n_f[:, 3:4], n_f[:, 2:3], 0.5, None, ALU.mult)
            for src in (rank17, gate17):
                v.memset(src[:, :, 2 * N_EXP:], 0.0)
            v.memset(ps[:, 4, :], 0.0)
            v.memset(Pe[1], 0.0)
            v.memset(now[1], 0.0)
            v.drain()
            v.tensor_copy(n_iter[0:1, 0:2], n_f[0:1, 2:4]).then_inc(sem("routed"), 1)

        def dve_program(v):
            cnt = Count()
            for l in range(L):
                lim = FFN0[l]
                s0 = blocks["xkv", l]
                if l:
                    dve_split_to(v, cnt, s0 + 1)
                if l == 0:
                    v.wait_ge(sem("gains"), 1)
                dve_gain(v, "mem", l)
                dve_split_to(v, cnt, s0 + 1)
                dve_lo(v, "mem", l, hTf)
                v.drain()
                for i in range(TT):
                    dve_sumsq(v, mem_n, i, 0)
                dve_var(v, "mem", D)
                dve_split_to(v, cnt, s0 + RING)
                dve_newton(v, "mem", l, norm_rs[:, 2:4])
                v.drain()

                def take_kv(b, i):
                    return v.tensor_scalar(mem_kv[:, b, i * NB:(i + 1) * NB], ps[:, LIN + i, :],
                                           norm_rs[:, 2 + i:3 + i], None, ALU.mult)
                dve_linear(v, cnt, "xkv", l, take_kv, lim, b1=1)
                if l == 0:
                    v.wait_ge(sem("x_in"), 16)
                for i in range(TT):
                    dve_sumsq(v, x_sb, i, 0)
                dve_var(v, "mix", D)
                dve_gain(v, "mix", l)
                dve_linear(v, cnt, "xkv", l, take_kv, lim, b0=1)
                dve_lo(v, "mix", l, hTf)
                v.wait_ge(sem("z_zero"), l + 1)
                dve_newton(v, "mix", l, norm_rs[:, 0:2])
                v.drain()
                dve_linear(v, cnt, "in", l, take_in(v), gate0[l], b1=GB0 - 1)
                v.wait_ge(sem("z_bias"), 32 * (l + 1))
                dve_linear(v, cnt, "in", l, take_in(v), gate0[l], b0=GB0 - 1, b1=GB0)
                dve_mixers(v, cnt, l)
                dve_merge(v, cnt, l, lim)
                dve_lo(v, "mrg", l, psT)
                dve_cross_keys_ss(v)
                dve_split_to(v, cnt, blocks["out", l] + RING)
                dve_linear(v, cnt, "out", l, add_to_x(v), lim, b1=1)
                dve_cross_keys(v, l)
                dve_linear(v, cnt, "out", l, add_to_x(v), lim, b0=1)
                dve_hT(v, "x", l)
                dve_split_to(v, cnt, blocks["xq", l] + RING)
                dve_newton(v, "x", l, norm_rs[:, 4:6])
                v.drain()

                def take_q(b, i):
                    return v.tensor_scalar(xq_n[:, i, :], ps[:, LIN + i, :], norm_rs[:, 4 + i:5 + i], None, ALU.mult)
                dve_linear(v, cnt, "xq", l, take_q, blocks["xq", l] + RING)
                dve_cross(v, cnt, l)
                dve_linear(v, cnt, "xo", l, add_to_x(v), lim + (2 if l == 0 else 0))
                dve_split_to(v, cnt, lim + (2 if l == 0 else 0))
                if l < L - 1:
                    dve_hT(v, "ffn", l)
                    dve_newton(v, "ffn", l, norm_rs[:, 6:8]).then_inc(sem("ffn_rs"), 1)
                    v.drain()
                else:
                    v.drain()
                    for i in range(TT):
                        dve_sumsq(v, x_sb, i, 0)
                    dve_var(v, "ffn", D)
                    dve_newton(v, "ffn", l, norm_rs[:, 6:8]).then_inc(sem("ffn_rs"), 1)
                    dve_gain(v, "ffn", l)
                    dve_lo(v, "ffn", l, hTf)
                if l == 0:
                    dve_dense(v, FFN0[0], N_DENSE)
                    cnt.n = FFN0[0] + 3 * N_DENSE
                    v.wait_ge(sem("mm_done"), FFN0[0] + 3 * N_DENSE)
                    v.tensor_tensor(x_sb[:, :, :].rearrange("p t d -> p (t d)"), psf[:, 0:2048],
                                    x_sb[:, :, :].rearrange("p t d -> p (t d)"), ALU.add) \
                        .then_inc(sem("ffn_added"), 1)
            dve_router(v)
            dve_moe(v)
            v.drain().then_inc(sem("x_final"), 1)

        block = ctx.enter_context(nc.Block())

        @block.sync
        def _(sp):
            sp_program(sp)

        @block.gpsimd
        def _(pool):
            pool_program(pool)

        @block.scalar
        def _(act):
            act_program(act)

        @block.vector
        def _(v):
            dve_program(v)

        @block.tensor
        def _(pe):
            pe_program(pe)


_INS = ["x", "mem", "rel_bias", "norm_mix", "w_in", "b_gate", "qn_dsa", "kn_dsa", "qn_swa", "kn_swa", "sinks",
        "w_pa", "w_pb", "w_pc", "w_out", "norm_x", "norm_mem", "w_xq", "w_xkv", "w_xo", "qn_x", "kn_x",
        "norm_ffn", "w_gu_dense", "w_down_dense", "w_router", "w_gu_moe", "w_down_moe"]


def shape_constants():
    import numpy as np
    a, b = np.arange(P)[:, None], np.arange(P)[None, :]
    tiles = np.stack([a == b, a > b, a >= 0 * b, a < b, b + 0 * a, np.where(b <= a, 0.0, -BIG)]).astype(np.float32)
    tiles[2] = 1.0
    rel = np.arange(P)[:, None] + P - np.arange(2 * P)[None, :]
    window = np.where((rel >= 0) & (rel < P), 0.0, -BIG).astype(np.float32)
    n = np.maximum(255 - np.arange(3 * P), 0)
    nf = np.maximum(n, 1).astype(np.float32)
    large = 16 + (np.log(nf / np.float32(16)) / np.float32(math.log(8)) * np.float32(16)).astype(np.int32)
    bucket = np.where(n < 16, n, np.minimum(large, 31))
    return tiles, window, (np.arange(32)[:, None] == bucket[None, :]).astype(np.float32)


def kernel(**inputs):
    import numpy as np
    import concourse.bacc as bacc
    from concourse.bass_utils import run_bass_kernel_spmd

    nc = bacc.Bacc("TRN2", target_bir_lowering=False, num_devices=1)
    arrays, t = {}, {}
    for name in _INS:
        arrays[f"in_{name}"] = np.ascontiguousarray(inputs[name])
    arrays["in_c_tiles"], arrays["in_c_window"], arrays["in_c_bucket"] = shape_constants()
    for name, a in arrays.items():
        t[name[3:]] = nc.dram_tensor(name, a.shape, mybir.dt.from_np(a.dtype), kind="ExternalInput").ap()
    shape = inputs["x"].shape
    out = nc.dram_tensor("out_x", shape, F32, kind="ExternalOutput").ap()
    build(nc, t, out)
    r = run_bass_kernel_spmd(nc, [arrays], core_ids=[0])
    return r.results[0]["out_x"]
```
